# Optimizing a Trainium2 kernel written in Bass

```python
import math
import jax, jax.numpy as jnp
from jax import lax
import numpy as np
import jax
import jax.numpy as jnp

D_MODEL = 1024
BATCH = 1
SEQ = 256
DEPTH = 1

GRID_W = 64
CTX_LEN = 256
EPS = 1e-6
ROPE_THETA = 10000.0
Q_BLOCK = 128

DIFF_HEADS = 4
DIFF_HEAD_DIM = 64
DIFF_V_DIM = 2 * DIFF_HEAD_DIM
DIFF_WIDTH = DIFF_HEADS * DIFF_V_DIM
DIFF_SCALE = DIFF_HEAD_DIM ** -0.5

MLA_HEADS = 4
MLA_NOPE = 128
MLA_ROPE = 64
MLA_V = 128
MLA_Q_RANK = 256
MLA_KV_RANK = 128
MLA_WIDTH = MLA_HEADS * MLA_V
MLA_SCALE = (MLA_NOPE + MLA_ROPE) ** -0.5

MIX_WIDTH = DIFF_WIDTH + MLA_WIDTH
ROPE_PAIRS = DIFF_HEAD_DIM // 4

IN_SPLITS = (DIFF_HEADS * 2 * DIFF_HEAD_DIM,
             DIFF_HEADS * 2 * DIFF_HEAD_DIM,
             DIFF_HEADS * DIFF_V_DIM,
             MLA_Q_RANK,
             MLA_KV_RANK,
             MLA_ROPE)
IN_COLS = sum(IN_SPLITS)

N_EXPERTS = 32
TOP_K = 4
D_FF = 1024
SWIGLU_LIMIT = 7.0
SWIGLU_ALPHA = 1.702
MOE_BLOCK = 128


def rmsnorm(x, w):
    xf = x.astype(jnp.float32)
    y = xf * lax.rsqrt(jnp.mean(xf * xf, axis=-1, keepdims=True) + EPS)
    return (y * w.astype(jnp.float32)).astype(x.dtype)

def modulate(h, shift, scale):
    return h * (1 + scale) + shift

def axial_angles(n):
    rows = n // GRID_W
    row = jnp.repeat(jnp.arange(rows, dtype=jnp.float32), GRID_W)
    col = jnp.tile(jnp.arange(GRID_W, dtype=jnp.float32), rows)
    inv = ROPE_THETA ** (-jnp.arange(ROPE_PAIRS, dtype=jnp.float32) / ROPE_PAIRS)
    return jnp.stack([row[:, None] * inv, col[:, None] * inv], axis=1)

def apply_axial_rope(x, ang):
    p = x.shape[-1] // 4
    xf = x.astype(jnp.float32).reshape(*x.shape[:-1], 2, 2, p)
    x1, x2 = xf[..., 0, :], xf[..., 1, :]
    cos, sin = jnp.cos(ang), jnp.sin(ang)
    out = jnp.stack([x1 * cos - x2 * sin, x2 * cos + x1 * sin], axis=-2)
    return out.reshape(x.shape).astype(x.dtype)

def mixer_inputs(h, w_in, q_norm_w, kv_norm_w, w_uq, w_ukv, ang):
    B, n, _ = h.shape
    proj = h @ w_in
    cuts = list(np.cumsum(IN_SPLITS)[:-1])
    dq, dk, dv, cq, ckv, kr = jnp.split(proj, cuts, axis=-1)
    dq = dq.reshape(B, n, DIFF_HEADS, 2, DIFF_HEAD_DIM)
    dk = dk.reshape(B, n, DIFF_HEADS, 2, DIFF_HEAD_DIM)
    dv = dv.reshape(B, n, DIFF_HEADS, DIFF_V_DIM)
    q = (rmsnorm(cq, q_norm_w) @ w_uq).reshape(B, n, MLA_HEADS, MLA_NOPE + MLA_ROPE)
    kv = (rmsnorm(ckv, kv_norm_w) @ w_ukv).reshape(B, n, MLA_HEADS, MLA_NOPE + MLA_V)
    q_nope, q_rope = q[..., :MLA_NOPE], q[..., MLA_NOPE:]
    k_nope, mv = kv[..., :MLA_NOPE], kv[..., MLA_NOPE:]
    if ang is not None:
        dq = apply_axial_rope(dq, ang[:, None, None])
        dk = apply_axial_rope(dk, ang[:, None, None])
        q_rope = apply_axial_rope(q_rope, ang[:, None])
        kr = apply_axial_rope(kr, ang)
    return (dq, dk, dv, q_nope, q_rope, k_nope, kr, mv)

def diff_attend(q, k, v, lam):
    s = jnp.einsum('bqhcd,bkhcd->bchqk', q, k).astype(jnp.float32) * DIFF_SCALE
    p = jax.nn.softmax(s, axis=-1)
    p = p[:, 0] - lam * p[:, 1]
    return jnp.einsum('bhqk,bkhe->bqhe', p.astype(v.dtype), v)

def mla_attend(q_nope, q_rope, k_nope, k_rope, v):
    s = (jnp.einsum('bqhd,bkhd->bhqk', q_nope, k_nope)
         + jnp.einsum('bqhr,bkr->bhqk', q_rope, k_rope)).astype(jnp.float32) * MLA_SCALE
    p = jax.nn.softmax(s, axis=-1)
    return jnp.einsum('bhqk,bkhe->bqhe', p.astype(v.dtype), v)

def to_blocks(t):
    B, n = t.shape[:2]
    return jnp.moveaxis(t.reshape(B, n // Q_BLOCK, Q_BLOCK, *t.shape[2:]), 1, 0)

def from_blocks(t):
    t = jnp.moveaxis(t, 0, 1)
    return t.reshape(t.shape[0], -1, *t.shape[3:])

def merge_heads(o_diff, o_mla, subln_w, lam_init, w_out):
    B, n = o_diff.shape[:2]
    o_diff = rmsnorm(o_diff, subln_w) * (1.0 - lam_init)
    mix = jnp.concatenate([o_diff.reshape(B, n, DIFF_WIDTH), o_mla.reshape(B, n, MLA_WIDTH)], axis=-1)
    return mix @ w_out

def clamped_swiglu(g, u):
    g = jnp.minimum(g, SWIGLU_LIMIT)
    u = jnp.clip(u, -SWIGLU_LIMIT, SWIGLU_LIMIT)
    return g * jax.nn.sigmoid(SWIGLU_ALPHA * g) * (u + 1)

def moe(h, router_w, router_b, w1, b1, w2, b2):
    T, D = h.shape
    logits = (h @ router_w + router_b).astype(jnp.float32)
    top_v, top_i = lax.top_k(logits, TOP_K)
    gates = jax.nn.softmax(top_v, axis=-1).astype(h.dtype)
    flat_e = top_i.reshape(-1)
    flat_tok = jnp.repeat(jnp.arange(T, dtype=jnp.int32), TOP_K)
    order = jnp.argsort(flat_e)
    e_sorted = flat_e[order]
    tok_sorted = flat_tok[order]
    gate_sorted = gates.reshape(-1)[order]
    counts = jnp.bincount(flat_e, length=N_EXPERTS)
    padded = ((counts + MOE_BLOCK - 1) // MOE_BLOCK) * MOE_BLOCK
    ends = jnp.cumsum(padded)
    pad_start = ends - padded
    grp_start = jnp.cumsum(counts) - counts
    n_assign = T * TOP_K
    rank = jnp.arange(n_assign, dtype=jnp.int32) - grp_start[e_sorted]
    dest = pad_start[e_sorted] + rank
    n_blocks = (n_assign + N_EXPERTS * (MOE_BLOCK - 1) + MOE_BLOCK - 1) // MOE_BLOCK
    row_tok = jnp.full((n_blocks * MOE_BLOCK,), T, jnp.int32).at[dest].set(tok_sorted)
    h_pad = jnp.concatenate([h, jnp.zeros((1, D), h.dtype)], axis=0)
    xs = h_pad[row_tok].reshape(n_blocks, MOE_BLOCK, D)
    blk_e = jnp.minimum(jnp.searchsorted(ends, jnp.arange(n_blocks) * MOE_BLOCK, side='right'),
                        N_EXPERTS - 1)

    def expert_block(args):
        xb, e = args
        hid = xb @ w1[e] + b1[e]
        return clamped_swiglu(hid[:, :D_FF], hid[:, D_FF:]) @ w2[e] + b2[e]

    ys = lax.map(expert_block, (xs, blk_e)).reshape(-1, D)
    contrib = ys[dest] * gate_sorted[:, None]
    return jax.ops.segment_sum(contrib, tok_sorted, num_segments=T)

def first_inputs(seed: int = 0) -> dict:
    key = jax.random.key(seed)
    ks = jax.random.split(key, 32)
    f32 = jnp.float32
    L = DEPTH

    def nrm(k, shape, scale):
        return jax.random.normal(k, shape, f32) * scale

    def gain(k, shape):
        return 1.0 + 0.05 * jax.random.normal(k, shape, f32)

    return {
        'x': nrm(ks[0], (BATCH, SEQ, D_MODEL), 1.0),
        'c': nrm(ks[1], (BATCH, D_MODEL), 1.0),
        'ctx': nrm(ks[2], (BATCH, CTX_LEN, D_MODEL), 1.0),
        'c_ctx': nrm(ks[3], (D_MODEL,), 1.0),
        'w_ada': nrm(ks[4], (L, D_MODEL, 6 * D_MODEL), 0.5 * D_MODEL ** -0.5),
        'b_ada': nrm(ks[5], (L, 6 * D_MODEL), 0.02),
        'attn_norm_w': gain(ks[6], (L, D_MODEL)),
        'w_in': nrm(ks[7], (L, D_MODEL, IN_COLS), D_MODEL ** -0.5),
        'q_norm_w': gain(ks[8], (L, MLA_Q_RANK)),
        'kv_norm_w': gain(ks[9], (L, MLA_KV_RANK)),
        'w_uq': nrm(ks[10], (L, MLA_Q_RANK, MLA_HEADS * (MLA_NOPE + MLA_ROPE)), MLA_Q_RANK ** -0.5),
        'w_ukv': nrm(ks[11], (L, MLA_KV_RANK, MLA_HEADS * (MLA_NOPE + MLA_V)), MLA_KV_RANK ** -0.5),
        'lambda_q1': nrm(ks[12], (L, DIFF_HEAD_DIM), 0.1),
        'lambda_k1': nrm(ks[13], (L, DIFF_HEAD_DIM), 0.1),
        'lambda_q2': nrm(ks[14], (L, DIFF_HEAD_DIM), 0.1),
        'lambda_k2': nrm(ks[15], (L, DIFF_HEAD_DIM), 0.1),
        'subln_w': gain(ks[16], (L, DIFF_V_DIM)),
        'w_out': nrm(ks[17], (L, MIX_WIDTH, D_MODEL), MIX_WIDTH ** -0.5),
        'ffn_norm_w': gain(ks[18], (L, D_MODEL)),
        'router_w': nrm(ks[19], (L, D_MODEL, N_EXPERTS), D_MODEL ** -0.5),
        'router_b': nrm(ks[20], (L, N_EXPERTS), 0.01),
        'w1': nrm(ks[21], (L, N_EXPERTS, D_MODEL, 2 * D_FF), D_MODEL ** -0.5),
        'b1': nrm(ks[22], (L, N_EXPERTS, 2 * D_FF), 0.02),
        'w2': nrm(ks[23], (L, N_EXPERTS, D_FF, D_MODEL), D_FF ** -0.5),
        'b2': nrm(ks[24], (L, N_EXPERTS, D_MODEL), 0.02),
        'final_norm_w': gain(ks[25], (D_MODEL,)),
    }

def first_block(x, c, ctx, c_ctx, w_ada, b_ada, attn_norm_w, w_in, q_norm_w, kv_norm_w, w_uq, w_ukv,
              lambda_q1, lambda_k1, lambda_q2, lambda_k2, subln_w, w_out, ffn_norm_w,
              router_w, router_b, w1, b1, w2, b2, final_norm_w):
    B, n, D = x.shape
    ang = axial_angles(n)
    for l in range(DEPTH):
        last = l == DEPTH - 1
        lam_init = 0.8 - 0.6 * math.exp(-0.3 * l)
        mod_lat = (jax.nn.silu(c) @ w_ada[l] + b_ada[l])[:, None, :]
        mod_ctx = (jax.nn.silu(c_ctx) @ w_ada[l] + b_ada[l])[None, None, :]
        sa, sca, ga, sf, scf, gf = jnp.split(mod_lat, 6, axis=-1)
        csa, csca, cga, csf, cscf, cgf = jnp.split(mod_ctx, 6, axis=-1)
        lam = (jnp.exp(jnp.sum(lambda_q1[l].astype(jnp.float32) * lambda_k1[l].astype(jnp.float32)))
               - jnp.exp(jnp.sum(lambda_q2[l].astype(jnp.float32) * lambda_k2[l].astype(jnp.float32)))
               + lam_init)
        mp = (w_in[l], q_norm_w[l], kv_norm_w[l], w_uq[l], w_ukv[l])

        l_dq, l_dk, l_dv, l_qn, l_qr, l_kn, l_kr, l_v = mixer_inputs(
            modulate(rmsnorm(x, attn_norm_w[l]), sa, sca), *mp, ang)
        c_dq, c_dk, c_dv, c_qn, c_qr, c_kn, c_kr, c_v = mixer_inputs(
            modulate(rmsnorm(ctx, attn_norm_w[l]), csa, csca), *mp, None)
        dk_all = jnp.concatenate([c_dk, l_dk], axis=1)
        dv_all = jnp.concatenate([c_dv, l_dv], axis=1)
        kn_all = jnp.concatenate([c_kn, l_kn], axis=1)
        kr_all = jnp.concatenate([c_kr, l_kr], axis=1)
        v_all = jnp.concatenate([c_v, l_v], axis=1)
        o_diff = from_blocks(lax.map(lambda qb: diff_attend(qb, dk_all, dv_all, lam), to_blocks(l_dq)))
        o_mla = from_blocks(lax.map(lambda qs: mla_attend(qs[0], qs[1], kn_all, kr_all, v_all),
                                    (to_blocks(l_qn), to_blocks(l_qr))))
        x_new = x + ga * merge_heads(o_diff, o_mla, subln_w[l], lam_init, w_out[l])
        if not last:
            oc_diff = diff_attend(c_dq, c_dk, c_dv, lam)
            oc_mla = mla_attend(c_qn, c_qr, c_kn, c_kr, c_v)
            ctx = ctx + cga * merge_heads(oc_diff, oc_mla, subln_w[l], lam_init, w_out[l])
        x = x_new

        hf = modulate(rmsnorm(x, ffn_norm_w[l]), sf, scf)
        x = x + gf * moe(hf.reshape(B * n, D), router_w[l], router_b[l], w1[l], b1[l], w2[l], b2[l]).reshape(B, n, D)
        if not last:
            hc = modulate(rmsnorm(ctx, ffn_norm_w[l]), csf, cscf)
            ctx = ctx + cgf * moe(hc.reshape(-1, D), router_w[l], router_b[l], w1[l], b1[l], w2[l], b2[l]).reshape(ctx.shape)
    return rmsnorm(x, final_norm_w)


POOL_WINDOWS = (2, 4, 8, 16)
POOL_GROUP = D_MODEL // 8
POOL_WIDTH = len(POOL_WINDOWS) * POOL_GROUP
DIL_PAIRS = ((128, 1), (512, 4), (2048, 16))
DIL_HEADS_PER_GROUP = 4
DIL_HEADS = len(DIL_PAIRS) * DIL_HEADS_PER_GROUP
DIL_HEAD_DIM = 64
DIL_QKV_WIDTH = DIL_HEADS * DIL_HEAD_DIM
DIL_OUT_WIDTH = DIL_HEADS_PER_GROUP * DIL_HEAD_DIM
REL_BUCKETS = 32
REL_MAX_DIST = 2048
SB_HEADS = 4
SB_HEAD_DIM = 128
SB_WIDTH = SB_HEADS * SB_HEAD_DIM
SB_BLOCK = 128
S5_WIDTH = D_MODEL // 2
S5_CH = 16
S5_GROUPS = S5_WIDTH // S5_CH
S5_STATE = 64
FFN_HIDDEN = ((8 * D_MODEL + 3 * 256 - 1) // (3 * 256)) * 256
N_BRANCHES = 4
IN_WIDTH = POOL_WIDTH + 3 * DIL_QKV_WIDTH + 3 * SB_WIDTH + S5_WIDTH
BRANCH_WIDTHS = (POOL_WIDTH, DIL_OUT_WIDTH, SB_WIDTH, S5_WIDTH)
BRANCH_WIDTH = sum(BRANCH_WIDTHS)


def rmsnorm_2(x, g):
    xf = x.astype(jnp.float32)
    y = xf * lax.rsqrt(jnp.mean(xf * xf, axis=-1, keepdims=True) + EPS)
    return (y * g.astype(jnp.float32)).astype(x.dtype)

def pool_mixer(u, w_grp, scale):
    B_, S_, _ = u.shape
    uf = u.astype(jnp.float32)
    cs = jnp.concatenate([jnp.zeros_like(uf[:, :1]), jnp.cumsum(uf, axis=1)], axis=1)
    t = jnp.arange(S_)
    outs = []
    for gi, w in enumerate(POOL_WINDOWS):
        sl = slice(gi * POOL_GROUP, (gi + 1) * POOL_GROUP)
        lo = jnp.maximum(t + 1 - w, 0)
        cnt = (t + 1 - lo).astype(jnp.float32)
        mean = (cs[:, 1:, sl] - cs[:, lo, sl]) / cnt[None, :, None]
        outs.append(mean - uf[:, :, sl])
    p = jnp.stack(outs, axis=2)
    y = jnp.einsum('bsgc,gcd->bsgd', p, w_grp.astype(jnp.float32)).reshape(B_, S_, POOL_WIDTH)
    return (y * scale.astype(jnp.float32)).astype(u.dtype)

def t5_bucket(dist):
    exact = REL_BUCKETS // 2
    df = jnp.maximum(dist, 1).astype(jnp.float32)
    large = exact + (jnp.log(df / exact) / math.log(REL_MAX_DIST / exact)
                     * (REL_BUCKETS - exact)).astype(jnp.int32)
    large = jnp.minimum(large, REL_BUCKETS - 1)
    return jnp.where(dist < exact, dist, large)

def dilated_group(q, k, v, bias_tab, window, dil):
    B_, S_, H, E = q.shape
    band = window // dil
    L = S_ // dil
    nb = -(-L // band)
    Lp = nb * band

    def to_sub(a):
        a = a.reshape(B_, L, dil, H, E).transpose(0, 2, 3, 1, 4)
        return jnp.pad(a, ((0, 0), (0, 0), (0, 0), (0, Lp - L), (0, 0)))

    def band_keys(a):
        a = jnp.pad(a, ((0, 0), (0, 0), (0, 0), (band, 0), (0, 0))).reshape(B_, dil, H, nb + 1, band, E)
        return jnp.concatenate([a[:, :, :, :-1], a[:, :, :, 1:]], axis=4)

    qb = to_sub(q).reshape(B_, dil, H, nb, band, E)
    kb = band_keys(to_sub(k))
    vb = band_keys(to_sub(v))
    i = jnp.arange(band)[:, None]
    c = jnp.arange(2 * band)[None, :]
    dist_sub = band + i - c
    in_band = (dist_sub >= 0) & (dist_sub <= band)
    n = jnp.arange(nb)[:, None, None]
    mask = in_band[None] & ((n > 0) | (c[None] >= band))
    buckets = t5_bucket(jnp.clip(dist_sub, 0, band) * dil)
    bias = bias_tab.astype(jnp.float32)[buckets].transpose(2, 0, 1)
    s = jnp.einsum('bdhnqe,bdhnke->bdhnqk', qb, kb, preferred_element_type=jnp.float32) / math.sqrt(E)
    s = jnp.where(mask[None, None, None], s + bias[None, None, :, None], -1e30)
    m = jnp.max(s, axis=-1, keepdims=True)
    p = jnp.exp(s - m)
    den = jnp.sum(p, axis=-1, keepdims=True)
    o = jnp.einsum('bdhnqk,bdhnke->bdhnqe', p, vb.astype(jnp.float32)) / den
    lse = (m + jnp.log(den))[..., 0]
    o = o.reshape(B_, dil, H, Lp, E)[:, :, :, :L].transpose(0, 3, 1, 2, 4).reshape(B_, S_, H, E)
    lse = lse.reshape(B_, dil, H, Lp)[:, :, :, :L].transpose(0, 3, 1, 2).reshape(B_, S_, H)
    return o, lse

def dilated_attention(qkv, rel_bias):
    B_, S_ = qkv.shape[:2]
    outs, lses = [], []
    for g, (window, dil) in enumerate(DIL_PAIRS):
        hs = slice(g * DIL_HEADS_PER_GROUP, (g + 1) * DIL_HEADS_PER_GROUP)
        o, lse = dilated_group(qkv[:, :, 0, hs], qkv[:, :, 1, hs], qkv[:, :, 2, hs],
                               rel_bias[:, hs], window, dil)
        outs.append(o)
        lses.append(lse)
    o = jnp.stack(outs, axis=0)
    alpha = jax.nn.softmax(jnp.stack(lses, axis=0), axis=0)
    y = jnp.sum(alpha[..., None] * o, axis=0)
    return y.reshape(B_, S_, DIL_OUT_WIDTH).astype(qkv.dtype)

def stick_breaking_attention(qkv):
    B_, S_, _, H, E = qkv.shape
    nb = S_ // SB_BLOCK
    qh = qkv[:, :, 0].transpose(0, 2, 1, 3)
    kh = qkv[:, :, 1].transpose(0, 2, 1, 3)
    vh = qkv[:, :, 2].transpose(0, 2, 1, 3).astype(jnp.float32)
    qblk = qh.reshape(B_, H, nb, SB_BLOCK, E).transpose(2, 0, 1, 3, 4)
    key_pos = jnp.arange(S_)

    def one_block(args):
        qb, bi = args
        z = jnp.einsum('bhqe,bhke->bhqk', qb, kh, preferred_element_type=jnp.float32) / math.sqrt(E)
        q_pos = bi * SB_BLOCK + jnp.arange(SB_BLOCK)
        mask = key_pos[None, :] < q_pos[:, None]
        log_not = jnp.where(mask, jax.nn.log_sigmoid(-z), 0.0)
        excl = lax.cumsum(log_not, axis=3, reverse=True) - log_not
        w = jnp.where(mask, jnp.exp(jax.nn.log_sigmoid(z) + excl), 0.0)
        return jnp.einsum('bhqk,bhke->bhqe', w, vh)

    o = lax.map(one_block, (qblk, jnp.arange(nb)))
    return o.transpose(1, 0, 3, 2, 4).reshape(B_, S_, SB_WIDTH).astype(qkv.dtype)

def s5_mixer(u, a_re, a_im, log_dt, b_re, b_im, c_re, c_im, d_skip, w_glu):
    B_, S_, _ = u.shape
    f32 = jnp.float32
    uf = u.astype(f32).reshape(B_, S_, S5_GROUPS, S5_CH)
    lam = lax.complex(a_re.astype(f32), a_im.astype(f32))
    dt = jnp.exp(log_dt.astype(f32))[:, None]
    lam_bar = jnp.exp(lam * dt)
    b_t = lax.complex(b_re.astype(f32), b_im.astype(f32))
    b_bar = ((lam_bar - 1.0) / lam)[:, :, None] * b_t
    bu = jnp.einsum('gpc,bsgc->bsgp', b_bar, uf.astype(jnp.complex64))
    a = jnp.broadcast_to(lam_bar, (1, S_) + lam_bar.shape)

    def combine(left, right):
        a_l, b_l = left
        a_r, b_r = right
        return a_r * a_l, a_r * b_l + b_r

    _, h = lax.associative_scan(combine, (a, bu), axis=1)
    c_t = lax.complex(c_re.astype(f32), c_im.astype(f32))
    y = jnp.real(jnp.einsum('gcp,bsgp->bsgc', c_t, h)) + d_skip.astype(f32).reshape(S5_GROUPS, S5_CH) * uf
    y = jax.nn.gelu(y.reshape(B_, S_, S5_WIDTH))
    gl = y @ w_glu.astype(f32)
    y = gl[..., :S5_WIDTH] * jax.nn.sigmoid(gl[..., S5_WIDTH:])
    return y.astype(u.dtype)

def second_inputs(seed: int = 0) -> dict:
    key = jax.random.key(seed)
    ks = jax.random.split(key, 22)
    nrm = jax.random.normal
    f32 = jnp.float32
    x = nrm(ks[0], (BATCH, SEQ, D_MODEL), f32)
    attn_norm_g = 1.0 + 0.02 * nrm(ks[1], (DEPTH, D_MODEL), f32)
    w_in = nrm(ks[2], (DEPTH, D_MODEL, IN_WIDTH), f32) * D_MODEL ** -0.5
    pool_w = nrm(ks[3], (DEPTH, len(POOL_WINDOWS), POOL_GROUP, POOL_GROUP), f32) * POOL_GROUP ** -0.5
    pool_scale = 1.0 + 0.02 * nrm(ks[4], (DEPTH, POOL_WIDTH), f32)
    rel_bias = 0.5 * nrm(ks[5], (REL_BUCKETS, DIL_HEADS), f32)
    s5_a_re = -0.5 + 0.01 * nrm(ks[6], (DEPTH, S5_GROUPS, S5_STATE), f32)
    s5_a_im = jnp.pi * jnp.arange(S5_STATE, dtype=f32)[None, None, :] + 0.01 * nrm(ks[7], (DEPTH, S5_GROUPS, S5_STATE), f32)
    s5_log_dt = jax.random.uniform(ks[8], (DEPTH, S5_GROUPS), f32, minval=math.log(1e-3), maxval=math.log(1e-1))
    s5_b_re = nrm(ks[9], (DEPTH, S5_GROUPS, S5_STATE, S5_CH), f32) * (2 * S5_CH) ** -0.5
    s5_b_im = nrm(ks[10], (DEPTH, S5_GROUPS, S5_STATE, S5_CH), f32) * (2 * S5_CH) ** -0.5
    s5_c_re = nrm(ks[11], (DEPTH, S5_GROUPS, S5_CH, S5_STATE), f32) * S5_STATE ** -0.5
    s5_c_im = nrm(ks[12], (DEPTH, S5_GROUPS, S5_CH, S5_STATE), f32) * S5_STATE ** -0.5
    s5_d = nrm(ks[13], (DEPTH, S5_WIDTH), f32)
    s5_w_glu = nrm(ks[14], (DEPTH, S5_WIDTH, 2 * S5_WIDTH), f32) * S5_WIDTH ** -0.5
    row_scale = jnp.concatenate([jnp.full((w,), w ** -0.5, f32) for w in BRANCH_WIDTHS])
    w_branch = nrm(ks[15], (DEPTH, BRANCH_WIDTH, D_MODEL), f32) * row_scale[None, :, None]
    w_gate = nrm(ks[16], (DEPTH, N_BRANCHES, D_MODEL, D_MODEL), f32) * D_MODEL ** -0.5
    w_out = nrm(ks[17], (DEPTH, D_MODEL, D_MODEL), f32) * D_MODEL ** -0.5
    ffn_norm_g = 1.0 + 0.02 * nrm(ks[18], (DEPTH, D_MODEL), f32)
    w_up = nrm(ks[19], (DEPTH, D_MODEL, 2 * FFN_HIDDEN), f32) * D_MODEL ** -0.5
    w_down = nrm(ks[20], (DEPTH, FFN_HIDDEN, D_MODEL), f32) * FFN_HIDDEN ** -0.5
    final_norm_g = 1.0 + 0.02 * nrm(ks[21], (D_MODEL,), f32)
    return {'x': x, 'attn_norm_g': attn_norm_g, 'w_in': w_in, 'pool_w': pool_w,
            'pool_scale': pool_scale, 'rel_bias': rel_bias, 's5_a_re': s5_a_re,
            's5_a_im': s5_a_im, 's5_log_dt': s5_log_dt, 's5_b_re': s5_b_re, 's5_b_im': s5_b_im,
            's5_c_re': s5_c_re, 's5_c_im': s5_c_im, 's5_d': s5_d, 's5_w_glu': s5_w_glu,
            'w_branch': w_branch, 'w_gate': w_gate, 'w_out': w_out, 'ffn_norm_g': ffn_norm_g,
            'w_up': w_up, 'w_down': w_down, 'final_norm_g': final_norm_g}

def second_block(x, attn_norm_g, w_in, pool_w, pool_scale, rel_bias, s5_a_re, s5_a_im, s5_log_dt,
              s5_b_re, s5_b_im, s5_c_re, s5_c_im, s5_d, s5_w_glu, w_branch, w_gate, w_out,
              ffn_norm_g, w_up, w_down, final_norm_g):
    B_, S_, _ = x.shape
    o1 = POOL_WIDTH
    o2 = o1 + 3 * DIL_QKV_WIDTH
    o3 = o2 + 3 * SB_WIDTH
    for l in range(DEPTH):
        xn = rmsnorm_2(x, attn_norm_g[l])
        proj = xn @ w_in[l]
        u_pool = proj[..., :o1]
        qkv_dil = proj[..., o1:o2].reshape(B_, S_, 3, DIL_HEADS, DIL_HEAD_DIM)
        qkv_sb = proj[..., o2:o3].reshape(B_, S_, 3, SB_HEADS, SB_HEAD_DIM)
        u_s5 = proj[..., o3:]
        y_pool = pool_mixer(u_pool, pool_w[l], pool_scale[l])
        y_dil = dilated_attention(qkv_dil, rel_bias)
        y_sb = stick_breaking_attention(qkv_sb)
        y_s5 = s5_mixer(u_s5, s5_a_re[l], s5_a_im[l], s5_log_dt[l], s5_b_re[l], s5_b_im[l],
                        s5_c_re[l], s5_c_im[l], s5_d[l], s5_w_glu[l])
        merged = jnp.zeros_like(x)
        row = 0
        for bi, yb in enumerate((y_pool, y_dil, y_sb, y_s5)):
            width = BRANCH_WIDTHS[bi]
            gate = jax.nn.sigmoid(xn @ w_gate[l, bi])
            merged = merged + gate * (yb @ w_branch[l, row:row + width])
            row += width
        x = x + merged @ w_out[l]
        hn = rmsnorm_2(x, ffn_norm_g[l])
        gu = hn @ w_up[l]
        h = jax.nn.silu(gu[..., :FFN_HIDDEN]) * gu[..., FFN_HIDDEN:]
        x = x + h @ w_down[l]
    return rmsnorm_2(x, final_norm_g)


def setup_inputs(seed=0):
    out = dict(first_inputs(seed))
    for name, value in second_inputs(seed + 1).items():
        if name != "x":
            out[name + "_2"] = value
    return out


def reference(
    x, c, ctx, c_ctx, w_ada, b_ada, attn_norm_w, w_in, q_norm_w, kv_norm_w, w_uq, w_ukv,
    lambda_q1, lambda_k1, lambda_q2, lambda_k2, subln_w, w_out, ffn_norm_w, router_w, router_b,
    w1, b1, w2, b2, final_norm_w, attn_norm_g_2, w_in_2, pool_w_2, pool_scale_2, rel_bias_2,
    s5_a_re_2, s5_a_im_2, s5_log_dt_2, s5_b_re_2, s5_b_im_2, s5_c_re_2, s5_c_im_2, s5_d_2,
    s5_w_glu_2, w_branch_2, w_gate_2, w_out_2, ffn_norm_g_2, w_up_2, w_down_2, final_norm_g_2,
):
    x = first_block(
        x, c, ctx, c_ctx, w_ada, b_ada, attn_norm_w, w_in, q_norm_w, kv_norm_w, w_uq, w_ukv,
        lambda_q1, lambda_k1, lambda_q2, lambda_k2, subln_w, w_out, ffn_norm_w, router_w,
        router_b, w1, b1, w2, b2, final_norm_w,
    )
    return second_block(
        x, attn_norm_g_2, w_in_2, pool_w_2, pool_scale_2, rel_bias_2, s5_a_re_2, s5_a_im_2,
        s5_log_dt_2, s5_b_re_2, s5_b_im_2, s5_c_re_2, s5_c_im_2, s5_d_2, s5_w_glu_2, w_branch_2,
        w_gate_2, w_out_2, ffn_norm_g_2, w_up_2, w_down_2, final_norm_g_2,
    )


_drawn_inputs = setup_inputs


def setup_inputs(seed=0):
    import zlib

    import numpy as np

    out = dict(_drawn_inputs(seed))
    spreads = {}
    factors = {'attn_norm_w': 3.099,
     'q_norm_w': 8.0,
     'kv_norm_w': 8.0,
     'lambda_q1': 3.338,
     'lambda_q2': 200.0,
     'lambda_k2': 3.135,
     'subln_w': 3.532,
     'router_b': 10.663,
     'b1': 8.0,
     'b2': 8.0,
     'attn_norm_g_2': 4.152,
     'pool_scale_2': 6.681,
     's5_a_re_2': 64.0,
     's5_a_im_2': 31.4,
     's5_log_dt_2': 33.096,
     's5_b_re_2': 43.752,
     's5_b_im_2': 44.896,
     's5_c_re_2': 44.16,
     's5_c_im_2': 43.416,
     'ffn_norm_g_2': 13.331,
     'final_norm_g_2': 22.829,
     'rel_bias_2': 3.505}
    for name, (base, spread) in spreads.items():
        noise = np.random.default_rng([zlib.crc32(name.encode()), seed]).standard_normal(out[name].shape)
        drawn = base * np.exp(spread * noise) if base else spread * noise
        out[name] = jnp.asarray(drawn.astype(out[name].dtype))
    for name, factor in factors.items():
        out[name] = (out[name] * factor).astype(out[name].dtype)
    return out
```

```python
from contextlib import ExitStack

import concourse.bass as bass
from concourse import mybir

ALU = mybir.AluOpType
ACT = mybir.ActivationFunctionType
F32 = mybir.dt.float32
AX_X = mybir.AxisListType.X
EPS = 1e-6
NS = 8
SLOT = 2048
NE = 32
BIG = 1.0e30

PAR = {}
CST = {}


def _table(into, rows):
    at = 0
    for name, n in rows:
        into[name] = (at, at + n)
        at += n
    return at


PAR_N = _table(PAR, [("c2", 16), ("b_ada", 48), ("attn_w", 8), ("qn_w", 2), ("kvn_w", 1), ("sub_w", 1),
                     ("ffn_w", 8), ("fin_w", 8), ("attn2_w", 8), ("ffn2_w", 8), ("fin2_w", 8), ("lam", 4),
                     ("b1", 512), ("pscale", 4), ("s5_are", 16), ("s5_aim", 16), ("s5_ldt", 16), ("s5_d", 4)])
CST_N = _table(CST, [("ident", 128), ("ones", 128), ("rot", 128), ("tri", 128), ("cos", 256), ("sin", 256),
                     ("m01", 384), ("mneg", 384), ("inv", 1024), ("hot", 1152), ("eps", 1)])


class Done:

    def __init__(self, eng, sem=None, val=None):
        self.eng, self.sem, self.val, self.asked = eng, sem, val, sem is not None


class Rot:

    def __init__(self, aps):
        self.aps, self.users, self.n = aps, [[] for _ in aps], -1

    def get(self):
        self.n += 1
        i = self.n % len(self.aps)
        users, self.users[i] = self.users[i], []
        return self.aps[i], users, self.users[i]


def build(nc, I, out):
    ctx = ExitStack()
    with ctx:
        def sb(name, n):
            return ctx.enter_context(nc.sbuf_tensor(name, [128, n], F32))

        ring = sb("ring", NS * SLOT)
        par = sb("par", PAR_N)
        cst = sb("cst", CST_N)
        xT = sb("xT", 2048)
        small = sb("small", 400)
        AR = 28600
        arena = sb("arena", AR)
        PS = ctx.enter_context(nc.psum_tensor("PS", [128, 4096], F32))
        skew = nc.dram_tensor("skew_scratch", [12, 128, 384], F32, kind="Internal").ap()

        esem = {e: ctx.enter_context(nc.semaphore("n_" + e)) for e in ("pe", "act", "dve", "pool")}
        slot_sem = [ctx.enter_context(nc.semaphore(f"slot{i}")) for i in range(NS)]
        queue = {e: [] for e in ("pe", "act", "dve", "pool", "sp")}

        def flat(after):
            for a in after:
                if a is None:
                    continue
                if isinstance(a, Done):
                    yield a
                else:
                    yield from flat(a)

        def op(eng, fn, *after):
            waits = list(flat(after))
            for w in waits:
                w.asked = True
            d = Done(eng)
            queue[eng].append((fn, waits, d))
            return d

        nsem = [0]

        def dma(eng, dst, src, *after, sem=None, val=16):
            waits = list(flat(after))
            for w in waits:
                w.asked = True
            if sem is None:
                sem = ctx.enter_context(nc.semaphore(f"dma{nsem[0]}"))
                nsem[0] += 1
            d = Done(eng, sem, val)
            queue[eng].append((lambda e: e.dma_start(dst, src), waits, d))
            return d

        def mm(o, l, r, start, stop, *after):
            return op("pe", lambda e: e.matmul(o, l, r, start=start, stop=stop, skip_group_check=True), *after)

        def tr(o, i, *after):
            n = i.shape[0]
            return op("pe", lambda e: e.transpose(o, i, C("ident")[0:n, 0:n]), *after)

        def act(o, i, f, *after, scale=1.0, bias=0.0, acc=None):
            if acc is None:
                return op("act", lambda e: e.activation(o, i, f, bias=bias, scale=scale), *after)
            return op("act", lambda e: e.activation(o, i, f, bias=bias, scale=scale, accum_out=acc), *after)

        def tt(o, a, b, f, *after, eng="dve"):
            return op(eng, lambda e: e.tensor_tensor(o, a, b, f), *after)

        def ts(o, a, s1, f1, s2, f2, *after, eng="dve"):
            if f2 is None:
                return op(eng, lambda e: e.tensor_scalar(o, a, s1, None, f1), *after)
            return op(eng, lambda e: e.tensor_scalar(o, a, s1, s2, f1, f2), *after)

        def stt(o, a, s, b, f1, f2, *after):
            return op("dve", lambda e: e.scalar_tensor_tensor(out=o, in0=a, scalar=s, in1=b, op0=f1, op1=f2), *after)

        def recip(o, a, *after):
            return op("dve", lambda e: e.reciprocal(o, a), *after)

        def copy(o, a, *after, eng="dve"):
            if eng == "act":
                return act(o, a, ACT.Copy, *after)
            return op(eng, lambda e: e.tensor_copy(o, a), *after)

        def memset(o, v, *after, eng="pool"):
            return op(eng, lambda e: e.memset(o, v), *after)

        def C(name):
            a, b = CST[name]
            return cst[:, a:b]

        def Pm(name, i=None):
            a, b = PAR[name]
            return par[:, a:b] if i is None else par[:, a + i:a + i + 1]

        at = [0, 0]

        def take(*dims):
            n = 1
            for d in dims:
                n *= d
            a = at[0]
            at[0] += n
            assert at[0] <= AR, at[0]
            v = arena[:, a:a + n]
            if len(dims) == 2:
                v = v.rearrange("p (a b) -> p a b", a=dims[0])
            if len(dims) == 3:
                v = v.rearrange("p (a b c) -> p a b c", a=dims[0], b=dims[1])
            return v

        def sm(n=1):
            a = at[1]
            at[1] += n
            assert at[1] <= 400
            return small[:, a:a + n]

        def barrier():
            return [queue[e][-1][2] for e in ("pe", "act", "dve", "pool") if queue[e]]

        banks = Rot([PS[:, i * 512:(i + 1) * 512] for i in range(8)])

        loads = [0]
        release = [None] * NS

        class W:

            def __init__(self, src, n, per=4):
                k = src.shape[0] // 128
                self.per, self.slots = per, []
                for a in range(0, k, per):
                    m = min(per, k - a)
                    i = loads[0]
                    loads[0] += 1
                    s = i % NS
                    v = ring[:, s * SLOT:s * SLOT + m * n].rearrange("p (k n) -> p k n", k=m)
                    d = dma("sp", v, src[a * 128:(a + m) * 128, :].rearrange("(k p) n -> p k n", p=128),
                            release[s], sem=slot_sem[s], val=16 * (i // NS + 1))
                    release[s] = None
                    self.slots.append((v, d, s))

            def ap(self, k, a, b):
                return self.slots[k // self.per][0][:, k % self.per, a:b]

            def ready(self, k):
                return self.slots[k // self.per][1]

            def free(self, d):
                for _, _, s in self.slots:
                    release[s] = d

        def group(o, w, a, b, rhs, K, *after):
            for k in range(K):
                d = mm(o, w.ap(k, a, b), rhs(k), k == 0, k == K - 1, after if k == 0 else None, w.ready(k))
            return d

        ctxT = take(8, 256)
        xv = xT[:, :].rearrange("p (k t) -> p k t", k=8)
        d_par = dma("act", par[:, :], I["par"])
        d_cst = dma("act", cst[:, :], I["cst"])
        d_ctx = dma("act", ctxT, I["ctxT"].rearrange("(k p) t -> p k t", p=128))
        d_x = dma("act", xv, I["xT"].rearrange("(k p) t -> p k t", p=128))
        eps = cst[:, CST["eps"][0]:CST["eps"][1]]
        ones = C("ones")

        def rms(src, K, n, D, rb, sq, *after):
            bk, free, users = banks.get()
            for k in range(K):
                s, sfree, suse = sq.get()
                q = act(s[:, 0:n], src(k), ACT.Square, after, sfree)
                d = mm(bk[:, 0:n], ones, s[:, 0:n], k == 0, k == K - 1, q, free if k == 0 else None, d_cst)
                suse.append(d)
            r = act(rb, bk[:, 0:n], ACT.Sqrt, d, scale=1.0 / D, bias=eps)
            users.append(r)
            return recip(rb, rb, r)

        e2 = sm(16)
        sc2 = sm(16)
        c2 = Pm("c2")
        d = act(e2, c2, ACT.Exp, d_par, scale=-1.0)
        d = ts(e2, e2, 1.0, ALU.add, None, None, d)
        d = recip(e2, e2, d)
        d_silu = tt(sc2, c2, e2, ALU.mult, d)
        c2v = sc2.rearrange("p (k v) -> p k v", v=2)
        mods = sm(96).rearrange("p (j v) -> p j v", v=2)
        d_mod = {}

        def modulation(m):
            bk, free, users = banks.get()
            for c in range(2):
                w = W(I["w_ada"][:, m * 1024 + c * 512:m * 1024 + (c + 1) * 512], 512)
                for j in range(4):
                    d = group(bk[:, (c * 4 + j) * 2:(c * 4 + j) * 2 + 2], w, j * 128, (j + 1) * 128,
                              lambda k: c2v[:, k, :], 8, d_silu, free)
                w.free(d)
            a, b = PAR["b_ada"]
            bias = par[:, a + m * 8:a + m * 8 + 8].unsqueeze(2).to_broadcast([128, 8, 2])
            d = tt(mods[:, m * 8:m * 8 + 8, :], bk[:, 0:16].rearrange("p (j v) -> p j v", v=2), bias, ALU.add, d)
            users.append(d)
            d_mod[m] = d

        modulation(0)
        modulation(1)
        aw = sm(16).rearrange("p (j v) -> p j v", v=2)
        d = ts(aw, mods[:, 8:16, :], 1.0, ALU.add, None, None, d_mod[1])
        d_aw = tt(aw, aw, Pm("attn_w").unsqueeze(2).to_broadcast([128, 8, 2]), ALU.mult, d)

        hT = take(8, 512)
        sq = Rot([take(512) for _ in range(2)])
        rbs = take(2, 256)
        d_h = []
        for v, src, dd in ((1, ctxT, d_ctx), (0, xv, d_x)):
            t0 = 0 if v else 256
            r = rms(lambda k: src[:, k, :], 8, 256, 1024, rbs[:, v, :], sq, dd)
            for k in range(8):
                d = stt(hT[:, k, t0:t0 + 256], src[:, k, :], aw[:, k, v:v + 1], rbs[:, v, :], ALU.mult, ALU.mult, r, d_aw)
                d = ts(hT[:, k, t0:t0 + 256], hT[:, k, t0:t0 + 256], mods[:, k, v:v + 1], ALU.add, None, None, d, d_mod[0])
            d_h.append(d)

        w_in = I["w_in"]
        raw = Rot([take(512) for _ in range(3)])

        def rope(bk, rows, n0, n, dst, d, users):
            s, sfree, suse = raw.get()
            c1 = copy(s[0:rows, 0:n], bk[0:rows, 0:n], d, sfree, eng="act")
            users.append(c1)
            b2, free2, users2 = banks.get()
            m = mm(b2[0:rows, 0:256], C("rot")[0:rows, 0:rows], s[0:rows, n0:n], True, True, c1, free2)
            a1 = tt(dst[0:rows, n0:n], s[0:rows, n0:n], C("cos")[0:rows, :], ALU.mult, c1)
            s2, s2free, s2use = raw.get()
            a2 = tt(s2[0:rows, 0:256], b2[0:rows, 0:256], C("sin")[0:rows, :], ALU.mult, m, s2free)
            users2.append(a2)
            a3 = tt(dst[0:rows, n0:n], dst[0:rows, n0:n], s2[0:rows, 0:256], ALU.add, a1, a2)
            s2use.append(a3)
            suse.append([m, a1])
            if n0:
                c2 = copy(dst[0:rows, 0:n0], s[0:rows, 0:n0], c1, eng="act")
                suse.append(c2)
                return [a3, c2]
            return a3

        dq = take(4, 256)
        dk = take(4, 512)
        dv = take(4, 512)
        w = W(w_in[:, 0:512], 512)
        d_dq, d_dk, d_dv = [], [], []
        for j in range(4):
            bk, free, users = banks.get()
            d = group(bk[:, 0:256], w, j * 128, (j + 1) * 128, lambda k: hT[:, k, 256:512], 8, d_h, free)
            d_dq.append(rope(bk, 128, 0, 256, dq[:, j, :], d, users))
        w.free(d)
        w = W(w_in[:, 512:1024], 512)
        for j in range(4):
            bk, free, users = banks.get()
            d = group(bk, w, j * 128, (j + 1) * 128, lambda k: hT[:, k, :], 8, free)
            d_dk.append(rope(bk, 128, 256, 512, dk[:, j, :], d, users))
        w.free(d)
        w = W(w_in[:, 1024:1536], 512)
        for t in range(4):
            bk, free, users = banks.get()
            for k in range(8):
                d = mm(bk, hT[:, k, t * 128:(t + 1) * 128], w.ap(k, 0, 512), k == 0, k == 7, free, w.ready(k))
            d_dv.append(copy(dv[:, t, :], bk, d, eng="act"))
            users.append(d_dv[-1])
        w.free(d)
        cq = take(2, 256)
        ckv = take(512)
        kr = take(512)
        w = W(w_in[:, 1536:1984], 448)
        d_cq = []
        for j in range(2):
            bk, free, users = banks.get()
            d = group(bk[:, 0:256], w, j * 128, (j + 1) * 128, lambda k: hT[:, k, 256:512], 8, free)
            d_cq.append(copy(cq[:, j, :], bk[:, 0:256], d))
            users.append(d_cq[-1])
        bk, free, users = banks.get()
        d = group(bk, w, 256, 384, lambda k: hT[:, k, :], 8, free)
        d_ckv = copy(ckv, bk, d)
        users.append(d_ckv)
        bk, free, users = banks.get()
        d = group(bk[0:64, :], w, 384, 448, lambda k: hT[:, k, :], 8, free)
        w.free(d)
        d_kr = rope(bk, 64, 256, 512, kr, d, users)

        rq = take(256)
        rk = take(512)
        r = rms(lambda k: cq[:, k, :], 2, 256, 256, rq, sq, d_cq)
        for j in range(2):
            d_cqn = stt(cq[:, j, :], cq[:, j, :], Pm("qn_w", j), rq, ALU.mult, ALU.mult, r)
        r = rms(lambda k: ckv, 1, 512, 128, rk, sq, d_ckv)
        d_ckvn = stt(ckv, ckv, Pm("kvn_w"), rk, ALU.mult, ALU.mult, r)
        wq = W(I["w_uq"], 768, per=2)
        qn = take(4, 256)
        qr = take(4, 256)
        d_qn, d_qr = [], []
        for h in range(4):
            bk, free, users = banks.get()
            d = group(bk[:, 0:256], wq, h * 192, h * 192 + 128, lambda k: cq[:, k, :], 2, free, d_cqn)
            d_qn.append(copy(qn[:, h, :], bk[:, 0:256], d, eng="act"))
            users.append(d_qn[-1])
            bk, free, users = banks.get()
            d = group(bk[0:64, 0:256], wq, h * 192 + 128, h * 192 + 192, lambda k: cq[:, k, :], 2, free)
            d_qr.append(rope(bk, 64, 0, 256, qr[:, h, :], d, users))
        wq.free(d)
        wk = W(I["w_ukv"], 1024, per=1)
        kn = take(4, 512)
        mv = take(4, 512)
        d_kn, d_mv = [], []
        for h in range(4):
            bk, free, users = banks.get()
            d = mm(bk, wk.ap(0, h * 256, h * 256 + 128), ckv, True, True, free, d_ckvn, wk.ready(0))
            d_kn.append(copy(kn[:, h, :], bk, d, eng="act"))
            users.append(d_kn[-1])
        wv = wk.ap(0, 0, 1024).rearrange("p (h c) -> p h c", h=4)[:, :, 128:256]
        for t in range(4):
            bk, free, users = banks.get()
            d = mm(bk.rearrange("p (h c) -> p h c", h=4), ckv[:, t * 128:(t + 1) * 128], wv, True, True, free)
            d_mv.append(copy(mv[:, t, :], bk, d))
            users.append(d_mv[-1])
        wk.free(d)

        lp = sm(2)
        lam4 = Pm("lam")
        d = tt(lp[0:64, :], lam4[0:64, 0:2], lam4[0:64, 2:4], ALU.mult, d_par)
        bk, free, users = banks.get()
        d = mm(bk[:, 0:2], ones[0:64, :], lp[0:64, :], True, True, d, free)
        le = sm(2)
        d = act(le, bk[:, 0:2], ACT.Exp, d)
        users.append(d)
        nlam = sm()
        d = tt(nlam, le[:, 1:2], le[:, 0:1], ALU.subtract, d)
        lam_init = 0.8 - 0.6 * 1.0
        d_lam = ts(nlam, nlam, -lam_init, ALU.add, None, None, d)

        Pb = Rot([take(512) for _ in range(4)])
        PT = Rot([take(512) for _ in range(2)])
        mix = take(8, 256)

        def softmax(bk, n, scale, d, users):
            mx, den = sm(), sm()
            d1 = op("dve", lambda e: e.tensor_reduce(mx, bk[:, 0:n], AX_X, ALU.max), d)
            d1 = ts(mx, mx, -scale, ALU.mult, None, None, d1)
            p, pfree, puse = Pb.get()
            d2 = act(p[:, 0:n], bk[:, 0:n], ACT.Exp, d1, pfree, scale=scale, bias=mx, acc=den)
            users.append(d2)
            d3 = recip(den, den, d2)
            return p, den, [d2, d3], puse

        def values(p, n, dp, puse, V, dv_, o, osl, dd, first):
            bk, free, users = banks.get()
            for b in range(n):
                d = tr(bk[:, b * 128:(b + 1) * 128], p[:, b * 128:(b + 1) * 128], dp, free)
            puse.append(d)
            t, tfree, tuse = PT.get()
            d = copy(t[:, 0:n * 128], bk[:, 0:n * 128], d, tfree, eng="act")
            users.append(d)
            for b in range(n):
                m = mm(o[:, osl], V(b), t[:, b * 128:(b + 1) * 128], b == 0, b == n - 1, d, dv_, dd if b == 0 else None)
            tuse.append(m)
            return m

        d_mix = [None] * 8
        for h in range(4):
            ob, ofree, ousers = banks.get()
            for t in range(2):
                ps = []
                for c in range(2):
                    bk, free, users = banks.get()
                    rows = slice(c * 64, c * 64 + 64)
                    d = mm(bk, dq[rows, h, t * 128:(t + 1) * 128], dk[rows, h, :], True, True, free, d_dq[h], d_dk[h])
                    ps.append(softmax(bk, 512, 0.125, d, users))
                (p0, r0, e0, u0), (p1, r1, e1, u1) = ps
                d = tt(r1, r1, nlam, ALU.mult, e1, d_lam)
                d = ts(p1, p1, r1, ALU.mult, None, None, d)
                d = stt(p0, p0, r0, p1, ALU.mult, ALU.add, d, e0)
                u1.append(d)
                d = values(p0, 4, d, u0, lambda b: dv[:, b, h * 128:(h + 1) * 128], d_dv, ob,
                           slice(t * 128, t * 128 + 128), ofree, t == 0)
            dc = copy(mix[:, h, :], ob[:, 0:256], d)
            ousers.append(dc)
            r = rms(lambda k: mix[:, h, :], 1, 256, 128, rq, sq, dc)
            sw = sm()
            d = ts(sw, Pm("sub_w"), 1.0 - lam_init, ALU.mult, None, None)
            d_mix[h] = stt(mix[:, h, :], mix[:, h, :], sw, rq, ALU.mult, ALU.mult, r, d)
        for h in range(4):
            ob, ofree, ousers = banks.get()
            for t in range(2):
                bk, free, users = banks.get()
                mm(bk, qn[:, h, t * 128:(t + 1) * 128], kn[:, h, :], True, False, free, d_qn[h], d_kn[h])
                d = mm(bk, qr[0:64, h, t * 128:(t + 1) * 128], kr[0:64, :], False, True, d_qr[h], d_kr)
                p, r, e, u = softmax(bk, 512, 192 ** -0.5, d, users)
                d = ts(p, p, r, ALU.mult, None, None, e)
                d = values(p, 4, d, u, lambda b: mv[:, b, h * 128:(h + 1) * 128], d_mv, ob,
                           slice(t * 128, t * 128 + 128), ofree, t == 0)
            d_mix[4 + h] = copy(mix[:, 4 + h, :], ob[:, 0:256], d)
            ousers.append(d_mix[4 + h])

        modulation(2)
        d_x1 = []
        for c in range(2):
            w = W(I["w_out"][:, c * 512:(c + 1) * 512], 512)
            for j in range(4):
                f = c * 4 + j
                bk, free, users = banks.get()
                d = group(bk[:, 0:256], w, j * 128, (j + 1) * 128, lambda k: mix[:, k, :], 8, free, d_mix)
                d = stt(xv[:, f, :], bk[:, 0:256], mods[:, 16 + f, 0:1], xv[:, f, :], ALU.mult, ALU.add, d, d_mod[2])
                users.append(d)
                d_x1.append(d)
            w.free(queue["pe"][-1][2])

        modulation(3)
        modulation(4)
        fw = sm(8)
        d = ts(fw, mods[:, 32:40, 0], 1.0, ALU.add, None, None, d_mod[4])
        d_fw = tt(fw, fw, Pm("ffn_w"), ALU.mult, d)
        done = barrier()
        at[0] = 0
        sq = Rot([take(512) for _ in range(2)])
        rbrow = take(32)
        hf = take(8, 256)
        rf = take(256)
        d_rb = dma("act", rbrow[0:1, :], I["router_b"], done)
        r = rms(lambda k: xv[:, k, :], 8, 256, 1024, rf, sq, d_x1, done)
        for k in range(8):
            d = stt(hf[:, k, :], xv[:, k, :], fw[:, k:k + 1], rf, ALU.mult, ALU.mult, r, d_fw)
            d_hf = ts(hf[:, k, :], hf[:, k, :], mods[:, 24 + k, 0:1], ALU.add, None, None, d, d_mod[3])
        w = W(I["router_w"], 32, per=8)
        gT = take(256)
        for t in range(2):
            bk, free, users = banks.get()
            mm(bk[:, 0:32], ones[0:1, :], rbrow[0:1, :], True, False, free, d_rb)
            for k in range(8):
                d = mm(bk[:, 0:32], hf[:, k, t * 128:(t + 1) * 128], w.ap(k, 0, 32), False, k == 7, d_hf, w.ready(k))
            lg, rp, m8, m4 = take(40), take(40), sm(8), sm(8)
            da = copy(lg[:, 0:32], bk[:, 0:32], d)
            users.append(da)
            db = memset(lg[:, 32:40], -3.0e38, eng="dve")
            dc = memset(m4, -3.0e38, eng="dve")
            d = op("dve", lambda e, m8=m8, lg=lg: e.max(m8, lg[:, 0:32]), da)
            d = copy(m4[:, 0:4], m8[:, 0:4], d, dc)
            d = op("dve", lambda e, rp=rp, m4=m4, lg=lg: e.match_replace(rp, m4, lg, 3.0e38), d, da, db)
            d = tt(rp[:, 0:32], rp[:, 0:32], lg[:, 0:32], ALU.not_equal, d)
            nm, den = sm(), sm()
            d1 = ts(nm, m8[:, 0:1], -1.0, ALU.mult, None, None)
            d1 = act(lg[:, 0:32], lg[:, 0:32], ACT.Exp, d1, d, bias=nm)
            d = tt(lg[:, 0:32], lg[:, 0:32], rp[:, 0:32], ALU.mult, d1, d)
            d = op("dve", lambda e, den=den, lg=lg: e.tensor_reduce(den, lg[:, 0:32], AX_X, ALU.add), d)
            d = recip(den, den, d)
            d = ts(lg[:, 0:32], lg[:, 0:32], den, ALU.mult, None, None, d)
            bk, free, users = banks.get()
            d = tr(bk[0:32, 0:128], lg[:, 0:32], d, free)
            d_gT = copy(gT[0:32, t * 128:(t + 1) * 128], bk[0:32, 0:128], d)
            users.append(d_gT)
        w.free(queue["pe"][-1][2])

        tabm = take(12, 128)
        tabr = take(12)
        d = memset(tabr[32:64, :], 1.0, done, eng="pool")
        d0 = dma("act", tabr[0:32, :], I["rel_bias"], done)
        d = op("pool", lambda e: e.tensor_copy(tabm[0:33, :, :], tabr[0:33, :].unsqueeze(2).to_broadcast([33, 12, 128])), d, d0)
        d_skw = []
        tb = Rot([take(384) for _ in range(2)])
        ha = CST["hot"][0]
        for h in range(12):
            g = h // 4
            bk, free, users = banks.get()
            m = mm(bk[:, 0:384], tabm[0:33, h, :], cst[0:33, ha + g * 384:ha + (g + 1) * 384], True, True, d, free)
            t, tfree, tuse = tb.get()
            c = copy(t, bk[:, 0:384], m, tfree, eng="act")
            users.append(c)
            s = dma("act", skew[h, :, :], t, c)
            tuse.append(s)
            d_skw.append(s)

        bfree = []
        for i in range(8):
            _, f, _ = banks.get()
            bfree.append(f)
        yb = [PS[:, i * 512:(i + 1) * 512] for i in range(4)]
        hb = Rot([PS[:, i * 512:(i + 1) * 512] for i in range(4, 8)])
        for f in hb.users:
            f.extend(bfree)
        b2s = take(1024)
        d_b2 = dma("act", b2s[0:32, :], I["b2"], done)
        for j in range(8):
            d_y = mm(yb[j // 2][:, (j % 2) * 256:(j % 2) * 256 + 256], b2s[0:32, j * 128:(j + 1) * 128], gT[0:32, :],
                     j % 2 == 0, False, bfree, d_b2, d_gT)
        selr = Rot([take(128) for _ in range(2)])
        gb = Rot([take(256) for _ in range(2)])
        acts = Rot([take(8, 256) for _ in range(2)])
        tg = Rot([take(256) for _ in range(4)])
        tu = Rot([take(256) for _ in range(4)])
        tsg = Rot([take(256) for _ in range(4)])
        b1a = PAR["b1"][0]
        pend = None

        def down(pe_e, A, dA, wd_src, auses):
            w = W(wd_src, 1024, per=2)
            last = pe_e == NE - 1
            for k in range(8):
                for j in range(8):
                    d = mm(yb[j // 2][:, (j % 2) * 256:(j % 2) * 256 + 256], w.ap(k, j * 128, (j + 1) * 128), A[:, k, :],
                           False, last and k == 7, dA[k], w.ready(k))
            w.free(d)
            auses.append(d)
            return d

        for ex in range(NE):
            s, sf, su = selr.get()
            d = ts(s[0:32, :], ones[0:32, :], C("ident")[0:32, ex:ex + 1], ALU.mult, None, None, sf, d_cst)
            bk, free, users = hb.get()
            d = mm(bk[:, 0:256], s[0:32, :], gT[0:32, :], True, True, d, free)
            su.append(d)
            G, gf_, gu = gb.get()
            d_g = copy(G, bk[:, 0:256], d, gf_, eng="act")
            users.append(d_g)
            A, af, au = acts.get()
            dA = []
            for c in range(2):
                wg = W(I["w1"][ex, :, c * 512:(c + 1) * 512], 512)
                wu = W(I["w1"][ex, :, 1024 + c * 512:1024 + (c + 1) * 512], 512)
                for j in range(4):
                    f = c * 4 + j
                    bk, free, users = hb.get()
                    group(bk[:, 0:256], wg, j * 128, (j + 1) * 128, lambda k: hf[:, k, :], 8, free, d_hf)
                    d = group(bk[:, 256:512], wu, j * 128, (j + 1) * 128, lambda k: hf[:, k, :], 8)
                    g1, f1, u1 = tg.get()
                    uu, f2, u2 = tu.get()
                    sg, f3, u3 = tsg.get()
                    bg = par[:, b1a + ex * 16 + f:b1a + ex * 16 + f + 1]
                    bu = par[:, b1a + ex * 16 + 8 + f:b1a + ex * 16 + 8 + f + 1]
                    dg = ts(g1, bk[:, 0:256], bg, ALU.add, 7.0, ALU.min, d, f1)
                    du = ts(uu, bk[:, 256:512], bu, ALU.add, 7.0, ALU.min, d, f2)
                    users.append(du)
                    ds = act(sg, g1, ACT.Sigmoid, dg, f3, scale=1.702)
                    du = ts(uu, uu, -7.0, ALU.max, 1.0, ALU.add, du, eng="pool")
                    dg = tt(g1, g1, G, ALU.mult, ds, d_g, eng="pool")
                    ds = tt(sg, sg, uu, ALU.mult, ds, du)
                    d = tt(A[:, f, :], sg, g1, ALU.mult, ds, dg, af)
                    u1.append(d)
                    u2.append(ds)
                    u3.append(d)
                    gu.append(dg)
                    dA.append(d)
                wg.free(queue["pe"][-1][2])
                wu.free(queue["pe"][-1][2])
                if c == 0 and pend is not None:
                    down(*pend)
            pend = (ex, A, dA, I["w2"][ex], au)
        d_y = down(*pend)

        modulation_bank = Rot([PS[:, i * 512:(i + 1) * 512] for i in range(4, 8)])
        modulation_bank.users = hb.users
        modulation_bank.n = hb.n
        banks = modulation_bank
        modulation(5)
        d_xm = []
        for j in range(8):
            d_xm.append(stt(xv[:, j, :], yb[j // 2][:, (j % 2) * 256:(j % 2) * 256 + 256], mods[:, 40 + j, 0:1],
                            xv[:, j, :], ALU.mult, ALU.add, d_y, d_mod[5]))
        users4 = banks.users
        banks = Rot([PS[:, i * 512:(i + 1) * 512] for i in range(8)])
        banks.users = [[d_xm[-1]] for _ in range(4)] + users4

        done = barrier()
        at[0] = 0
        sq = Rot([take(512) for _ in range(2)])
        rf = take(256)
        xn = take(8, 256)

        def norm_to(dst, wname, *after):
            r = rms(lambda k: xv[:, k, :], 8, 256, 1024, rf, sq, *after)
            for k in range(8):
                d = stt(dst[:, k, :], xv[:, k, :], Pm(wname, k), rf, ALU.mult, ALU.mult, r)
            return d

        d = norm_to(xv, "fin_w", d_xm, done)
        d_xn = norm_to(xn, "attn2_w", d)

        T = take(12, 256)
        d_T = []
        for h in range(12):
            base = skew[h, :, :].rearrange("p n -> (p n)")[127:127 + 128 * 383]
            d_T.append(dma("act", T[:, h, :], base.rearrange("(p n) -> p n", n=383)[:, 0:256], d_skw, done))

        w2i = I["w_in_2"]

        def projT(c0, ntile, dst, eng="act"):
            ds = []
            j = 0
            while j < ntile:
                m = min(4, ntile - j)
                w = W(w2i[:, c0 + j * 128:c0 + (j + m) * 128], m * 128)
                for i in range(0, m, 2):
                    bk, free, users = banks.get()
                    n = min(2, m - i)
                    for q in range(n):
                        d = group(bk[:, q * 256:(q + 1) * 256], w, (i + q) * 128, (i + q + 1) * 128,
                                  lambda k: xn[:, k, :], 8, free, d_xn)
                    c = copy(dst[:, j + i:j + i + n, :], bk[:, 0:n * 256].rearrange("p (a b) -> p a b", a=n), d, eng=eng)
                    users.append(c)
                    ds += [c] * n
                w.free(d)
                j += m
            return ds

        def projV(c0, n, dst):
            ds = []
            j = 0
            while j < n:
                m = min(512, n - j)
                w = W(w2i[:, c0 + j:c0 + j + m], m)
                for t in range(2):
                    bk, free, users = banks.get()
                    for k in range(8):
                        d = mm(bk[:, 0:m], xn[:, k, t * 128:(t + 1) * 128], w.ap(k, 0, m), k == 0, k == 7,
                               free, d_xn, w.ready(k))
                    c = copy(dst[:, t, j:j + m], bk[:, 0:m], d, eng="act")
                    users.append(c)
                    ds.append(c)
                w.free(d)
                j += m
            return ds

        us = take(4, 256)
        d_us = projT(4352, 4, us)
        sbq, sbk = take(4, 256), take(4, 256)
        d_sq = projT(2816, 4, sbq)
        d_sk = projT(3328, 4, sbk)
        sbv = take(2, 512)
        d_sv = projV(3840, 512, sbv)
        dlq, dlk = take(6, 256), take(6, 256)
        d_lq = projT(512, 6, dlq)
        d_lk = projT(1280, 6, dlk)
        dlv = take(2, 768)
        d_lv = projV(2048, 768, dlv)
        pu = take(4, 256)
        d_pu = projT(0, 4, pu)

        mark = at[0]
        ysT = take(4, 256)
        mark2 = at[0]
        s5 = [take(16) for _ in range(16)]
        (dt, th, kk, rr, wc, wsn, lbr, lbi, dn, cfr, cfi, t1, t2, t3, t4, t5) = s5
        are, aim = Pm("s5_are"), Pm("s5_aim")
        d = act(dt, Pm("s5_ldt"), ACT.Exp, done)
        d = tt(th, aim, dt, ALU.mult, d)
        e1 = tt(t1, are, dt, ALU.mult, d)
        d_r = act(rr, t1, ACT.Exp, e1)
        two_pi = 6.283185307179586
        d = ts(kk, th, 1.0 / two_pi, ALU.mult, 12582912.0, ALU.add, d)
        d = ts(kk, kk, -12582912.0, ALU.add, None, None, d)
        for part in (6.28125, 0.0019350051879882812, 3.0199159819567e-07):
            d = stt(th, kk, -part, th, ALU.mult, ALU.add, d)
        d = ts(th, th, 3.1415925, ALU.min, -3.1415925, ALU.max, d)
        d_s = act(wsn, th, ACT.Sin, d)
        d = act(t2, th, ACT.Abs, d)
        d = ts(t2, t2, -1.0, ALU.mult, 1.5707963267948966, ALU.add, d)
        d_c = act(wc, t2, ACT.Sin, d)
        d = tt(lbr, rr, wc, ALU.mult, d_c, d_r)
        da = ts(lbr, lbr, -1.0, ALU.add, None, None, d)
        db = tt(lbi, rr, wsn, ALU.mult, d_s, d_r)
        d = tt(dn, are, are, ALU.mult)
        d1 = tt(t3, aim, aim, ALU.mult)
        d = tt(dn, dn, t3, ALU.add, d, d1)
        d = recip(dn, dn, d)
        d1 = tt(t4, lbr, are, ALU.mult, da)
        d2 = tt(t5, lbi, aim, ALU.mult, db)
        d3 = tt(t4, t4, t5, ALU.add, d1, d2)
        dr_ = tt(cfr, t4, dn, ALU.mult, d3, d)
        d1 = tt(t4, lbi, are, ALU.mult, dr_)
        d2 = tt(t5, lbr, aim, ALU.mult, d3)
        d3 = tt(t4, t4, t5, ALU.subtract, d1, d2)
        di_ = tt(cfi, t4, dn, ALU.mult, d3)
        bt = take(2, 512)
        ct = take(2, 512)
        cc = take(2, 512)
        d_bt = dma("act", bt[:, 0, :], I["s5_bre"], done)
        d_bt = [d_bt, dma("act", bt[:, 1, :], I["s5_bim"], done)]
        d_ct = [dma("act", ct[:, 0, :], I["s5_cre"], done), dma("act", ct[:, 1, :], I["s5_cim"], done)]

        def b32(x):
            return x.unsqueeze(2).to_broadcast([128, 16, 32])

        def v32(x):
            return x.rearrange("p (a b) -> p a b", b=32)

        ctmp = take(512)
        d1 = tt(v32(cc[:, 0, :]), v32(ct[:, 0, :]), b32(cfr), ALU.mult, d_ct, dr_)
        d2 = tt(v32(ctmp), v32(ct[:, 1, :]), b32(cfi), ALU.mult, d_ct, di_)
        d_cc = tt(cc[:, 0, :], cc[:, 0, :], ctmp, ALU.subtract, d1, d2)
        d1 = tt(v32(cc[:, 1, :]), v32(ct[:, 0, :]), b32(cfi), ALU.mult)
        d2 = tt(v32(ctmp), v32(ct[:, 1, :]), b32(cfr), ALU.mult, d_cc)
        d1 = tt(cc[:, 1, :], cc[:, 1, :], ctmp, ALU.add, d1, d2)
        d_cc = ts(cc[:, 1, :], cc[:, 1, :], -1.0, ALU.mult, None, None, d1)
        pc = [wc] + [take(16) for _ in range(7)]
        psn = [wsn] + [take(16) for _ in range(7)]
        d = [d_c, d_s]
        for k in range(7):
            a = tt(pc[k + 1], pc[k], pc[k], ALU.mult, d)
            b = tt(t1, psn[k], psn[k], ALU.mult, d, e1, d_r)
            a = tt(pc[k + 1], pc[k + 1], t1, ALU.subtract, a, b)
            b = tt(psn[k + 1], pc[k], psn[k], ALU.mult, d)
            b = ts(psn[k + 1], psn[k + 1], 2.0, ALU.mult, None, None, b)
            e1 = a
            d = [a, b]
        d_pw = d
        Ct, St = take(4, 256), take(4, 256)
        xr, xi, tm = take(4, 256), take(4, 256), take(4, 256)
        tp = tm
        d_tab_free = None
        d_prev = None
        for q in range(4):
            a = memset(Ct[:, :, 0:1], 1.0, d_tab_free, done)
            b = memset(St[:, :, 0:1], 0.0, d_tab_free)
            d = [a, b]
            for k in range(8):
                n = 1 << k

                def bc(x):
                    return x[:, q * 4:q * 4 + 4].unsqueeze(2).to_broadcast([128, 4, n])
                o = slice(n, 2 * n)
                p = slice(0, n)
                x1 = tt(Ct[:, :, o], Ct[:, :, p], bc(pc[k]), ALU.mult, d, d_pw, eng="pool")
                x2 = tt(tp[:, :, p], St[:, :, p], bc(psn[k]), ALU.mult, d, d_prev, eng="pool")
                x3 = tt(Ct[:, :, o], Ct[:, :, o], tp[:, :, p], ALU.subtract, x1, x2, eng="pool")
                x1 = tt(St[:, :, o], St[:, :, p], bc(pc[k]), ALU.mult, d, eng="pool")
                x2 = tt(tp[:, :, p], Ct[:, :, p], bc(psn[k]), ALU.mult, d, x3, eng="pool")
                x4 = tt(St[:, :, o], St[:, :, o], tp[:, :, p], ALU.add, x1, x2, eng="pool")
                d = [x3, x4]
            d_tab = d
            b4 = []
            for i in range(4):
                bk, free, users = banks.get()
                for v in range(2):
                    m = mm(bk[:, v * 256:(v + 1) * 256], bt[32 * i:32 * i + 32, v, q * 128:(q + 1) * 128],
                           us[32 * i:32 * i + 32, q, :], True, True, free, d_bt, d_us)
                xs = slice(i, i + 1)
                Pr, Pi = bk[:, 0:256].unsqueeze(1), bk[:, 256:512].unsqueeze(1)
                y1 = tt(xr[:, xs, :], Pr, Ct[:, xs, :], ALU.mult, m, d_tab, d_prev)
                y2 = tt(tm[:, xs, :], Pi, St[:, xs, :], ALU.mult, m)
                y1 = tt(xr[:, xs, :], xr[:, xs, :], tm[:, xs, :], ALU.add, y1, y2)
                y3 = tt(xi[:, xs, :], Pi, Ct[:, xs, :], ALU.mult)
                y2 = tt(tm[:, xs, :], Pr, St[:, xs, :], ALU.mult, y1)
                users.append(y2)
                y3 = tt(xi[:, xs, :], xi[:, xs, :], tm[:, xs, :], ALU.subtract, y3, y2)

                def scan(x, *after, rbc=rr[:, q * 4 + i:q * 4 + i + 1].to_broadcast([128, 256])):
                    return op("dve", lambda e: e.tensor_tensor_scan(x, rbc, x, 0.0, ALU.mult, ALU.add), *after)
                z1 = scan(xr[:, i, :], y1, d_r)
                z2 = scan(xi[:, i, :], y3)
                b4 += [z1, z2]
            hr = take(4, 256) if q == 0 else hr
            a1 = tt(hr, xr, Ct, ALU.mult, b4, d_prev)
            a2 = tt(tm, xi, St, ALU.mult, b4)
            a1 = tt(hr, hr, tm, ALU.subtract, a1, a2)
            a3 = tt(xr, xr, St, ALU.mult, a1)
            a2 = tt(tm, xi, Ct, ALU.mult, a1)
            a3 = tt(xr, xr, tm, ALU.add, a3, a2)
            d_tab_free = a2
            bk, free, users = banks.get()
            for i in range(4):
                o = bk[32 * i:32 * i + 32, 0:256]
                cs = slice((q * 4 + i) * 32, (q * 4 + i) * 32 + 32)
                mm(o, cc[:, 0, cs], hr[:, i, :], True, False, a1, d_cc, free)
                m = mm(o, cc[:, 1, cs], xr[:, i, :], False, True, a3)
            d_prev = [m, a3]
            d_ys = stt(ysT[:, q, :], us[:, q, :], Pm("s5_d", q), bk[:, 0:256], ALU.mult, ALU.add, m)
            users.append(d_ys)
        g1 = hr
        d = act(g1, ysT, ACT.Square, d_ys)
        d = ts(g1, g1, 0.044715, ALU.mult, 1.0, ALU.add, d)
        d = tt(g1, g1, ysT, ALU.mult, d)
        d = act(g1, g1, ACT.Sigmoid, d, scale=2.0 * 0.7978845608028654)
        d_gl = tt(g1, g1, ysT, ALU.mult, d)
        sgl = Rot([tm[:, 0, :], tm[:, 1, :]])
        for c in range(2):
            wg = W(I["s5_w_glu"][:, c * 256:(c + 1) * 256], 256)
            wu = W(I["s5_w_glu"][:, 512 + c * 256:512 + (c + 1) * 256], 256)
            for j in range(2):
                bk, free, users = banks.get()
                group(bk[:, 0:256], wg, j * 128, (j + 1) * 128, lambda k: g1[:, k, :], 4, free, d_gl)
                d = group(bk[:, 256:512], wu, j * 128, (j + 1) * 128, lambda k: g1[:, k, :], 4)
                s, sf, su = sgl.get()
                da = act(s, bk[:, 256:512], ACT.Sigmoid, d, sf)
                d_s5 = tt(ysT[:, c * 2 + j, :], bk[:, 0:256], s, ALU.mult, da)
                users.append(d_s5)
                su.append(d_s5)
            wg.free(d)
            wu.free(d)

        done5 = barrier()
        at[0] = mark2
        mg = arena[:, mark2:mark2 + 2048].rearrange("p (k t) -> p k t", k=8)
        Pb = Rot([take(768) for _ in range(2)])
        PT = Rot([take(768) for _ in range(2)])
        ysb = take(4, 256)
        zr = Rot([take(384) for _ in range(2)])
        er = Rot([take(384) for _ in range(2)])
        sr = Rot([take(384) for _ in range(2)])
        d_sb = []
        for h in range(4):
            hc = slice(h * 128, h * 128 + 128)
            bk, free, users = banks.get()
            mm(bk[:, 0:256], sbk[:, h, 0:128], sbq[:, h, :], True, True, free, d_sq[h], d_sk[h])
            m = mm(bk[:, 256:384], sbk[:, h, 128:256], sbq[:, h, 128:256], True, True)
            z, zf, zu = zr.get()
            e_, ef, eu = er.get()
            s, sf, su = sr.get()
            dz = act(z, bk[:, 0:384], ACT.Copy, m, zf, done5, scale=128 ** -0.5)
            users.append(dz)
            d = act(e_, z, ACT.Abs, dz, ef, done5)
            d = act(e_, e_, ACT.Exp, d, scale=-1.0)
            d = act(e_, e_, ACT.Ln, d, bias=1.0)
            d = stt(s, z, 0.0, e_, ALU.max, ALU.add, d, dz, sf, done5)
            eu.append(d)
            d = tt(s, s, C("m01"), ALU.mult, d)
            bk, free, users = banks.get()
            mm(bk[:, 0:256], C("tri"), s[:, 0:256], True, False, d, free)
            mm(bk[:, 128:256], ones, s[:, 256:384], False, True)
            m = mm(bk[:, 256:384], C("tri"), s[:, 256:384], True, True)
            d = tt(z, z, bk[:, 0:384], ALU.subtract, m)
            users.append(d)
            d = tt(z, z, C("mneg"), ALU.add, d)
            d = act(s, z, ACT.Exp, d)
            zu.append(d)
            bk, free, users = banks.get()
            mm(bk[:, 0:256], sbv[:, 0, hc], s[:, 0:256], True, False, d, free, d_sv)
            m = mm(bk[:, 128:256], sbv[:, 1, hc], s[:, 256:384], False, True)
            su.append(m)
            d = copy(ysb[:, h, :], bk[:, 0:256], m)
            users.append(d)
            d_sb.append(d)

        ydl = take(2, 256)
        Tv = T
        d_dl = []
        for hs in range(4):
            rows = slice((hs % 2) * 64, (hs % 2) * 64 + 64)
            for t in range(2):
                nk = 128 * (t + 1)
                x, xf, xu = Pb.get()
                dd = []
                for g in range(3):
                    h = g * 4 + hs
                    bk, free, users = banks.get()
                    m = mm(bk[:, 0:nk], dlq[rows, h // 2, t * 128:(t + 1) * 128], dlk[rows, h // 2, 0:nk], True, True,
                           free, d_lq[h // 2], d_lk[h // 2])
                    d = stt(x[:, g * nk:(g + 1) * nk], bk[:, 0:nk], 0.125, Tv[:, h, 256 - nk:256], ALU.mult, ALU.add,
                            m, d_T[h], xf)
                    users.append(d)
                    dd.append(d)
                mx, den = sm(), sm()
                xx = x[:, 0:3 * nk]
                d = op("dve", lambda e, mx=mx, xx=xx: e.tensor_reduce(mx, xx, AX_X, ALU.max), dd)
                d = ts(mx, mx, -1.0, ALU.mult, None, None, d)
                d = act(xx, xx, ACT.Exp, d, bias=mx, acc=den)
                d = recip(den, den, d)
                d = ts(xx, xx, den, ALU.mult, None, None, d)
                nb = 3 * (t + 1)
                pt, pf, pu_ = PT.get()
                for a in range(0, nb, 3):
                    bk, free, users = banks.get()
                    for b in range(3):
                        m = tr(bk[:, b * 128:(b + 1) * 128], x[:, (a + b) * 128:(a + b + 1) * 128], d, free)
                    c = copy(pt[:, a * 128:(a + 3) * 128], bk[:, 0:384], m, pf, eng="act")
                    users.append(c)
                xu.append(m)
                ob, ofree, ousers = banks.get()
                for b in range(nb):
                    g, kb = b // (t + 1), b % (t + 1)
                    h = g * 4 + hs
                    m = mm(ob[rows, 0:128], dlv[:, kb, h * 64:(h + 1) * 64], pt[:, b * 128:(b + 1) * 128],
                           b == 0, b == nb - 1, c, d_lv, ofree)
                pu_.append(m)
                d = copy(ydl[rows, hs // 2, t * 128:(t + 1) * 128], ob[rows, 0:128], m)
                ousers.append(d)
                d_dl.append(d)

        ypl = take(4, 256)
        pa, pb = take(4, 256), take(4, 256)
        src = pu
        d = [d_pu, done5]
        lv = []
        for i in range(4):
            n = 1 << i
            dst = pa if i % 2 == 0 else pb
            x1 = tt(dst[:, i:4, n:256], src[:, i:4, n:256], src[:, i:4, 0:256 - n], ALU.add, d, eng="pool")
            x2 = copy(dst[:, i:4, 0:n], src[:, i:4, 0:n], d, eng="pool")
            lv.append((dst, [x1, x2]))
            d = [x1, x2]
            inv = C("inv").rearrange("p (a b) -> p a b", a=4)
            y = tt(ypl[:, i, :], dst[:, i, :], inv[:, i, :], ALU.mult, d, eng="pool")
            y = tt(ypl[:, i, :], ypl[:, i, :], pu[:, i, :], ALU.subtract, y, eng="pool")
            d = [x1, x2, y]
            src = dst
        w = W(I["pool_w"], 128)
        d_pl = []
        for i in range(4):
            bk, free, users = banks.get()
            m = mm(bk[:, 0:256], w.ap(i, 0, 128), ypl[:, i, :], True, True, free, y, w.ready(i))
            d = ts(ypl[:, i, :], bk[:, 0:256], Pm("pscale", i), ALU.mult, None, None, m)
            users.append(d)
            d_pl.append(d)
        w.free(m)

        gs = Rot([take(256) for _ in range(3)])
        row = 0
        d_mg = [None] * 8
        for bi, (yt, K, dy) in enumerate(((ypl, 4, d_pl), (ydl, 2, d_dl), (ysb, 4, d_sb), (ysT, 4, d_s5))):
            for c in range(2):
                wg = W(I["w_gate"][bi, :, c * 512:(c + 1) * 512], 512)
                wb = W(I["w_branch"][row:row + K * 128, c * 512:(c + 1) * 512], 512)
                for j in range(4):
                    f = c * 4 + j
                    bk, free, users = banks.get()
                    group(bk[:, 0:256], wg, j * 128, (j + 1) * 128, lambda k: xn[:, k, :], 8, free)
                    m = group(bk[:, 256:512], wb, j * 128, (j + 1) * 128, lambda k: yt[:, k, :], K, dy)
                    s, sf, su = gs.get()
                    d = act(s, bk[:, 0:256], ACT.Sigmoid, m, sf)
                    if bi == 0:
                        d = tt(mg[:, f, :], bk[:, 256:512], s, ALU.mult, d)
                        users.append(d)
                    else:
                        d = tt(s, bk[:, 256:512], s, ALU.mult, d)
                        users.append(d)
                        d = tt(mg[:, f, :], mg[:, f, :], s, ALU.add, d, d_mg[f])
                    su.append(d)
                    d_mg[f] = d
                wg.free(m)
                wb.free(m)
            row += K * 128
        d_x2 = []
        for c in range(2):
            w = W(I["w_out_2"][:, c * 512:(c + 1) * 512], 512)
            for j in range(4):
                f = c * 4 + j
                bk, free, users = banks.get()
                m = group(bk[:, 0:256], w, j * 128, (j + 1) * 128, lambda k: mg[:, k, :], 8, free, d_mg)
                d = tt(xv[:, f, :], bk[:, 0:256], xv[:, f, :], ALU.add, m)
                users.append(d)
                d_x2.append(d)
            w.free(m)

        done = barrier()
        at[0] = 0
        sq = Rot([take(512) for _ in range(2)])
        rf = take(256)
        hn = take(8, 256)
        d_hn = norm_to(hn, "ffn2_w", d_x2, done)
        hh = take(22, 256)
        gs = Rot([take(256) for _ in range(3)])
        d_hh = []
        for c in range(6):
            n = 512 if c < 5 else 256
            wg = W(I["w_up"][:, c * 512:c * 512 + n], n)
            wu = W(I["w_up"][:, 2816 + c * 512:2816 + c * 512 + n], n)
            for j in range(n // 128):
                bk, free, users = banks.get()
                group(bk[:, 0:256], wg, j * 128, (j + 1) * 128, lambda k: hn[:, k, :], 8, free, d_hn)
                m = group(bk[:, 256:512], wu, j * 128, (j + 1) * 128, lambda k: hn[:, k, :], 8)
                s, sf, su = gs.get()
                d = act(s, bk[:, 0:256], ACT.Sigmoid, m, sf)
                d = tt(s, bk[:, 0:256], s, ALU.mult, d)
                d = tt(hh[:, c * 4 + j, :], bk[:, 256:512], s, ALU.mult, d)
                users.append(d)
                su.append(d)
                d_hh.append(d)
            wg.free(m)
            wu.free(m)
        acc = []
        for i in range(4):
            acc.append(banks.get())
        for c in range(11):
            w = W(I["w_down"][c * 256:(c + 1) * 256, :], 1024, per=2)
            for kk_ in range(2):
                k = c * 2 + kk_
                for j in range(8):
                    bk, free, users = acc[j // 2]
                    m = mm(bk[:, (j % 2) * 256:(j % 2) * 256 + 256], w.ap(kk_, j * 128, (j + 1) * 128), hh[:, k, :],
                           k == 0 and j % 2 == 0, k == 21, free, d_hh[k], w.ready(kk_))
            w.free(m)
        for i in range(4):
            bk, free, users = acc[i]
            d = tt(xv[:, 2 * i:2 * i + 2, :], bk.rearrange("p (a b) -> p a b", a=2), xv[:, 2 * i:2 * i + 2, :], ALU.add, m)
            users.append(d)
        d = norm_to(xv, "fin2_w", d)
        d_out = dma("sp", out.rearrange("(k p) t -> p k t", p=128), xv, d)
        last = [d_out] + d_skw
        queue["sp"].append((None, last, Done("sp")))

        for e in esem:
            n = 0
            for _, _, d in queue[e]:
                if d.sem is None and d.asked:
                    n += 1
                    d.sem, d.val = esem[e], n

        block = ctx.enter_context(nc.Block())

        def play(name):
            def body(eng):
                seen = {}
                for fn, waits, d in queue[name]:
                    need = {}
                    for w in waits:
                        k = id(w.sem)
                        if seen.get(k, 0) < w.val and (k not in need or need[k].val < w.val):
                            need[k] = w
                    for k, w in need.items():
                        eng.wait_ge(w.sem, w.val)
                        seen[k] = w.val
                    if fn is None:
                        continue
                    ins = fn(eng)
                    if d.sem is not None:
                        ins.then_inc(d.sem, 1 if d.sem is esem.get(name) else 16)
            return body

        block.sync(play("sp"))
        block.tensor(play("pe"))
        block.vector(play("dve"))
        block.scalar(play("act"))
        block.gpsimd(play("pool"))


_RAW = {"w_ada": (1024, 6144), "w_in": (1024, 1984), "w_uq": (256, 768), "w_ukv": (128, 1024), "w_out": (1024, 1024),
        "router_w": (1024, 32), "router_b": (1, 32), "w1": (32, 1024, 2048), "w2": (32, 1024, 1024), "b2": (32, 1024),
        "rel_bias_2": (32, 12), "w_in_2": (1024, 4864), "pool_w_2": (512, 128), "s5_w_glu_2": (512, 1024),
        "w_branch_2": (1792, 1024), "w_gate_2": (4, 1024, 1024), "w_out_2": (1024, 1024), "w_up_2": (1024, 5632),
        "w_down_2": (2816, 1024)}
_NAMES = {"rel_bias_2": "rel_bias", "pool_w_2": "pool_w", "s5_w_glu_2": "s5_w_glu", "w_branch_2": "w_branch",
          "w_gate_2": "w_gate", "w_up_2": "w_up", "w_down_2": "w_down"}


def constants():
    import numpy as np
    f = np.float32
    c = np.zeros((128, CST_N), f)

    def put(name, a):
        lo, hi = CST[name]
        c[:a.shape[0], lo:hi] = a
    i = np.arange(128)
    put("ident", np.eye(128, dtype=f))
    put("ones", np.ones((128, 128), f))
    rot = np.zeros((128, 128), f)
    for m in range(128):
        if (m // 16) % 2 == 0:
            rot[m + 16, m] = -1.0
        else:
            rot[m - 16, m] = 1.0
    put("rot", rot)
    put("tri", (i[:, None] >= i[None, :]).astype(f))
    t = np.arange(256)
    inv = f(10000.0) ** (-np.arange(16, dtype=f) / f(16))
    d = np.arange(128) % 64
    pos = np.where((d // 32 == 0)[:, None], (t // 64)[None, :], (t % 64)[None, :]).astype(f)
    ang = pos * inv[d % 16][:, None]
    put("cos", np.cos(ang).astype(f))
    put("sin", np.sin(ang).astype(f))
    q = np.concatenate([np.arange(256), np.arange(128, 256)])
    k = np.concatenate([np.zeros(256, int), np.full(128, 128)])[None, :] + i[:, None]
    valid = k < q[None, :]
    put("m01", valid.astype(f))
    put("mneg", np.where(valid, f(0), f(-BIG)))
    put("inv", np.broadcast_to(np.concatenate([1.0 / np.minimum(t + 1, w) for w in (2, 4, 8, 16)]).astype(f), (128, 1024)))
    dist = 255 - np.arange(384)
    df = np.maximum(dist, 1).astype(f)
    large = 16 + (np.log(df / f(16)) / f(np.log(2048 / 16)) * f(16)).astype(np.int32)
    bucket = np.where(dist < 16, dist, np.minimum(large, 31))
    hot = np.zeros((33, 3, 384), f)
    for g, (win, dil) in enumerate(((128, 1), (512, 4), (2048, 16))):
        ok = (dist >= 0) & (dist % dil == 0) & (dist <= win)
        for n in range(384):
            if ok[n]:
                hot[bucket[n], g, n] = 1.0
            else:
                hot[32, g, n] = -BIG
    put("hot", hot.reshape(33, 1152))
    put("eps", np.full((128, 1), EPS, f))
    return c


def kernel(**inputs):
    import numpy as _np
    import concourse.bacc as _bacc
    from concourse.bass_utils import run_bass_kernel_spmd as _run

    x = {k: _np.asarray(v) for k, v in inputs.items()}

    def col(a):
        return a.reshape(-1, 128).T

    p = _np.zeros((128, PAR_N), _np.float32)

    def put(name, a):
        lo, hi = PAR[name]
        p[:a.shape[0], lo:hi] = a

    put("c2", _np.stack([col(x["c"]), col(x["c_ctx"])], axis=2).reshape(128, 16))
    for name, src in (("b_ada", "b_ada"), ("attn_w", "attn_norm_w"), ("qn_w", "q_norm_w"), ("kvn_w", "kv_norm_w"),
                      ("sub_w", "subln_w"), ("ffn_w", "ffn_norm_w"), ("fin_w", "final_norm_w"),
                      ("attn2_w", "attn_norm_g_2"), ("ffn2_w", "ffn_norm_g_2"), ("fin2_w", "final_norm_g_2"),
                      ("b1", "b1"), ("pscale", "pool_scale_2"), ("s5_are", "s5_a_re_2"), ("s5_aim", "s5_a_im_2"),
                      ("s5_d", "s5_d_2")):
        put(name, col(x[src]))
    put("lam", _np.stack([x[n].reshape(64) for n in ("lambda_q1", "lambda_q2", "lambda_k1", "lambda_k2")], axis=1))
    put("s5_ldt", _np.repeat(x["s5_log_dt_2"].reshape(16, 2, 1), 64, axis=2).reshape(16, 128).T)
    arrays = {"par": p, "cst": constants(),
              "xT": _np.ascontiguousarray(x["x"].reshape(256, 1024).T),
              "ctxT": _np.ascontiguousarray(x["ctx"].reshape(256, 1024).T)}
    for v in ("re", "im"):
        b = x[f"s5_b_{v}_2"].reshape(4, 4, 2, 64, 16)
        bt = _np.zeros((4, 2, 16, 4, 2, 64), _np.float32)
        c = x[f"s5_c_{v}_2"].reshape(16, 2, 16, 64)
        ct = _np.zeros((2, 64, 16, 2, 16), _np.float32)
        for g in range(2):
            bt[:, g, :, :, g, :] = b[:, :, g].transpose(1, 3, 0, 2)
            ct[g, :, :, g, :] = c[:, g].transpose(2, 0, 1)
        arrays["s5_b" + v] = bt.reshape(128, 512)
        arrays["s5_c" + v] = ct.reshape(128, 512)
    for name, shape in _RAW.items():
        arrays[_NAMES.get(name, name)] = _np.ascontiguousarray(x[name]).reshape(shape)

    nc = _bacc.Bacc("TRN2", target_bir_lowering=False, num_devices=1)
    aps = {n: nc.dram_tensor("in_" + n, a.shape, F32, kind="ExternalInput").ap() for n, a in arrays.items()}
    out = nc.dram_tensor("out_0", (1024, 256), F32, kind="ExternalOutput").ap()
    build(nc, aps, out)
    r = _run(nc, [{"in_" + n: a for n, a in arrays.items()}], core_ids=[0])
    return _np.ascontiguousarray(r.results[0]["out_0"].T).reshape(1, 256, 1024)
```

```python
from contextlib import ExitStack

import concourse.bass as bass
from concourse import mybir

ALU = mybir.AluOpType
ACT = mybir.ActivationFunctionType
F32 = mybir.dt.float32
AX_X = mybir.AxisListType.X
EPS = 1e-6
NS = 8
SLOT = 2048
NE = 32
S = 96
BIG = 1.0e30

PAR = {}
CST = {}


def _table(into, rows):
    at = 0
    for name, n in rows:
        into[name] = (at, at + n)
        at += n
    return at


PAR_N = _table(PAR, [("c2", 16), ("b_ada", 48), ("attn_w", 8), ("qn_w", 2), ("kvn_w", 1), ("sub_w", 1),
                     ("ffn_w", 8), ("fin_w", 8), ("attn2_w", 8), ("ffn2_w", 8), ("fin2_w", 8), ("lam", 4),
                     ("b1", 512), ("pscale", 4), ("s5_are", 16), ("s5_aim", 16), ("s5_ldt", 16), ("s5_d", 4)])
CST_N = _table(CST, [("ident", 128), ("ones", 128), ("rot", 128), ("tri", 128), ("before", 128), ("iota", 3 * S), ("cos", 256), ("sin", 256),
                     ("m01", 384), ("mneg", 384), ("inv", 1024), ("hot", 1152), ("eps", 1)])


class Done:

    def __init__(self, eng, sem=None, val=None):
        self.dma = sem is not None
        self.eng, self.sem, self.val, self.asked = eng, sem, val, sem is not None


class Rot:

    def __init__(self, aps):
        self.aps, self.users, self.n = aps, [[] for _ in aps], -1

    def get(self):
        self.n += 1
        i = self.n % len(self.aps)
        users, self.users[i] = self.users[i], []
        return self.aps[i], users, self.users[i]


def build(nc, I, out):
    ctx = ExitStack()
    with ctx:
        def sb(name, n):
            return ctx.enter_context(nc.sbuf_tensor(name, [128, n], F32))

        ring = sb("ring", NS * SLOT)
        par = sb("par", PAR_N)
        cst = sb("cst", CST_N)
        xT = sb("xT", 2048)
        small = sb("small", 400)
        most = ctx.enter_context(nc.sbuf_tensor("most", [128, 2], mybir.dt.int32))
        AR = 28600
        arena = sb("arena", AR)
        PS = ctx.enter_context(nc.psum_tensor("PS", [128, 4096], F32))
        skew = nc.dram_tensor("skew_scratch", [12, 128, 384], F32, kind="Internal").ap()

        esem = [{e: ctx.enter_context(nc.semaphore(f"n{w}_{e}")) for e in ("pe", "act", "dve", "pool")}
                for w in range(2)]
        slot_sem = [[ctx.enter_context(nc.semaphore(f"slot{w}_{i}")) for i in range(NS)] for w in range(2)]
        epoch, slot_base = [0], [0]
        queue = {e: [] for e in ("pe", "act", "dve", "pool", "sp")}

        def flat(after):
            for a in after:
                if a is None:
                    continue
                if isinstance(a, Done):
                    yield a
                else:
                    yield from flat(a)

        def op(eng, fn, *after):
            waits = list(flat(after))
            for w in waits:
                w.asked = True
            d = Done(eng)
            d.epoch = epoch[0]
            queue[eng].append((fn, waits, d))
            return d

        nsem = [0]

        def dma(eng, dst, src, *after, sem=None, val=16):
            waits = list(flat(after))
            for w in waits:
                w.asked = True
            if sem is None:
                sem = ctx.enter_context(nc.semaphore(f"dma{nsem[0]}"))
                nsem[0] += 1
            d = Done(eng, sem, val)
            queue[eng].append((lambda e: e.dma_start(dst, src), waits, d))
            return d

        def mm(o, l, r, start, stop, *after):
            return op("pe", lambda e: e.matmul(o, l, r, start=start, stop=stop, skip_group_check=True), *after)

        def tr(o, i, *after):
            n = i.shape[0]
            return op("pe", lambda e: e.transpose(o, i, C("ident")[0:n, 0:n]), *after)

        def act(o, i, f, *after, scale=1.0, bias=0.0, acc=None):
            if acc is None:
                return op("act", lambda e: e.activation(o, i, f, bias=bias, scale=scale), *after)
            return op("act", lambda e: e.activation(o, i, f, bias=bias, scale=scale, accum_out=acc), *after)

        def tt(o, a, b, f, *after, eng="dve"):
            return op(eng, lambda e: e.tensor_tensor(o, a, b, f), *after)

        def ts(o, a, s1, f1, s2, f2, *after, eng="dve"):
            if f2 is None:
                return op(eng, lambda e: e.tensor_scalar(o, a, s1, None, f1), *after)
            return op(eng, lambda e: e.tensor_scalar(o, a, s1, s2, f1, f2), *after)

        def stt(o, a, s, b, f1, f2, *after):
            return op("dve", lambda e: e.scalar_tensor_tensor(out=o, in0=a, scalar=s, in1=b, op0=f1, op1=f2), *after)

        def recip(o, a, *after):
            return op("dve", lambda e: e.reciprocal(o, a), *after)

        def copy(o, a, *after, eng="dve"):
            if eng == "act":
                return act(o, a, ACT.Copy, *after)
            return op(eng, lambda e: e.tensor_copy(o, a), *after)

        def memset(o, v, *after, eng="pool"):
            return op(eng, lambda e: e.memset(o, v), *after)

        def C(name):
            a, b = CST[name]
            return cst[:, a:b]

        def Pm(name, i=None):
            a, b = PAR[name]
            return par[:, a:b] if i is None else par[:, a + i:a + i + 1]

        at = [0, 0]

        def take(*dims):
            n = 1
            for d in dims:
                n *= d
            a = at[0]
            at[0] += n
            assert at[0] <= AR, at[0]
            v = arena[:, a:a + n]
            if len(dims) == 2:
                v = v.rearrange("p (a b) -> p a b", a=dims[0])
            if len(dims) == 3:
                v = v.rearrange("p (a b c) -> p a b c", a=dims[0], b=dims[1])
            return v

        def sm(n=1):
            a = at[1]
            at[1] += n
            assert at[1] <= 400
            return small[:, a:a + n]

        def barrier():
            return [[q for q in queue[e] if callable(q[0])][-1][2] for e in ("pe", "act", "dve", "pool") if queue[e]]

        banks = Rot([PS[:, i * 512:(i + 1) * 512] for i in range(8)])

        loads = [0]
        release = [None] * NS

        class W:

            def __init__(self, src, n, per=4):
                k = src.shape[0] // 128
                self.per, self.slots = per, []
                for a in range(0, k, per):
                    m = min(per, k - a)
                    i = loads[0]
                    loads[0] += 1
                    s = i % NS
                    v = ring[:, s * SLOT:s * SLOT + m * n].rearrange("p (k n) -> p k n", k=m)
                    d = dma("sp", v, src[a * 128:(a + m) * 128, :].rearrange("(k p) n -> p k n", p=128),
                            release[s], sem=slot_sem[epoch[0]][s], val=16 * ((i - slot_base[0]) // NS + 1))
                    release[s] = None
                    self.slots.append((v, d, s))

            def ap(self, k, a, b):
                return self.slots[k // self.per][0][:, k % self.per, a:b]

            def ready(self, k):
                return self.slots[k // self.per][1]

            def free(self, d):
                for _, _, s in self.slots:
                    release[s] = d

        def group(o, w, a, b, rhs, K, *after):
            for k in range(K):
                d = mm(o, w.ap(k, a, b), rhs(k), k == 0, k == K - 1, after if k == 0 else None, w.ready(k))
            return d

        ctxT = take(8, 256)
        xv = xT[:, :].rearrange("p (k t) -> p k t", k=8)
        d_par = dma("act", par[:, :], I["par"])
        d_cst = dma("act", cst[:, :], I["cst"])
        d_ctx = dma("act", ctxT, I["ctxT"].rearrange("(k p) t -> p k t", p=128))
        d_x = dma("act", xv, I["xT"].rearrange("(k p) t -> p k t", p=128))
        eps = cst[:, CST["eps"][0]:CST["eps"][1]]
        ones = C("ones")

        def rms(src, K, n, D, rb, sq, *after):
            bk, free, users = banks.get()
            for k in range(K):
                s, sfree, suse = sq.get()
                q = act(s[:, 0:n], src(k), ACT.Square, after, sfree)
                d = mm(bk[:, 0:n], ones, s[:, 0:n], k == 0, k == K - 1, q, free if k == 0 else None, d_cst)
                suse.append(d)
            r = act(rb, bk[:, 0:n], ACT.Sqrt, d, scale=1.0 / D, bias=eps)
            users.append(r)
            return recip(rb, rb, r)

        e2 = sm(16)
        sc2 = sm(16)
        c2 = Pm("c2")
        d = act(e2, c2, ACT.Exp, d_par, scale=-1.0)
        d = ts(e2, e2, 1.0, ALU.add, None, None, d)
        d = recip(e2, e2, d)
        d_silu = tt(sc2, c2, e2, ALU.mult, d)
        c2v = sc2.rearrange("p (k v) -> p k v", v=2)
        mods = sm(96).rearrange("p (j v) -> p j v", v=2)
        d_mod = {}

        def modulation(m):
            bk, free, users = banks.get()
            for c in range(2):
                w = W(I["w_ada"][:, m * 1024 + c * 512:m * 1024 + (c + 1) * 512], 512)
                for j in range(4):
                    d = group(bk[:, (c * 4 + j) * 2:(c * 4 + j) * 2 + 2], w, j * 128, (j + 1) * 128,
                              lambda k: c2v[:, k, :], 8, d_silu, free)
                w.free(d)
            a, b = PAR["b_ada"]
            bias = par[:, a + m * 8:a + m * 8 + 8].unsqueeze(2).to_broadcast([128, 8, 2])
            d = tt(mods[:, m * 8:m * 8 + 8, :], bk[:, 0:16].rearrange("p (j v) -> p j v", v=2), bias, ALU.add, d)
            users.append(d)
            d_mod[m] = d

        modulation(0)
        modulation(1)
        aw = sm(16).rearrange("p (j v) -> p j v", v=2)
        d = ts(aw, mods[:, 8:16, :], 1.0, ALU.add, None, None, d_mod[1])
        d_aw = tt(aw, aw, Pm("attn_w").unsqueeze(2).to_broadcast([128, 8, 2]), ALU.mult, d)

        hT = take(8, 512)
        sq = Rot([take(512) for _ in range(2)])
        rbs = take(2, 256)
        d_h = []
        for v, src, dd in ((1, ctxT, d_ctx), (0, xv, d_x)):
            t0 = 0 if v else 256
            r = rms(lambda k: src[:, k, :], 8, 256, 1024, rbs[:, v, :], sq, dd)
            for k in range(8):
                d = stt(hT[:, k, t0:t0 + 256], src[:, k, :], aw[:, k, v:v + 1], rbs[:, v, :], ALU.mult, ALU.mult, r, d_aw)
                d = ts(hT[:, k, t0:t0 + 256], hT[:, k, t0:t0 + 256], mods[:, k, v:v + 1], ALU.add, None, None, d, d_mod[0])
            d_h.append(d)

        w_in = I["w_in"]
        raw = Rot([take(512) for _ in range(3)])

        def rope(bk, rows, n0, n, dst, d, users):
            s, sfree, suse = raw.get()
            c1 = copy(s[0:rows, 0:n], bk[0:rows, 0:n], d, sfree, eng="act")
            users.append(c1)
            b2, free2, users2 = banks.get()
            m = mm(b2[0:rows, 0:256], C("rot")[0:rows, 0:rows], s[0:rows, n0:n], True, True, c1, free2)
            a1 = tt(dst[0:rows, n0:n], s[0:rows, n0:n], C("cos")[0:rows, :], ALU.mult, c1)
            s2, s2free, s2use = raw.get()
            a2 = tt(s2[0:rows, 0:256], b2[0:rows, 0:256], C("sin")[0:rows, :], ALU.mult, m, s2free)
            users2.append(a2)
            a3 = tt(dst[0:rows, n0:n], dst[0:rows, n0:n], s2[0:rows, 0:256], ALU.add, a1, a2)
            s2use.append(a3)
            suse.append([m, a1])
            if n0:
                c2 = copy(dst[0:rows, 0:n0], s[0:rows, 0:n0], c1, eng="act")
                suse.append(c2)
                return [a3, c2]
            return a3

        dq = take(4, 256)
        dk = take(4, 512)
        dv = take(4, 512)
        w = W(w_in[:, 0:512], 512)
        d_dq, d_dk, d_dv = [], [], []
        for j in range(4):
            bk, free, users = banks.get()
            d = group(bk[:, 0:256], w, j * 128, (j + 1) * 128, lambda k: hT[:, k, 256:512], 8, d_h, free)
            d_dq.append(rope(bk, 128, 0, 256, dq[:, j, :], d, users))
        w.free(d)
        w = W(w_in[:, 512:1024], 512)
        for j in range(4):
            bk, free, users = banks.get()
            d = group(bk, w, j * 128, (j + 1) * 128, lambda k: hT[:, k, :], 8, free)
            d_dk.append(rope(bk, 128, 256, 512, dk[:, j, :], d, users))
        w.free(d)
        w = W(w_in[:, 1024:1536], 512)
        for t in range(4):
            bk, free, users = banks.get()
            for k in range(8):
                d = mm(bk, hT[:, k, t * 128:(t + 1) * 128], w.ap(k, 0, 512), k == 0, k == 7, free, w.ready(k))
            d_dv.append(copy(dv[:, t, :], bk, d, eng="act"))
            users.append(d_dv[-1])
        w.free(d)
        cq = take(2, 256)
        ckv = take(512)
        kr = take(512)
        w = W(w_in[:, 1536:1984], 448)
        d_cq = []
        for j in range(2):
            bk, free, users = banks.get()
            d = group(bk[:, 0:256], w, j * 128, (j + 1) * 128, lambda k: hT[:, k, 256:512], 8, free)
            d_cq.append(copy(cq[:, j, :], bk[:, 0:256], d))
            users.append(d_cq[-1])
        bk, free, users = banks.get()
        d = group(bk, w, 256, 384, lambda k: hT[:, k, :], 8, free)
        d_ckv = copy(ckv, bk, d)
        users.append(d_ckv)
        bk, free, users = banks.get()
        d = group(bk[0:64, :], w, 384, 448, lambda k: hT[:, k, :], 8, free)
        w.free(d)
        d_kr = rope(bk, 64, 256, 512, kr, d, users)

        rq = take(256)
        rk = take(512)
        r = rms(lambda k: cq[:, k, :], 2, 256, 256, rq, sq, d_cq)
        for j in range(2):
            d_cqn = stt(cq[:, j, :], cq[:, j, :], Pm("qn_w", j), rq, ALU.mult, ALU.mult, r)
        r = rms(lambda k: ckv, 1, 512, 128, rk, sq, d_ckv)
        d_ckvn = stt(ckv, ckv, Pm("kvn_w"), rk, ALU.mult, ALU.mult, r)
        wq = W(I["w_uq"], 768, per=2)
        qn = take(4, 256)
        qr = take(4, 256)
        d_qn, d_qr = [], []
        for h in range(4):
            bk, free, users = banks.get()
            d = group(bk[:, 0:256], wq, h * 192, h * 192 + 128, lambda k: cq[:, k, :], 2, free, d_cqn)
            d_qn.append(copy(qn[:, h, :], bk[:, 0:256], d, eng="act"))
            users.append(d_qn[-1])
            bk, free, users = banks.get()
            d = group(bk[0:64, 0:256], wq, h * 192 + 128, h * 192 + 192, lambda k: cq[:, k, :], 2, free)
            d_qr.append(rope(bk, 64, 0, 256, qr[:, h, :], d, users))
        wq.free(d)
        wk = W(I["w_ukv"], 1024, per=1)
        kn = take(4, 512)
        mv = take(4, 512)
        d_kn, d_mv = [], []
        for h in range(4):
            bk, free, users = banks.get()
            d = mm(bk, wk.ap(0, h * 256, h * 256 + 128), ckv, True, True, free, d_ckvn, wk.ready(0))
            d_kn.append(copy(kn[:, h, :], bk, d, eng="act"))
            users.append(d_kn[-1])
        wv = wk.ap(0, 0, 1024).rearrange("p (h c) -> p h c", h=4)[:, :, 128:256]
        for t in range(4):
            bk, free, users = banks.get()
            d = mm(bk.rearrange("p (h c) -> p h c", h=4), ckv[:, t * 128:(t + 1) * 128], wv, True, True, free)
            d_mv.append(copy(mv[:, t, :], bk, d))
            users.append(d_mv[-1])
        wk.free(d)

        lp = sm(2)
        lam4 = Pm("lam")
        d = tt(lp[0:64, :], lam4[0:64, 0:2], lam4[0:64, 2:4], ALU.mult, d_par)
        bk, free, users = banks.get()
        d = mm(bk[:, 0:2], ones[0:64, :], lp[0:64, :], True, True, d, free)
        le = sm(2)
        d = act(le, bk[:, 0:2], ACT.Exp, d)
        users.append(d)
        nlam = sm()
        d = tt(nlam, le[:, 1:2], le[:, 0:1], ALU.subtract, d)
        lam_init = 0.8 - 0.6 * 1.0
        d_lam = ts(nlam, nlam, -lam_init, ALU.add, None, None, d)

        Pb = Rot([take(512) for _ in range(4)])
        PT = Rot([take(512) for _ in range(2)])
        mix = take(8, 256)

        def softmax(bk, n, scale, d, users):
            mx, den = sm(), sm()
            d1 = op("dve", lambda e: e.tensor_reduce(mx, bk[:, 0:n], AX_X, ALU.max), d)
            d1 = ts(mx, mx, -scale, ALU.mult, None, None, d1)
            p, pfree, puse = Pb.get()
            d2 = act(p[:, 0:n], bk[:, 0:n], ACT.Exp, d1, pfree, scale=scale, bias=mx, acc=den)
            users.append(d2)
            d3 = recip(den, den, d2)
            return p, den, [d2, d3], puse

        def values(p, n, dp, puse, V, dv_, o, osl, dd, first):
            bk, free, users = banks.get()
            for b in range(n):
                d = tr(bk[:, b * 128:(b + 1) * 128], p[:, b * 128:(b + 1) * 128], dp, free)
            puse.append(d)
            t, tfree, tuse = PT.get()
            d = copy(t[:, 0:n * 128], bk[:, 0:n * 128], d, tfree, eng="act")
            users.append(d)
            for b in range(n):
                m = mm(o[:, osl], V(b), t[:, b * 128:(b + 1) * 128], b == 0, b == n - 1, d, dv_, dd if b == 0 else None)
            tuse.append(m)
            return m

        d_mix = [None] * 8
        for h in range(4):
            ob, ofree, ousers = banks.get()
            for t in range(2):
                ps = []
                for c in range(2):
                    bk, free, users = banks.get()
                    rows = slice(c * 64, c * 64 + 64)
                    d = mm(bk, dq[rows, h, t * 128:(t + 1) * 128], dk[rows, h, :], True, True, free, d_dq[h], d_dk[h])
                    ps.append(softmax(bk, 512, 0.125, d, users))
                (p0, r0, e0, u0), (p1, r1, e1, u1) = ps
                d = tt(r1, r1, nlam, ALU.mult, e1, d_lam)
                d = ts(p1, p1, r1, ALU.mult, None, None, d)
                d = stt(p0, p0, r0, p1, ALU.mult, ALU.add, d, e0)
                u1.append(d)
                d = values(p0, 4, d, u0, lambda b: dv[:, b, h * 128:(h + 1) * 128], d_dv, ob,
                           slice(t * 128, t * 128 + 128), ofree, t == 0)
            dc = copy(mix[:, h, :], ob[:, 0:256], d)
            ousers.append(dc)
            r = rms(lambda k: mix[:, h, :], 1, 256, 128, rq, sq, dc)
            sw = sm()
            d = ts(sw, Pm("sub_w"), 1.0 - lam_init, ALU.mult, None, None)
            d_mix[h] = stt(mix[:, h, :], mix[:, h, :], sw, rq, ALU.mult, ALU.mult, r, d)
        for h in range(4):
            ob, ofree, ousers = banks.get()
            for t in range(2):
                bk, free, users = banks.get()
                mm(bk, qn[:, h, t * 128:(t + 1) * 128], kn[:, h, :], True, False, free, d_qn[h], d_kn[h])
                d = mm(bk, qr[0:64, h, t * 128:(t + 1) * 128], kr[0:64, :], False, True, d_qr[h], d_kr)
                p, r, e, u = softmax(bk, 512, 192 ** -0.5, d, users)
                d = ts(p, p, r, ALU.mult, None, None, e)
                d = values(p, 4, d, u, lambda b: mv[:, b, h * 128:(h + 1) * 128], d_mv, ob,
                           slice(t * 128, t * 128 + 128), ofree, t == 0)
            d_mix[4 + h] = copy(mix[:, 4 + h, :], ob[:, 0:256], d)
            ousers.append(d_mix[4 + h])

        modulation(2)
        d_x1 = []
        for c in range(2):
            w = W(I["w_out"][:, c * 512:(c + 1) * 512], 512)
            for j in range(4):
                f = c * 4 + j
                bk, free, users = banks.get()
                d = group(bk[:, 0:256], w, j * 128, (j + 1) * 128, lambda k: mix[:, k, :], 8, free, d_mix)
                d = stt(xv[:, f, :], bk[:, 0:256], mods[:, 16 + f, 0:1], xv[:, f, :], ALU.mult, ALU.add, d, d_mod[2])
                users.append(d)
                d_x1.append(d)
            w.free(queue["pe"][-1][2])

        modulation(3)
        modulation(4)
        fw = sm(8)
        d = ts(fw, mods[:, 32:40, 0], 1.0, ALU.add, None, None, d_mod[4])
        d_fw = tt(fw, fw, Pm("ffn_w"), ALU.mult, d)
        done = barrier()
        at[0] = 0
        sq = Rot([take(512) for _ in range(2)])
        rbrow = take(32)
        hf = take(8, 256)
        rf = take(256)
        d_rb = dma("act", rbrow[0:1, :], I["router_b"], done)
        r = rms(lambda k: xv[:, k, :], 8, 256, 1024, rf, sq, d_x1, done)
        for k in range(8):
            d = stt(hf[:, k, :], xv[:, k, :], fw[:, k:k + 1], rf, ALU.mult, ALU.mult, r, d_fw)
            d_hf = ts(hf[:, k, :], hf[:, k, :], mods[:, 24 + k, 0:1], ALU.add, None, None, d, d_mod[3])
        w = W(I["router_w"], 32, per=8)
        gT = take(256)
        route, d_mask, d_gate = [], [], []
        for t in range(2):
            bk, free, users = banks.get()
            mm(bk[:, 0:32], ones[0:1, :], rbrow[0:1, :], True, False, free, d_rb)
            for k in range(8):
                d = mm(bk[:, 0:32], hf[:, k, t * 128:(t + 1) * 128], w.ap(k, 0, 32), False, k == 7, d_hf, w.ready(k))
            lg, rp, m8, m4 = take(40), take(40), sm(8), sm(8)
            route.append((lg, rp))
            da = copy(lg[:, 0:32], bk[:, 0:32], d)
            users.append(da)
            db = memset(lg[:, 32:40], -3.0e38, eng="dve")
            dc = memset(m4, -3.0e38, eng="dve")
            d = op("dve", lambda e, m8=m8, lg=lg: e.max(m8, lg[:, 0:32]), da)
            d = copy(m4[:, 0:4], m8[:, 0:4], d, dc)
            d = op("dve", lambda e, rp=rp, m4=m4, lg=lg: e.match_replace(rp, m4, lg, 3.0e38), d, da, db)
            d = tt(rp[:, 0:32], rp[:, 0:32], lg[:, 0:32], ALU.not_equal, d)
            d_mask.append(d)
            nm, den = sm(), sm()
            d1 = ts(nm, m8[:, 0:1], -1.0, ALU.mult, None, None)
            d1 = act(lg[:, 0:32], lg[:, 0:32], ACT.Exp, d1, d, bias=nm)
            d = tt(lg[:, 0:32], lg[:, 0:32], rp[:, 0:32], ALU.mult, d1, d)
            d = op("dve", lambda e, den=den, lg=lg: e.tensor_reduce(den, lg[:, 0:32], AX_X, ALU.add), d)
            d = recip(den, den, d)
            d = ts(lg[:, 0:32], lg[:, 0:32], den, ALU.mult, None, None, d)
            d_gate.append(d)
            bk, free, users = banks.get()
            d = tr(bk[0:32, 0:128], lg[:, 0:32], d, free)
            d_gT = copy(gT[0:32, t * 128:(t + 1) * 128], bk[0:32, 0:128], d)
            users.append(d_gT)
        w.free(queue["pe"][-1][2])

        tabm = take(12, 128)
        tabr = take(12)
        d = memset(tabr[32:64, :], 1.0, done, eng="pool")
        d0 = dma("act", tabr[0:32, :], I["rel_bias"], done)
        d = op("pool", lambda e: e.tensor_copy(tabm[0:33, :, :], tabr[0:33, :].unsqueeze(2).to_broadcast([33, 12, 128])), d, d0)
        d_skw = []
        tb = Rot([take(384) for _ in range(2)])
        ha = CST["hot"][0]
        for h in range(12):
            g = h // 4
            bk, free, users = banks.get()
            m = mm(bk[:, 0:384], tabm[0:33, h, :], cst[0:33, ha + g * 384:ha + (g + 1) * 384], True, True, d, free)
            t, tfree, tuse = tb.get()
            c = copy(t, bk[:, 0:384], m, tfree, eng="act")
            users.append(c)
            s = dma("act", skew[h, :, :], t, c)
            tuse.append(s)
            d_skw.append(s)

        posm, gts = [take(32) for _ in range(2)], [g for g, _ in route]
        cnt = take(32)
        mxf = take(1)
        d_pos = []
        bk, free, users = banks.get()
        for t in range(2):
            for u in range(t):
                mm(bk[:, 0:32], ones, route[u][1][:, 0:32], True, False, d_mask, free)
            m = mm(bk[:, 0:32], C("before"), route[t][1][:, 0:32], t == 0, True, d_mask, free)
            d = stt(posm[t], bk[:, 0:32], 1.0, route[t][1][:, 0:32], ALU.add, ALU.mult, m)
            d_pos.append(ts(posm[t], posm[t], -1.0, ALU.add, None, None, d))
            users.append(d)
            free = [free, d]
        mm(bk[:, 32:64], ones, route[0][1][:, 0:32], True, False, free)
        m = mm(bk[:, 32:64], ones, route[1][1][:, 0:32], False, True)
        bk_cnt = bk[:, 32:64]
        d = op("dve", lambda e: e.tensor_reduce(mxf, bk_cnt, AX_X, ALU.max), m)
        users.append(d)
        d_max = copy(most[:, 0:1], mxf, d)

        hm = [take(1024) for _ in range(2)]
        d_hm = []
        for t in range(2):
            for c in range(2):
                bk, free, users = banks.get()
                for j in range(4):
                    m = tr(bk[:, j * 128:(j + 1) * 128], hf[:, c * 4 + j, t * 128:(t + 1) * 128], free, d_hf)
                d = copy(hm[t][:, c * 512:(c + 1) * 512], bk, m, eng="act" if c else "dve")
                users.append(d)
                d_hm.append(d)

        modulation(5)

        bfree = []
        for i in range(8):
            _, f, _ = banks.get()
            bfree.append(f)
        yb = [PS[:, i * 512:(i + 1) * 512] for i in range(4)]
        hb = Rot([PS[:, i * 512:(i + 1) * 512] for i in range(4, 8)])
        for f in hb.users:
            f.extend(bfree)
        b2s = take(1024)
        d_b2 = dma("act", b2s[0:32, :], I["b2"], done)
        for j in range(8):
            d_y = mm(yb[j // 2][:, (j % 2) * 256:(j % 2) * 256 + 256], b2s[0:32, j * 128:(j + 1) * 128], gT[0:32, :],
                     j % 2 == 0, False, bfree, d_b2, d_gT)
        sel = Rot([take(2, S) for _ in range(2)])
        selg = Rot([take(2, S) for _ in range(2)])
        xs_ = Rot([take(8, S) for _ in range(2)])
        pgt = Rot([take(256) for _ in range(3)])
        acts = Rot([take(8, S) for _ in range(2)])
        ysr = Rot([take(1024) for _ in range(2)])
        tg = Rot([take(2, S) for _ in range(3)])
        tu = Rot([take(2, S) for _ in range(3)])
        tsg = Rot([take(2, S) for _ in range(3)])
        b1a = PAR["b1"][0]

        def gather(ex, p):
            P_, pf, pu_ = sel.get()
            Q_, qf, qu = selg.get()
            dp = []
            for t in range(2):
                io = C("iota")[:, p * S:(p + 1) * S]
                dp.append(ts(P_[:, t, :], io, posm[t][:, ex:ex + 1], ALU.is_equal, None, None, pf, d_pos, d_cst))
                dp.append(ts(Q_[:, t, :], io, posm[t][:, ex:ex + 1], ALU.is_equal, gts[t][:, ex:ex + 1], ALU.mult,
                             qf, d_gate))
            X, xf, xu = xs_.get()
            G, gf_, gu = pgt.get()
            dx, dg = [], []
            for c in range(2):
                bk, free, users = hb.get()
                for j in range(4):
                    for t in range(2):
                        f = (c * 4 + j) * 128
                        m = mm(bk[:, j * S:(j + 1) * S], hm[t][:, f:f + 128], P_[:, t, :], t == 0, t == 1, dp, free, d_hm)
                m = tr(bk[0:S, 384:512], Q_[:, c, :], dp)
                d1 = copy(X[:, c * 4:c * 4 + 4, :], bk[:, 0:4 * S].rearrange("p (a b) -> p a b", a=4), m, xf, eng="act")
                d2 = copy(G[0:S, c * 128:(c + 1) * 128], bk[0:S, 384:512], d1, gf_, eng="act")
                users += [d1, d2]
                dx.append(d1)
                dg.append(d2)
            pu_.append(m)
            qu.append(m)
            return X, dx, xu, G, dg, gu

        def up(ex, c, gat, A, dA, af):
            X, dx, xu = gat[:3]
            wg = W(I["w1"][ex, :, c * 512:(c + 1) * 512], 512)
            wu = W(I["w1"][ex, :, 1024 + c * 512:1024 + (c + 1) * 512], 512)
            for j in range(0, 4, 2):
                bk, free, users = hb.get()
                for q in range(2):
                    group(bk[:, q * S:(q + 1) * S], wg, (j + q) * 128, (j + q + 1) * 128, lambda k: X[:, k, :], 8, free, dx)
                    m = group(bk[:, (2 + q) * S:(3 + q) * S], wu, (j + q) * 128, (j + q + 1) * 128,
                              lambda k: X[:, k, :], 8)
                g1, f1, u1 = tg.get()
                uu, f2, u2 = tu.get()
                sg, f3, u3 = tsg.get()
                dg, du = [], []
                for q in range(2):
                    b = b1a + ex * 16 + c * 4 + j + q
                    dg.append(ts(g1[:, q, :], bk[:, q * S:(q + 1) * S], par[:, b:b + 1], ALU.add, 7.0, ALU.min, m, f1))
                for q in range(2):
                    b = b1a + ex * 16 + 8 + c * 4 + j + q
                    du.append(ts(uu[:, q, :], bk[:, (2 + q) * S:(3 + q) * S], par[:, b:b + 1], ALU.add, 7.0, ALU.min, m, f2))
                users.append(du)
                ds = act(sg, g1, ACT.Sigmoid, dg, f3, scale=1.702)
                du = ts(uu, uu, -7.0, ALU.max, 1.0, ALU.add, du)
                du = tt(uu, uu, g1, ALU.mult, du, dg)
                d = tt(A[:, c * 4 + j:c * 4 + j + 2, :], sg, uu, ALU.mult, ds, du, af)
                u1.append(du)
                u2.append(d)
                u3.append(d)
                dA.append(d)
            wg.free(m)
            wu.free(m)
            xu.append(m)

        def down(ex, A, dA, au):
            w = W(I["w2"][ex], 1024, per=2)
            bs = [hb.get() for _ in range(2)]
            for k in range(8):
                for c in range(2):
                    bk, free, users = bs[c]
                    m = mm(bk[0:S, :], A[:, k, :], w.ap(k, c * 512, (c + 1) * 512), k == 0, k == 7, free,
                           dA[k // 2], w.ready(k))
            w.free(m)
            au.append(m)
            Y, yf, yu = ysr.get()
            ds = []
            for c in range(2):
                bk, free, users = bs[c]
                d = copy(Y[0:S, c * 512:(c + 1) * 512], bk[0:S, :], m, yf, eng="act" if c else "dve")
                users.append(d)
                ds.append(d)
            return Y, ds, yu

        def scatter(Y, ds, yu, gat):
            G, dg, gu = gat[3:]
            for j in range(8):
                m = mm(yb[j // 2][:, (j % 2) * 256:(j % 2) * 256 + 256], Y[0:S, j * 128:(j + 1) * 128], G[0:S, :],
                       False, False, ds, dg)
            yu.append(m)
            gu.append(m)
            return m

        def all_experts(p):
            gat = gather(0, p)
            prev = None
            for ex in range(NE):
                A, af, au = acts.get()
                dA = []
                up(ex, 0, gat, A, dA, af)
                nxt = gather(ex + 1, p) if ex + 1 < NE else None
                if prev:
                    y = down(*prev[0])
                up(ex, 1, gat, A, dA, af)
                if prev:
                    scatter(*y, prev[1])
                prev = ((ex, A, dA, au), gat)
                gat = nxt
            y = down(*prev[0])
            return scatter(*y, prev[1])

        d_all = all_experts(0)
        d_max.asked = True
        for p in range(1, 3):
            for e in queue:
                queue[e].append(("if", [d_max], p * S))
            d_all = all_experts(p)
        for p in range(1, 3):
            for e in queue:
                queue[e].append(("end", [], None))

        epoch[0] = 1
        fence = sm(4)
        f_dve = memset(fence[:, 0:1], 0.0, eng="dve")
        f_act = act(fence[:, 1:2], eps, ACT.Copy)
        f_pool = memset(fence[:, 2:3], 0.0, eng="pool")
        f_pe = mm(hb.aps[0][:, 0:1], ones, cst[:, 0:1], True, True, f_dve, f_act, f_pool)
        done = [f_dve, f_act, f_pool, f_pe]
        for i in range(NS):
            release[i] = f_pe
        slot_base[0] = loads[0] = loads[0] + (-loads[0]) % NS
        d_xm = []
        for j in range(8):
            d_xm.append(stt(xv[:, j, :], yb[j // 2][:, (j % 2) * 256:(j % 2) * 256 + 256], mods[:, 40 + j, 0:1],
                            xv[:, j, :], ALU.mult, ALU.add, f_pe))
        banks = Rot([PS[:, i * 512:(i + 1) * 512] for i in range(8)])
        banks.users = [[d_xm[-1], f_pe] for _ in range(8)]
        at[0] = 0
        sq = Rot([take(512) for _ in range(2)])
        rf = take(256)
        xn = take(8, 256)

        def norm_to(dst, wname, *after):
            r = rms(lambda k: xv[:, k, :], 8, 256, 1024, rf, sq, *after)
            for k in range(8):
                d = stt(dst[:, k, :], xv[:, k, :], Pm(wname, k), rf, ALU.mult, ALU.mult, r)
            return d

        d = norm_to(xv, "fin_w", d_xm, done)
        d_xn = norm_to(xn, "attn2_w", d)

        T = take(12, 256)
        d_T = []
        for h in range(12):
            base = skew[h, :, :].rearrange("p n -> (p n)")[127:127 + 128 * 383]
            d_T.append(dma("act", T[:, h, :], base.rearrange("(p n) -> p n", n=383)[:, 0:256], d_skw, done))

        w2i = I["w_in_2"]

        def projT(c0, ntile, dst, eng="act"):
            ds = []
            j = 0
            while j < ntile:
                m = min(4, ntile - j)
                w = W(w2i[:, c0 + j * 128:c0 + (j + m) * 128], m * 128)
                for i in range(0, m, 2):
                    bk, free, users = banks.get()
                    n = min(2, m - i)
                    for q in range(n):
                        d = group(bk[:, q * 256:(q + 1) * 256], w, (i + q) * 128, (i + q + 1) * 128,
                                  lambda k: xn[:, k, :], 8, free, d_xn)
                    c = copy(dst[:, j + i:j + i + n, :], bk[:, 0:n * 256].rearrange("p (a b) -> p a b", a=n), d, eng=eng)
                    users.append(c)
                    ds += [c] * n
                w.free(d)
                j += m
            return ds

        def projV(c0, n, dst):
            ds = []
            j = 0
            while j < n:
                m = min(512, n - j)
                w = W(w2i[:, c0 + j:c0 + j + m], m)
                for t in range(2):
                    bk, free, users = banks.get()
                    for k in range(8):
                        d = mm(bk[:, 0:m], xn[:, k, t * 128:(t + 1) * 128], w.ap(k, 0, m), k == 0, k == 7,
                               free, d_xn, w.ready(k))
                    c = copy(dst[:, t, j:j + m], bk[:, 0:m], d, eng="act")
                    users.append(c)
                    ds.append(c)
                w.free(d)
                j += m
            return ds

        us = take(4, 256)
        d_us = projT(4352, 4, us)
        sbq, sbk = take(4, 256), take(4, 256)
        d_sq = projT(2816, 4, sbq)
        d_sk = projT(3328, 4, sbk)
        sbv = take(2, 512)
        d_sv = projV(3840, 512, sbv)
        dlq, dlk = take(6, 256), take(6, 256)
        d_lq = projT(512, 6, dlq)
        d_lk = projT(1280, 6, dlk)
        dlv = take(2, 768)
        d_lv = projV(2048, 768, dlv)
        pu = take(4, 256)
        d_pu = projT(0, 4, pu)

        mark = at[0]
        ysT = take(4, 256)
        mark2 = at[0]
        s5 = [take(16) for _ in range(16)]
        (dt, th, kk, rr, wc, wsn, lbr, lbi, dn, cfr, cfi, t1, t2, t3, t4, t5) = s5
        are, aim = Pm("s5_are"), Pm("s5_aim")
        d = act(dt, Pm("s5_ldt"), ACT.Exp, done)
        d = tt(th, aim, dt, ALU.mult, d)
        e1 = tt(t1, are, dt, ALU.mult, d)
        d_r = act(rr, t1, ACT.Exp, e1)
        two_pi = 6.283185307179586
        d = ts(kk, th, 1.0 / two_pi, ALU.mult, 12582912.0, ALU.add, d)
        d = ts(kk, kk, -12582912.0, ALU.add, None, None, d)
        for part in (6.28125, 0.0019350051879882812, 3.0199159819567e-07):
            d = stt(th, kk, -part, th, ALU.mult, ALU.add, d)
        d = ts(th, th, 3.1415925, ALU.min, -3.1415925, ALU.max, d)
        d_s = act(wsn, th, ACT.Sin, d)
        d = act(t2, th, ACT.Abs, d)
        d = ts(t2, t2, -1.0, ALU.mult, 1.5707963267948966, ALU.add, d)
        d_c = act(wc, t2, ACT.Sin, d)
        d = tt(lbr, rr, wc, ALU.mult, d_c, d_r)
        da = ts(lbr, lbr, -1.0, ALU.add, None, None, d)
        db = tt(lbi, rr, wsn, ALU.mult, d_s, d_r)
        d = tt(dn, are, are, ALU.mult)
        d1 = tt(t3, aim, aim, ALU.mult)
        d = tt(dn, dn, t3, ALU.add, d, d1)
        d = recip(dn, dn, d)
        d1 = tt(t4, lbr, are, ALU.mult, da)
        d2 = tt(t5, lbi, aim, ALU.mult, db)
        d3 = tt(t4, t4, t5, ALU.add, d1, d2)
        dr_ = tt(cfr, t4, dn, ALU.mult, d3, d)
        d1 = tt(t4, lbi, are, ALU.mult, dr_)
        d2 = tt(t5, lbr, aim, ALU.mult, d3)
        d3 = tt(t4, t4, t5, ALU.subtract, d1, d2)
        di_ = tt(cfi, t4, dn, ALU.mult, d3)
        bt = take(2, 512)
        ct = take(2, 512)
        cc = take(2, 512)
        d_bt = dma("act", bt[:, 0, :], I["s5_bre"], done)
        d_bt = [d_bt, dma("act", bt[:, 1, :], I["s5_bim"], done)]
        d_ct = [dma("act", ct[:, 0, :], I["s5_cre"], done), dma("act", ct[:, 1, :], I["s5_cim"], done)]

        def b32(x):
            return x.unsqueeze(2).to_broadcast([128, 16, 32])

        def v32(x):
            return x.rearrange("p (a b) -> p a b", b=32)

        ctmp = take(512)
        d1 = tt(v32(cc[:, 0, :]), v32(ct[:, 0, :]), b32(cfr), ALU.mult, d_ct, dr_)
        d2 = tt(v32(ctmp), v32(ct[:, 1, :]), b32(cfi), ALU.mult, d_ct, di_)
        d_cc = tt(cc[:, 0, :], cc[:, 0, :], ctmp, ALU.subtract, d1, d2)
        d1 = tt(v32(cc[:, 1, :]), v32(ct[:, 0, :]), b32(cfi), ALU.mult)
        d2 = tt(v32(ctmp), v32(ct[:, 1, :]), b32(cfr), ALU.mult, d_cc)
        d1 = tt(cc[:, 1, :], cc[:, 1, :], ctmp, ALU.add, d1, d2)
        d_cc = ts(cc[:, 1, :], cc[:, 1, :], -1.0, ALU.mult, None, None, d1)
        pc = [wc] + [take(16) for _ in range(7)]
        psn = [wsn] + [take(16) for _ in range(7)]
        d = [d_c, d_s]
        for k in range(7):
            a = tt(pc[k + 1], pc[k], pc[k], ALU.mult, d)
            b = tt(t1, psn[k], psn[k], ALU.mult, d, e1, d_r)
            a = tt(pc[k + 1], pc[k + 1], t1, ALU.subtract, a, b)
            b = tt(psn[k + 1], pc[k], psn[k], ALU.mult, d)
            b = ts(psn[k + 1], psn[k + 1], 2.0, ALU.mult, None, None, b)
            e1 = a
            d = [a, b]
        d_pw = d
        Ct, St = take(4, 256), take(4, 256)
        xr, xi, tm = take(4, 256), take(4, 256), take(4, 256)
        tp = tm
        d_tab_free = None
        d_prev = None
        for q in range(4):
            a = memset(Ct[:, :, 0:1], 1.0, d_tab_free, done)
            b = memset(St[:, :, 0:1], 0.0, d_tab_free)
            d = [a, b]
            for k in range(8):
                n = 1 << k

                def bc(x):
                    return x[:, q * 4:q * 4 + 4].unsqueeze(2).to_broadcast([128, 4, n])
                o = slice(n, 2 * n)
                p = slice(0, n)
                x1 = tt(Ct[:, :, o], Ct[:, :, p], bc(pc[k]), ALU.mult, d, d_pw, eng="pool")
                x2 = tt(tp[:, :, p], St[:, :, p], bc(psn[k]), ALU.mult, d, d_prev, eng="pool")
                x3 = tt(Ct[:, :, o], Ct[:, :, o], tp[:, :, p], ALU.subtract, x1, x2, eng="pool")
                x1 = tt(St[:, :, o], St[:, :, p], bc(pc[k]), ALU.mult, d, eng="pool")
                x2 = tt(tp[:, :, p], Ct[:, :, p], bc(psn[k]), ALU.mult, d, x3, eng="pool")
                x4 = tt(St[:, :, o], St[:, :, o], tp[:, :, p], ALU.add, x1, x2, eng="pool")
                d = [x3, x4]
            d_tab = d
            b4 = []
            for i in range(4):
                bk, free, users = banks.get()
                for v in range(2):
                    m = mm(bk[:, v * 256:(v + 1) * 256], bt[32 * i:32 * i + 32, v, q * 128:(q + 1) * 128],
                           us[32 * i:32 * i + 32, q, :], True, True, free, d_bt, d_us)
                xs = slice(i, i + 1)
                Pr, Pi = bk[:, 0:256].unsqueeze(1), bk[:, 256:512].unsqueeze(1)
                y1 = tt(xr[:, xs, :], Pr, Ct[:, xs, :], ALU.mult, m, d_tab, d_prev)
                y2 = tt(tm[:, xs, :], Pi, St[:, xs, :], ALU.mult, m)
                y1 = tt(xr[:, xs, :], xr[:, xs, :], tm[:, xs, :], ALU.add, y1, y2)
                y3 = tt(xi[:, xs, :], Pi, Ct[:, xs, :], ALU.mult)
                y2 = tt(tm[:, xs, :], Pr, St[:, xs, :], ALU.mult, y1)
                users.append(y2)
                y3 = tt(xi[:, xs, :], xi[:, xs, :], tm[:, xs, :], ALU.subtract, y3, y2)

                def scan(x, *after, rbc=rr[:, q * 4 + i:q * 4 + i + 1].to_broadcast([128, 256])):
                    return op("dve", lambda e: e.tensor_tensor_scan(x, rbc, x, 0.0, ALU.mult, ALU.add), *after)
                z1 = scan(xr[:, i, :], y1, d_r)
                z2 = scan(xi[:, i, :], y3)
                b4 += [z1, z2]
            hr = take(4, 256) if q == 0 else hr
            a1 = tt(hr, xr, Ct, ALU.mult, b4, d_prev)
            a2 = tt(tm, xi, St, ALU.mult, b4)
            a1 = tt(hr, hr, tm, ALU.subtract, a1, a2)
            a3 = tt(xr, xr, St, ALU.mult, a1)
            a2 = tt(tm, xi, Ct, ALU.mult, a1)
            a3 = tt(xr, xr, tm, ALU.add, a3, a2)
            d_tab_free = a2
            bk, free, users = banks.get()
            for i in range(4):
                o = bk[32 * i:32 * i + 32, 0:256]
                cs = slice((q * 4 + i) * 32, (q * 4 + i) * 32 + 32)
                mm(o, cc[:, 0, cs], hr[:, i, :], True, False, a1, d_cc, free)
                m = mm(o, cc[:, 1, cs], xr[:, i, :], False, True, a3)
            d_prev = [m, a3]
            d_ys = stt(ysT[:, q, :], us[:, q, :], Pm("s5_d", q), bk[:, 0:256], ALU.mult, ALU.add, m)
            users.append(d_ys)
        g1 = hr
        d = act(g1, ysT, ACT.Square, d_ys)
        d = ts(g1, g1, 0.044715, ALU.mult, 1.0, ALU.add, d)
        d = tt(g1, g1, ysT, ALU.mult, d)
        d = act(g1, g1, ACT.Sigmoid, d, scale=2.0 * 0.7978845608028654)
        d_gl = tt(g1, g1, ysT, ALU.mult, d)
        sgl = Rot([tm[:, 0, :], tm[:, 1, :]])
        for c in range(2):
            wg = W(I["s5_w_glu"][:, c * 256:(c + 1) * 256], 256)
            wu = W(I["s5_w_glu"][:, 512 + c * 256:512 + (c + 1) * 256], 256)
            for j in range(2):
                bk, free, users = banks.get()
                group(bk[:, 0:256], wg, j * 128, (j + 1) * 128, lambda k: g1[:, k, :], 4, free, d_gl)
                d = group(bk[:, 256:512], wu, j * 128, (j + 1) * 128, lambda k: g1[:, k, :], 4)
                s, sf, su = sgl.get()
                da = act(s, bk[:, 256:512], ACT.Sigmoid, d, sf)
                d_s5 = tt(ysT[:, c * 2 + j, :], bk[:, 0:256], s, ALU.mult, da)
                users.append(d_s5)
                su.append(d_s5)
            wg.free(d)
            wu.free(d)

        done5 = barrier()
        at[0] = mark2
        mg = arena[:, mark2:mark2 + 2048].rearrange("p (k t) -> p k t", k=8)
        Pb = Rot([take(768) for _ in range(2)])
        PT = Rot([take(768) for _ in range(2)])
        ysb = take(4, 256)
        zr = Rot([take(384) for _ in range(2)])
        er = Rot([take(384) for _ in range(2)])
        sr = Rot([take(384) for _ in range(2)])
        d_sb = []
        for h in range(4):
            hc = slice(h * 128, h * 128 + 128)
            bk, free, users = banks.get()
            mm(bk[:, 0:256], sbk[:, h, 0:128], sbq[:, h, :], True, True, free, d_sq[h], d_sk[h])
            m = mm(bk[:, 256:384], sbk[:, h, 128:256], sbq[:, h, 128:256], True, True)
            z, zf, zu = zr.get()
            e_, ef, eu = er.get()
            s, sf, su = sr.get()
            dz = act(z, bk[:, 0:384], ACT.Copy, m, zf, done5, scale=128 ** -0.5)
            users.append(dz)
            d = act(e_, z, ACT.Abs, dz, ef, done5)
            d = act(e_, e_, ACT.Exp, d, scale=-1.0)
            d = act(e_, e_, ACT.Ln, d, bias=1.0)
            d = stt(s, z, 0.0, e_, ALU.max, ALU.add, d, dz, sf, done5)
            eu.append(d)
            d = tt(s, s, C("m01"), ALU.mult, d)
            bk, free, users = banks.get()
            mm(bk[:, 0:256], C("tri"), s[:, 0:256], True, False, d, free)
            mm(bk[:, 128:256], ones, s[:, 256:384], False, True)
            m = mm(bk[:, 256:384], C("tri"), s[:, 256:384], True, True)
            d = tt(z, z, bk[:, 0:384], ALU.subtract, m)
            users.append(d)
            d = tt(z, z, C("mneg"), ALU.add, d)
            d = act(s, z, ACT.Exp, d)
            zu.append(d)
            bk, free, users = banks.get()
            mm(bk[:, 0:256], sbv[:, 0, hc], s[:, 0:256], True, False, d, free, d_sv)
            m = mm(bk[:, 128:256], sbv[:, 1, hc], s[:, 256:384], False, True)
            su.append(m)
            d = copy(ysb[:, h, :], bk[:, 0:256], m)
            users.append(d)
            d_sb.append(d)

        ydl = take(2, 256)
        Tv = T
        d_dl = []
        for hs in range(4):
            rows = slice((hs % 2) * 64, (hs % 2) * 64 + 64)
            for t in range(2):
                nk = 128 * (t + 1)
                x, xf, xu = Pb.get()
                dd = []
                for g in range(3):
                    h = g * 4 + hs
                    bk, free, users = banks.get()
                    m = mm(bk[:, 0:nk], dlq[rows, h // 2, t * 128:(t + 1) * 128], dlk[rows, h // 2, 0:nk], True, True,
                           free, d_lq[h // 2], d_lk[h // 2])
                    d = stt(x[:, g * nk:(g + 1) * nk], bk[:, 0:nk], 0.125, Tv[:, h, 256 - nk:256], ALU.mult, ALU.add,
                            m, d_T[h], xf)
                    users.append(d)
                    dd.append(d)
                mx, den = sm(), sm()
                xx = x[:, 0:3 * nk]
                d = op("dve", lambda e, mx=mx, xx=xx: e.tensor_reduce(mx, xx, AX_X, ALU.max), dd)
                d = ts(mx, mx, -1.0, ALU.mult, None, None, d)
                d = act(xx, xx, ACT.Exp, d, bias=mx, acc=den)
                d = recip(den, den, d)
                d = ts(xx, xx, den, ALU.mult, None, None, d)
                nb = 3 * (t + 1)
                pt, pf, pu_ = PT.get()
                for a in range(0, nb, 3):
                    bk, free, users = banks.get()
                    for b in range(3):
                        m = tr(bk[:, b * 128:(b + 1) * 128], x[:, (a + b) * 128:(a + b + 1) * 128], d, free)
                    c = copy(pt[:, a * 128:(a + 3) * 128], bk[:, 0:384], m, pf, eng="act")
                    users.append(c)
                xu.append(m)
                ob, ofree, ousers = banks.get()
                for b in range(nb):
                    g, kb = b // (t + 1), b % (t + 1)
                    h = g * 4 + hs
                    m = mm(ob[rows, 0:128], dlv[:, kb, h * 64:(h + 1) * 64], pt[:, b * 128:(b + 1) * 128],
                           b == 0, b == nb - 1, c, d_lv, ofree)
                pu_.append(m)
                d = copy(ydl[rows, hs // 2, t * 128:(t + 1) * 128], ob[rows, 0:128], m)
                ousers.append(d)
                d_dl.append(d)

        ypl = take(4, 256)
        pa, pb = take(4, 256), take(4, 256)
        src = pu
        d = [d_pu, done5]
        lv = []
        for i in range(4):
            n = 1 << i
            dst = pa if i % 2 == 0 else pb
            x1 = tt(dst[:, i:4, n:256], src[:, i:4, n:256], src[:, i:4, 0:256 - n], ALU.add, d, eng="pool")
            x2 = copy(dst[:, i:4, 0:n], src[:, i:4, 0:n], d, eng="pool")
            lv.append((dst, [x1, x2]))
            d = [x1, x2]
            inv = C("inv").rearrange("p (a b) -> p a b", a=4)
            y = tt(ypl[:, i, :], dst[:, i, :], inv[:, i, :], ALU.mult, d, eng="pool")
            y = tt(ypl[:, i, :], ypl[:, i, :], pu[:, i, :], ALU.subtract, y, eng="pool")
            d = [x1, x2, y]
            src = dst
        w = W(I["pool_w"], 128)
        d_pl = []
        for i in range(4):
            bk, free, users = banks.get()
            m = mm(bk[:, 0:256], w.ap(i, 0, 128), ypl[:, i, :], True, True, free, y, w.ready(i))
            d = ts(ypl[:, i, :], bk[:, 0:256], Pm("pscale", i), ALU.mult, None, None, m)
            users.append(d)
            d_pl.append(d)
        w.free(m)

        gs = Rot([take(256) for _ in range(3)])
        row = 0
        d_mg = [None] * 8
        for bi, (yt, K, dy) in enumerate(((ypl, 4, d_pl), (ydl, 2, d_dl), (ysb, 4, d_sb), (ysT, 4, d_s5))):
            for c in range(2):
                wg = W(I["w_gate"][bi, :, c * 512:(c + 1) * 512], 512)
                wb = W(I["w_branch"][row:row + K * 128, c * 512:(c + 1) * 512], 512)
                for j in range(4):
                    f = c * 4 + j
                    bk, free, users = banks.get()
                    group(bk[:, 0:256], wg, j * 128, (j + 1) * 128, lambda k: xn[:, k, :], 8, free)
                    m = group(bk[:, 256:512], wb, j * 128, (j + 1) * 128, lambda k: yt[:, k, :], K, dy)
                    s, sf, su = gs.get()
                    d = act(s, bk[:, 0:256], ACT.Sigmoid, m, sf)
                    if bi == 0:
                        d = tt(mg[:, f, :], bk[:, 256:512], s, ALU.mult, d)
                        users.append(d)
                    else:
                        d = tt(s, bk[:, 256:512], s, ALU.mult, d)
                        users.append(d)
                        d = tt(mg[:, f, :], mg[:, f, :], s, ALU.add, d, d_mg[f])
                    su.append(d)
                    d_mg[f] = d
                wg.free(m)
                wb.free(m)
            row += K * 128
        d_x2 = []
        for c in range(2):
            w = W(I["w_out_2"][:, c * 512:(c + 1) * 512], 512)
            for j in range(4):
                f = c * 4 + j
                bk, free, users = banks.get()
                m = group(bk[:, 0:256], w, j * 128, (j + 1) * 128, lambda k: mg[:, k, :], 8, free, d_mg)
                d = tt(xv[:, f, :], bk[:, 0:256], xv[:, f, :], ALU.add, m)
                users.append(d)
                d_x2.append(d)
            w.free(m)

        done = barrier()
        at[0] = 0
        sq = Rot([take(512) for _ in range(2)])
        rf = take(256)
        hn = take(8, 256)
        d_hn = norm_to(hn, "ffn2_w", d_x2, done)
        hh = take(22, 256)
        gs = Rot([take(256) for _ in range(3)])
        d_hh = []
        for c in range(6):
            n = 512 if c < 5 else 256
            wg = W(I["w_up"][:, c * 512:c * 512 + n], n)
            wu = W(I["w_up"][:, 2816 + c * 512:2816 + c * 512 + n], n)
            for j in range(n // 128):
                bk, free, users = banks.get()
                group(bk[:, 0:256], wg, j * 128, (j + 1) * 128, lambda k: hn[:, k, :], 8, free, d_hn)
                m = group(bk[:, 256:512], wu, j * 128, (j + 1) * 128, lambda k: hn[:, k, :], 8)
                s, sf, su = gs.get()
                d = act(s, bk[:, 0:256], ACT.Sigmoid, m, sf)
                d = tt(s, bk[:, 0:256], s, ALU.mult, d)
                d = tt(hh[:, c * 4 + j, :], bk[:, 256:512], s, ALU.mult, d)
                users.append(d)
                su.append(d)
                d_hh.append(d)
            wg.free(m)
            wu.free(m)
        acc = []
        for i in range(4):
            acc.append(banks.get())
        for c in range(11):
            w = W(I["w_down"][c * 256:(c + 1) * 256, :], 1024, per=2)
            for kk_ in range(2):
                k = c * 2 + kk_
                for j in range(8):
                    bk, free, users = acc[j // 2]
                    m = mm(bk[:, (j % 2) * 256:(j % 2) * 256 + 256], w.ap(kk_, j * 128, (j + 1) * 128), hh[:, k, :],
                           k == 0 and j % 2 == 0, k == 21, free, d_hh[k], w.ready(kk_))
            w.free(m)
        for i in range(4):
            bk, free, users = acc[i]
            d = tt(xv[:, 2 * i:2 * i + 2, :], bk.rearrange("p (a b) -> p a b", a=2), xv[:, 2 * i:2 * i + 2, :], ALU.add, m)
            users.append(d)
        d = norm_to(xv, "fin2_w", d)
        d_out = dma("sp", out.rearrange("(k p) t -> p k t", p=128), xv, d)
        last = [d_out] + d_skw
        queue["sp"].append((None, last, Done("sp")))

        for e in esem[0]:
            n = [0, 0]
            for fn, _, d in queue[e]:
                if callable(fn) and d.sem is None and d.asked:
                    n[d.epoch] += 1
                    d.sem, d.val = esem[d.epoch][e], n[d.epoch]

        block = ctx.enter_context(nc.Block())

        def play(name):
            def body(eng):
                seen, inner = {}, []
                for fn, waits, d in queue[name]:
                    if fn == "end":
                        body_, kept = inner.pop()
                        body_.__exit__(None, None, None)
                        seen = kept
                        continue
                    need = {}
                    for w in waits:
                        k = id(w.sem)
                        if seen.get(k, 0) < w.val and (k not in need or need[k].val < w.val):
                            need[k] = w
                    for k, w in need.items():
                        eng.wait_ge(w.sem, w.val)
                        seen[k] = w.val
                    if fn == "if":
                        n = eng.value_load(most[0:1, 0:1], min_val=0, max_val=256)
                        body_ = eng.If(n > d)
                        inner.append((body_, dict(seen)))
                        body_.__enter__()
                        continue
                    if fn is None:
                        continue
                    ins = fn(eng)
                    if d.sem is not None:
                        ins.then_inc(d.sem, 16 if d.dma else 1)
            return body

        block.sync(play("sp"))
        block.tensor(play("pe"))
        block.vector(play("dve"))
        block.scalar(play("act"))
        block.gpsimd(play("pool"))


_RAW = {"w_ada": (1024, 6144), "w_in": (1024, 1984), "w_uq": (256, 768), "w_ukv": (128, 1024), "w_out": (1024, 1024),
        "router_w": (1024, 32), "router_b": (1, 32), "w1": (32, 1024, 2048), "w2": (32, 1024, 1024), "b2": (32, 1024),
        "rel_bias_2": (32, 12), "w_in_2": (1024, 4864), "pool_w_2": (512, 128), "s5_w_glu_2": (512, 1024),
        "w_branch_2": (1792, 1024), "w_gate_2": (4, 1024, 1024), "w_out_2": (1024, 1024), "w_up_2": (1024, 5632),
        "w_down_2": (2816, 1024)}
_NAMES = {"rel_bias_2": "rel_bias", "pool_w_2": "pool_w", "s5_w_glu_2": "s5_w_glu", "w_branch_2": "w_branch",
          "w_gate_2": "w_gate", "w_up_2": "w_up", "w_down_2": "w_down"}


def constants():
    import numpy as np
    f = np.float32
    c = np.zeros((128, CST_N), f)

    def put(name, a):
        lo, hi = CST[name]
        c[:a.shape[0], lo:hi] = a
    i = np.arange(128)
    put("ident", np.eye(128, dtype=f))
    put("ones", np.ones((128, 128), f))
    rot = np.zeros((128, 128), f)
    for m in range(128):
        if (m // 16) % 2 == 0:
            rot[m + 16, m] = -1.0
        else:
            rot[m - 16, m] = 1.0
    put("rot", rot)
    put("tri", (i[:, None] >= i[None, :]).astype(f))
    put("before", (i[:, None] < i[None, :]).astype(f))
    put("iota", np.broadcast_to(np.arange(3 * S, dtype=f), (128, 3 * S)))
    t = np.arange(256)
    inv = f(10000.0) ** (-np.arange(16, dtype=f) / f(16))
    d = np.arange(128) % 64
    pos = np.where((d // 32 == 0)[:, None], (t // 64)[None, :], (t % 64)[None, :]).astype(f)
    ang = pos * inv[d % 16][:, None]
    put("cos", np.cos(ang).astype(f))
    put("sin", np.sin(ang).astype(f))
    q = np.concatenate([np.arange(256), np.arange(128, 256)])
    k = np.concatenate([np.zeros(256, int), np.full(128, 128)])[None, :] + i[:, None]
    valid = k < q[None, :]
    put("m01", valid.astype(f))
    put("mneg", np.where(valid, f(0), f(-BIG)))
    put("inv", np.broadcast_to(np.concatenate([1.0 / np.minimum(t + 1, w) for w in (2, 4, 8, 16)]).astype(f), (128, 1024)))
    dist = 255 - np.arange(384)
    df = np.maximum(dist, 1).astype(f)
    large = 16 + (np.log(df / f(16)) / f(np.log(2048 / 16)) * f(16)).astype(np.int32)
    bucket = np.where(dist < 16, dist, np.minimum(large, 31))
    hot = np.zeros((33, 3, 384), f)
    for g, (win, dil) in enumerate(((128, 1), (512, 4), (2048, 16))):
        ok = (dist >= 0) & (dist % dil == 0) & (dist <= win)
        for n in range(384):
            if ok[n]:
                hot[bucket[n], g, n] = 1.0
            else:
                hot[32, g, n] = -BIG
    put("hot", hot.reshape(33, 1152))
    put("eps", np.full((128, 1), EPS, f))
    return c


def kernel(**inputs):
    import numpy as _np
    import concourse.bacc as _bacc
    from concourse.bass_utils import run_bass_kernel_spmd as _run

    x = {k: _np.asarray(v) for k, v in inputs.items()}

    def col(a):
        return a.reshape(-1, 128).T

    p = _np.zeros((128, PAR_N), _np.float32)

    def put(name, a):
        lo, hi = PAR[name]
        p[:a.shape[0], lo:hi] = a

    put("c2", _np.stack([col(x["c"]), col(x["c_ctx"])], axis=2).reshape(128, 16))
    for name, src in (("b_ada", "b_ada"), ("attn_w", "attn_norm_w"), ("qn_w", "q_norm_w"), ("kvn_w", "kv_norm_w"),
                      ("sub_w", "subln_w"), ("ffn_w", "ffn_norm_w"), ("fin_w", "final_norm_w"),
                      ("attn2_w", "attn_norm_g_2"), ("ffn2_w", "ffn_norm_g_2"), ("fin2_w", "final_norm_g_2"),
                      ("b1", "b1"), ("pscale", "pool_scale_2"), ("s5_are", "s5_a_re_2"), ("s5_aim", "s5_a_im_2"),
                      ("s5_d", "s5_d_2")):
        put(name, col(x[src]))
    put("lam", _np.stack([x[n].reshape(64) for n in ("lambda_q1", "lambda_q2", "lambda_k1", "lambda_k2")], axis=1))
    put("s5_ldt", _np.repeat(x["s5_log_dt_2"].reshape(16, 2, 1), 64, axis=2).reshape(16, 128).T)
    arrays = {"par": p, "cst": constants(),
              "xT": _np.ascontiguousarray(x["x"].reshape(256, 1024).T),
              "ctxT": _np.ascontiguousarray(x["ctx"].reshape(256, 1024).T)}
    for v in ("re", "im"):
        b = x[f"s5_b_{v}_2"].reshape(4, 4, 2, 64, 16)
        bt = _np.zeros((4, 2, 16, 4, 2, 64), _np.float32)
        c = x[f"s5_c_{v}_2"].reshape(16, 2, 16, 64)
        ct = _np.zeros((2, 64, 16, 2, 16), _np.float32)
        for g in range(2):
            bt[:, g, :, :, g, :] = b[:, :, g].transpose(1, 3, 0, 2)
            ct[g, :, :, g, :] = c[:, g].transpose(2, 0, 1)
        arrays["s5_b" + v] = bt.reshape(128, 512)
        arrays["s5_c" + v] = ct.reshape(128, 512)
    for name, shape in _RAW.items():
        arrays[_NAMES.get(name, name)] = _np.ascontiguousarray(x[name]).reshape(shape)

    nc = _bacc.Bacc("TRN2", target_bir_lowering=False, num_devices=1)
    aps = {n: nc.dram_tensor("in_" + n, a.shape, F32, kind="ExternalInput").ap() for n, a in arrays.items()}
    out = nc.dram_tensor("out_0", (1024, 256), F32, kind="ExternalOutput").ap()
    build(nc, aps, out)
    r = _run(nc, [{"in_" + n: a for n, a in arrays.items()}], core_ids=[0])
    return _np.ascontiguousarray(r.results[0]["out_0"].T).reshape(1, 256, 1024)
```

```python
from contextlib import ExitStack

import concourse.bass as bass
from concourse import mybir

ALU = mybir.AluOpType
ACT = mybir.ActivationFunctionType
F32 = mybir.dt.float32
AX_X = mybir.AxisListType.X
EPS = 1e-6
NS = 8
NX = 2
SLOT = 2048
NE = 32
S = 128
BIG = 1.0e30

PAR = {}
CST = {}


def _table(into, rows):
    at = 0
    for name, n in rows:
        into[name] = (at, at + n)
        at += n
    return at


PAR_N = _table(PAR, [("c2", 16), ("b_ada", 48), ("attn_w", 8), ("qn_w", 2), ("kvn_w", 1), ("sub_w", 1),
                     ("ffn_w", 8), ("fin_w", 8), ("attn2_w", 8), ("ffn2_w", 8), ("fin2_w", 8), ("lam", 4),
                     ("b1", 512), ("pscale", 4), ("s5_are", 16), ("s5_aim", 16), ("s5_ldt", 16), ("s5_d", 4)])
CST_N = _table(CST, [("ident", 128), ("ones", 128), ("rot", 128), ("tri", 128), ("before", 128), ("iota", 2 * S), ("cos", 256), ("sin", 256),
                     ("m01", 384), ("mneg", 384), ("inv", 1024), ("eps", 1)])


class Done:

    def __init__(self, eng, sem=None, val=None):
        self.dma = sem is not None
        self.eng, self.sem, self.val, self.asked = eng, sem, val, sem is not None


class Rot:

    def __init__(self, aps):
        self.aps, self.users, self.n = aps, [[] for _ in aps], -1

    def get(self):
        self.n += 1
        i = self.n % len(self.aps)
        users, self.users[i] = self.users[i], []
        return self.aps[i], users, self.users[i]


def build(nc, I, out):
    ctx = ExitStack()
    with ctx:
        def sb(name, n):
            return ctx.enter_context(nc.sbuf_tensor(name, [128, n], F32))

        ring = sb("ring", NS * SLOT)
        par = sb("par", PAR_N)
        cst = sb("cst", CST_N)
        xT = sb("xT", 2048)
        small = sb("small", 480)
        most = ctx.enter_context(nc.sbuf_tensor("most", [128, 2], mybir.dt.int32))
        AR = 30200
        arena = sb("arena", AR)
        PS = ctx.enter_context(nc.psum_tensor("PS", [128, 4096], F32))
        tabs = nc.dram_tensor("phase_scratch", [4, 2, 128, 1024], F32, kind="Internal").ap()
        skew = nc.dram_tensor("skew_scratch", [12, 128, 384], F32, kind="Internal").ap()

        esem = [{e: ctx.enter_context(nc.semaphore(f"n{w}_{e}")) for e in ("pe", "act", "dve", "pool")}
                for w in range(2)]
        epoch = [0]
        queue = {e: [] for e in ("pe", "act", "dve", "pool", "sp")}

        def flat(after):
            for a in after:
                if a is None:
                    continue
                if isinstance(a, Done):
                    yield a
                else:
                    yield from flat(a)

        def op(eng, fn, *after):
            waits = list(flat(after))
            for w in waits:
                w.asked = True
            d = Done(eng)
            d.epoch = epoch[0]
            queue[eng].append((fn, waits, d))
            return d

        nsem = [0]

        def dma(eng, dst, src, *after, sem=None, val=16):
            waits = list(flat(after))
            for w in waits:
                w.asked = True
            if sem is None:
                sem = ctx.enter_context(nc.semaphore(f"dma{nsem[0]}"))
                nsem[0] += 1
            d = Done(eng, sem, val)
            queue[eng].append((lambda e: e.dma_start(dst, src), waits, d))
            return d

        def mm(o, l, r, start, stop, *after):
            return op("pe", lambda e: e.matmul(o, l, r, start=start, stop=stop, skip_group_check=True), *after)

        def tr(o, i, *after):
            n = i.shape[0]
            return op("pe", lambda e: e.transpose(o, i, C("ident")[0:n, 0:n]), *after)

        def act(o, i, f, *after, scale=1.0, bias=0.0, acc=None):
            if acc is None:
                return op("act", lambda e: e.activation(o, i, f, bias=bias, scale=scale), *after)
            return op("act", lambda e: e.activation(o, i, f, bias=bias, scale=scale, accum_out=acc), *after)

        def tt(o, a, b, f, *after, eng="dve"):
            return op(eng, lambda e: e.tensor_tensor(o, a, b, f), *after)

        def ts(o, a, s1, f1, s2, f2, *after, eng="dve"):
            if f2 is None:
                return op(eng, lambda e: e.tensor_scalar(o, a, s1, None, f1), *after)
            return op(eng, lambda e: e.tensor_scalar(o, a, s1, s2, f1, f2), *after)

        def stt(o, a, s, b, f1, f2, *after):
            return op("dve", lambda e: e.scalar_tensor_tensor(out=o, in0=a, scalar=s, in1=b, op0=f1, op1=f2), *after)

        def recip(o, a, *after):
            return op("dve", lambda e: e.reciprocal(o, a), *after)

        def copy(o, a, *after, eng="dve"):
            if eng == "act":
                return act(o, a, ACT.Copy, *after)
            return op(eng, lambda e: e.tensor_copy(o, a), *after)

        def memset(o, v, *after, eng="pool"):
            return op(eng, lambda e: e.memset(o, v), *after)

        def C(name):
            a, b = CST[name]
            return cst[:, a:b]

        def Pm(name, i=None):
            a, b = PAR[name]
            return par[:, a:b] if i is None else par[:, a + i:a + i + 1]

        at = [0, 0, AR]

        def take(*dims):
            n = 1
            for d in dims:
                n *= d
            a = at[0]
            at[0] += n
            assert at[0] <= at[2], at[0]
            v = arena[:, a:a + n]
            if len(dims) == 2:
                v = v.rearrange("p (a b) -> p a b", a=dims[0])
            if len(dims) == 3:
                v = v.rearrange("p (a b c) -> p a b c", a=dims[0], b=dims[1])
            return v

        def sm(n=1):
            a = at[1]
            at[1] += n
            assert at[1] <= 480
            return small[:, a:a + n]

        def barrier():
            return [[q for q in queue[e] if callable(q[0])][-1][2] for e in ("pe", "act", "dve", "pool") if queue[e]]

        banks = Rot([PS[:, i * 512:(i + 1) * 512] for i in range(8)])

        class Slot:
            def __init__(self, i, view):
                self.view, self.users, self.fills = view, [], 0
                self.sems = [ctx.enter_context(nc.semaphore(f"slot{w}_{i}")) for w in range(2)]

        fixed = [Slot(i, ring[:, i * SLOT:(i + 1) * SLOT]) for i in range(NS)]
        slots = list(fixed)
        turn = [0]

        class W:

            def __init__(self, src, n, per=4):
                k = src.shape[0] // 128
                self.per, self.slots = per, []
                for a in range(0, k, per):
                    m = min(per, k - a)
                    s = slots[turn[0] % len(slots)]
                    turn[0] += 1
                    s.fills += 1
                    v = s.view[:, 0:m * n].rearrange("p (k n) -> p k n", k=m)
                    d = dma("sp", v, src[a * 128:(a + m) * 128, :].rearrange("(k p) n -> p k n", p=128),
                            s.users, sem=s.sems[epoch[0]], val=16 * s.fills)
                    s.users = []
                    self.slots.append((v, d, s))

            def ap(self, k, a, b):
                return self.slots[k // self.per][0][:, k % self.per, a:b]

            def ready(self, k):
                return self.slots[k // self.per][1]

            def free(self, d):
                for _, _, s in self.slots:
                    s.users = [d]

        def group(o, w, a, b, rhs, K, *after):
            for k in range(K):
                d = mm(o, w.ap(k, a, b), rhs(k), k == 0, k == K - 1, after if k == 0 else None, w.ready(k))
            return d

        def steps(parts):
            for one in parts:
                yield from one

        ctxT = take(8, 256)
        xv = xT[:, :].rearrange("p (k t) -> p k t", k=8)
        d_par = dma("act", par[:, :], I["par"])
        d_cst = dma("act", cst[:, :], I["cst"])
        d_ctx = dma("act", ctxT, I["ctxT"].rearrange("(k p) t -> p k t", p=128))
        d_x = dma("act", xv, I["xT"].rearrange("(k p) t -> p k t", p=128))
        eps = cst[:, CST["eps"][0]:CST["eps"][1]]
        ones = C("ones")

        def rms(src, K, n, D, rb, sq, *after):
            bk, free, users = banks.get()
            for k in range(K):
                s, sfree, suse = sq.get()
                q = act(s[:, 0:n], src(k), ACT.Square, after, sfree)
                d = mm(bk[:, 0:n], ones, s[:, 0:n], k == 0, k == K - 1, q, free if k == 0 else None, d_cst)
                suse.append(d)
            r = act(rb, bk[:, 0:n], ACT.Sqrt, d, scale=1.0 / D, bias=eps)
            users.append(r)
            return recip(rb, rb, r)

        e2 = sm(16)
        sc2 = sm(16)
        c2 = Pm("c2")
        d = act(e2, c2, ACT.Exp, d_par, scale=-1.0)
        d = ts(e2, e2, 1.0, ALU.add, None, None, d)
        d = recip(e2, e2, d)
        d_silu = tt(sc2, c2, e2, ALU.mult, d)
        c2v = sc2.rearrange("p (k v) -> p k v", v=2)
        mods = sm(96).rearrange("p (j v) -> p j v", v=2)
        d_mod = {}

        rowb = Rot([take(512) for _ in range(2)])

        def modulation(m, rots=None):
            col_rot, row_rot = rots or (banks, banks)
            bk, free, users = col_rot.get()
            for c in range(2):
                w = W(I["w_ada"][:, m * 1024 + c * 512:m * 1024 + (c + 1) * 512], 512)
                rk_, rfree, rusers = row_rot.get()
                for k in range(8):
                    d = mm(rk_[0:2, :], c2v[:, k, :], w.ap(k, 0, 512), k == 0, k == 7, d_silu, rfree, w.ready(k))
                w.free(d)
                row, wfree, wuse = rowb.get()
                d = copy(row[0:2, :], rk_[0:2, :], d, wfree, eng="act")
                rusers.append(d)
                yield
                for j in range(4):
                    d = tr(bk[:, (c * 4 + j) * 2:(c * 4 + j) * 2 + 2], row[0:2, j * 128:(j + 1) * 128], d, free, d_cst)
                wuse.append(d)
                yield
            a, b = PAR["b_ada"]
            bias = par[:, a + m * 8:a + m * 8 + 8].unsqueeze(2).to_broadcast([128, 8, 2])
            d = tt(mods[:, m * 8:m * 8 + 8, :], bk[:, 0:16].rearrange("p (j v) -> p j v", v=2), bias, ALU.add, d)
            users.append(d)
            d_mod[m] = d

        sq = Rot([take(512) for _ in range(2)])
        rbs = take(2, 256)
        for _ in modulation(0):
            pass
        d_rb = [rms(lambda k: src[:, k, :], 8, 256, 1024, rbs[:, v, :], sq, dd)
                for v, src, dd in ((0, xv, d_x), (1, ctxT, d_ctx))]
        for _ in modulation(1):
            pass
        aw = sm(16).rearrange("p (j v) -> p j v", v=2)
        d = ts(aw, mods[:, 8:16, :], 1.0, ALU.add, None, None, d_mod[1])
        d_aw = tt(aw, aw, Pm("attn_w").unsqueeze(2).to_broadcast([128, 8, 2]), ALU.mult, d)

        hT = take(8, 512)
        d_h = []
        for v, src in ((0, xv), (1, ctxT)):
            t0 = 0 if v else 256
            r = d_rb[v]
            for k in range(8):
                d = stt(hT[:, k, t0:t0 + 256], src[:, k, :], aw[:, k, v:v + 1], rbs[:, v, :], ALU.mult, ALU.mult, r, d_aw)
                d = ts(hT[:, k, t0:t0 + 256], hT[:, k, t0:t0 + 256], mods[:, k, v:v + 1], ALU.add, None, None, d, d_mod[0])
            d_h.append(d)

        w_in = I["w_in"]
        raw = Rot([take(512) for _ in range(3)])

        def rope(bk, rows, n0, n, dst, d, users):
            s, sfree, suse = raw.get()
            c1 = copy(s[0:rows, 0:n], bk[0:rows, 0:n], d, sfree, eng="act")
            users.append(c1)
            b2, free2, users2 = banks.get()
            m = mm(b2[0:rows, 0:256], C("rot")[0:rows, 0:rows], s[0:rows, n0:n], True, True, c1, free2)
            a1 = tt(dst[0:rows, n0:n], s[0:rows, n0:n], C("cos")[0:rows, :], ALU.mult, c1)
            s2, s2free, s2use = raw.get()
            a2 = tt(s2[0:rows, 0:256], b2[0:rows, 0:256], C("sin")[0:rows, :], ALU.mult, m, s2free)
            users2.append(a2)
            a3 = tt(dst[0:rows, n0:n], dst[0:rows, n0:n], s2[0:rows, 0:256], ALU.add, a1, a2)
            s2use.append(a3)
            suse.append([m, a1])
            if n0:
                c2 = copy(dst[0:rows, 0:n0], s[0:rows, 0:n0], c1, eng="act")
                suse.append(c2)
                return [a3, c2]
            return a3

        dq = take(4, 256)
        dk = take(4, 512)
        dv = take(4, 512)
        w = W(w_in[:, 0:512], 512)
        d_dq, d_dk, d_dv = [], [], []
        for j in range(4):
            bk, free, users = banks.get()
            d = group(bk[:, 0:256], w, j * 128, (j + 1) * 128, lambda k: hT[:, k, 256:512], 8, d_h[0], free)
            d_dq.append(rope(bk, 128, 0, 256, dq[:, j, :], d, users))
        w.free(d)
        w = W(w_in[:, 512:1024], 512)
        for j in range(4):
            bk, free, users = banks.get()
            d = group(bk, w, j * 128, (j + 1) * 128, lambda k: hT[:, k, :], 8, d_h, free)
            d_dk.append(rope(bk, 128, 256, 512, dk[:, j, :], d, users))
        w.free(d)
        w = W(w_in[:, 1024:1536], 512)
        for t in range(4):
            bk, free, users = banks.get()
            for k in range(8):
                d = mm(bk, hT[:, k, t * 128:(t + 1) * 128], w.ap(k, 0, 512), k == 0, k == 7, free, w.ready(k))
            d_dv.append(copy(dv[:, t, :], bk, d, eng="act"))
            users.append(d_dv[-1])
        w.free(d)
        cq = take(2, 256)
        ckv = take(512)
        kr = take(512)
        w = W(w_in[:, 1536:1984], 448)
        d_cq = []
        for j in range(2):
            bk, free, users = banks.get()
            d = group(bk[:, 0:256], w, j * 128, (j + 1) * 128, lambda k: hT[:, k, 256:512], 8, free)
            d_cq.append(copy(cq[:, j, :], bk[:, 0:256], d))
            users.append(d_cq[-1])
        bk, free, users = banks.get()
        d = group(bk, w, 256, 384, lambda k: hT[:, k, :], 8, free)
        d_ckv = copy(ckv, bk, d)
        users.append(d_ckv)
        bk, free, users = banks.get()
        d = group(bk[0:64, :], w, 384, 448, lambda k: hT[:, k, :], 8, free)
        w.free(d)
        d_spent = [d, d_h]
        d_kr = rope(bk, 64, 256, 512, kr, d, users)

        rq = take(256)
        rk = take(512)
        r = rms(lambda k: cq[:, k, :], 2, 256, 256, rq, sq, d_cq)
        for j in range(2):
            d_cqn = stt(cq[:, j, :], cq[:, j, :], Pm("qn_w", j), rq, ALU.mult, ALU.mult, r)
        r = rms(lambda k: ckv, 1, 512, 128, rk, sq, d_ckv)
        d_ckvn = stt(ckv, ckv, Pm("kvn_w"), rk, ALU.mult, ALU.mult, r)
        wq = W(I["w_uq"], 768, per=2)
        qn = take(4, 256)
        qr = take(4, 256)
        d_qn, d_qr = [], []
        for h in range(4):
            bk, free, users = banks.get()
            d = group(bk[:, 0:256], wq, h * 192, h * 192 + 128, lambda k: cq[:, k, :], 2, free, d_cqn)
            d_qn.append(copy(qn[:, h, :], bk[:, 0:256], d, eng="act"))
            users.append(d_qn[-1])
            bk, free, users = banks.get()
            d = group(bk[0:64, 0:256], wq, h * 192 + 128, h * 192 + 192, lambda k: cq[:, k, :], 2, free)
            d_qr.append(rope(bk, 64, 0, 256, qr[:, h, :], d, users))
        wq.free(d)
        wk = W(I["w_ukv"], 1024, per=1)
        kn = take(4, 512)
        mv = take(4, 512)
        d_kn, d_mv = [], []
        for h in range(4):
            bk, free, users = banks.get()
            d = mm(bk, wk.ap(0, h * 256, h * 256 + 128), ckv, True, True, free, d_ckvn, wk.ready(0))
            d_kn.append(copy(kn[:, h, :], bk, d, eng="act"))
            users.append(d_kn[-1])
        wv = wk.ap(0, 0, 1024).rearrange("p (h c) -> p h c", h=4)[:, :, 128:256]
        for t in range(4):
            bk, free, users = banks.get()
            d = mm(bk.rearrange("p (h c) -> p h c", h=4), ckv[:, t * 128:(t + 1) * 128], wv, True, True, free)
            d_mv.append(copy(mv[:, t, :], bk, d))
            users.append(d_mv[-1])
        wk.free(d)

        lp = sm(2)
        lam4 = Pm("lam")
        d = tt(lp[0:64, :], lam4[0:64, 0:2], lam4[0:64, 2:4], ALU.mult, d_par)
        bk, free, users = banks.get()
        d = mm(bk[:, 0:2], ones[0:64, :], lp[0:64, :], True, True, d, free)
        le = sm(2)
        d = act(le, bk[:, 0:2], ACT.Exp, d)
        users.append(d)
        nlam = sm()
        d = tt(nlam, le[:, 1:2], le[:, 0:1], ALU.subtract, d)
        lam_init = 0.8 - 0.6 * 1.0
        d_lam = ts(nlam, nlam, -lam_init, ALU.add, None, None, d)

        flat_h = hT.rearrange("p a b -> p (a b)")
        flat_c = ctxT.rearrange("p a b -> p (a b)")
        Pb = Rot([flat_h[:, i * 512:(i + 1) * 512] for i in range(8)])
        PT = Rot([flat_c[:, i * 512:(i + 1) * 512] for i in range(4)])
        for u in Pb.users + PT.users:
            u.extend(d_spent)
        rqr = Rot([take(256) for _ in range(2)])
        mix = take(8, 256)

        def split(rot, n):
            two = Rot(rot.aps[:n]), Rot(rot.aps[n:])
            two[0].users, two[1].users = rot.users[:n], rot.users[n:]
            return two

        banks, mod_banks = split(banks, 6)
        mod_rots = split(mod_banks, 1)

        def softmax(bk, n, scale, d, users):
            mx, den = sm(), sm()
            d1 = op("dve", lambda e: e.tensor_reduce(mx, bk[:, 0:n], AX_X, ALU.max), d)
            d1 = ts(mx, mx, -scale, ALU.mult, None, None, d1)
            p, pfree, puse = Pb.get()
            d2 = act(p[:, 0:n], bk[:, 0:n], ACT.Exp, d1, pfree, scale=scale, bias=mx, acc=den)
            users.append(d2)
            d3 = recip(den, den, d2)
            return p, den, [d2, d3], puse

        def attend(h, t, V, dV, scores):
            p, d, puse = scores(h, t)
            yield
            bk, free, users = banks.get()
            for b in range(4):
                m = tr(bk[:, b * 128:(b + 1) * 128], p[:, b * 128:(b + 1) * 128], d, free)
            puse.append(m)
            pt, tfree, tuse = PT.get()
            c = copy(pt, bk, m, tfree, eng="act")
            users.append(c)
            yield
            bk, free, users = banks.get()
            for b in range(4):
                m = mm(bk[:, 0:128], V[:, b, (h % 4) * 128:(h % 4) * 128 + 128], pt[:, b * 128:(b + 1) * 128],
                       b == 0, b == 3, c, dV, free)
            tuse.append(m)
            d = copy(mix[:, h, t * 128:(t + 1) * 128], bk[:, 0:128], m)
            users.append(d)
            d_mix[h].append(d)
            if h < 4 and t:
                rq_, rfree, ruse = rqr.get()
                r = rms(lambda k: mix[:, h, :], 1, 256, 128, rq_, sq, d_mix[h], rfree)
                d = stt(mix[:, h, :], mix[:, h, :], subw, rq_, ALU.mult, ALU.mult, r, d_subw)
                ruse.append(d)
                d_mix[h].append(d)
            yield

        def diff_scores(h, t):
            ps = []
            for c in range(2):
                bk, free, users = banks.get()
                rows = slice(c * 64, c * 64 + 64)
                d = mm(bk, dq[rows, h, t * 128:(t + 1) * 128], dk[rows, h, :], True, True, free, d_dq[h], d_dk[h])
                ps.append(softmax(bk, 512, 0.125, d, users))
            (p0, r0, e0, u0), (p1, r1, e1, u1) = ps
            d = tt(r1, r1, nlam, ALU.mult, e1, d_lam)
            d = ts(p1, p1, r1, ALU.mult, None, None, d)
            d = stt(p0, p0, r0, p1, ALU.mult, ALU.add, d, e0)
            u1.append(d)
            return p0, d, u0

        def mla_scores(h, t):
            h = h - 4
            bk, free, users = banks.get()
            mm(bk, qn[:, h, t * 128:(t + 1) * 128], kn[:, h, :], True, False, free, d_qn[h], d_kn[h])
            d = mm(bk, qr[0:64, h, t * 128:(t + 1) * 128], kr[0:64, :], False, True, d_qr[h], d_kr)
            p, r, e, u = softmax(bk, 512, 192 ** -0.5, d, users)
            return p, ts(p, p, r, ALU.mult, None, None, e), u

        subw = sm()
        d_subw = ts(subw, Pm("sub_w"), 1.0 - lam_init, ALU.mult, None, None)
        d_mix = [[] for _ in range(8)]
        side = steps(modulation(m, mod_rots) for m in (2, 3, 4, 5))
        quads = [[attend(h, t, dv, d_dv, diff_scores) for h in (a, a + 1) for t in range(2)] for a in (0, 2)]
        quads += [[attend(h, t, mv, d_mv, mla_scores) for h in (a, a + 1) for t in range(2)] for a in (4, 6)]
        for u in quads[0]:
            next(u)
            next(side, None)
        for i, quad in enumerate(quads):
            for u in quad:
                next(u)
                next(side, None)
            ahead = quads[i + 1] if i + 1 < 4 else [None] * 4
            for u, v in zip(quad, ahead):
                if v:
                    next(v)
                    next(side, None)
                next(u)
                next(side, None)

        d_x1 = []
        for c in range(2):
            w = W(I["w_out"][:, c * 512:(c + 1) * 512], 512)
            for j in range(4):
                f = c * 4 + j
                bk, free, users = banks.get()
                d = group(bk[:, 0:256], w, j * 128, (j + 1) * 128, lambda k: mix[:, k, :], 8, free, d_mix)
                if j == 3:
                    w.free(d)
                d = stt(xv[:, f, :], bk[:, 0:256], mods[:, 16 + f, 0:1], xv[:, f, :], ALU.mult, ALU.add, d, d_mod[2])
                users.append(d)
                d_x1.append(d)
        for _ in side:
            pass
        both = Rot(banks.aps + mod_banks.aps)
        both.users = banks.users + mod_rots[0].users + mod_rots[1].users
        banks = both

        fw = sm(8)
        d = ts(fw, mods[:, 32:40, 0], 1.0, ALU.add, None, None, d_mod[4])
        d_fw = tt(fw, fw, Pm("ffn_w"), ALU.mult, d)
        done = barrier()
        at[0] = 0
        sq = Rot([take(512) for _ in range(2)])
        rbrow = take(32)
        hf = take(8, 256)
        rf = take(256)
        d_rb = dma("act", rbrow[0:1, :], I["router_b"], done)
        r = rms(lambda k: xv[:, k, :], 8, 256, 1024, rf, sq, d_x1, done)
        for k in range(8):
            d = stt(hf[:, k, :], xv[:, k, :], fw[:, k:k + 1], rf, ALU.mult, ALU.mult, r, d_fw)
            d_hf = ts(hf[:, k, :], hf[:, k, :], mods[:, 24 + k, 0:1], ALU.add, None, None, d, d_mod[3])
        w_router = W(I["router_w"], 32, per=8)
        hm = [take(1024) for _ in range(2)]
        d_hm = []
        for t in range(2):
            for c in range(2):
                bk, free, users = banks.get()
                for j in range(4):
                    m = tr(bk[:, j * 128:(j + 1) * 128], hf[:, c * 4 + j, t * 128:(t + 1) * 128], free, d_hf)
                d = copy(hm[t][:, c * 512:(c + 1) * 512], bk, m, eng="act")
                users.append(d)
                d_hm.append(d)

        w = w_router
        gT = take(256)
        route, d_mask, d_gate = [], [], []
        for t in range(2):
            bk, free, users = banks.get()
            mm(bk[:, 0:32], ones[0:1, :], rbrow[0:1, :], True, False, free, d_rb)
            for k in range(8):
                d = mm(bk[:, 0:32], hf[:, k, t * 128:(t + 1) * 128], w.ap(k, 0, 32), False, k == 7, d_hf, w.ready(k))
            lg, rp, m8, m4 = take(40), take(40), sm(8), sm(8)
            route.append((lg, rp))
            da = copy(lg[:, 0:32], bk[:, 0:32], d)
            users.append(da)
            db = memset(lg[:, 32:40], -3.0e38, eng="dve")
            dc = memset(m4, -3.0e38, eng="dve")
            d = op("dve", lambda e, m8=m8, lg=lg: e.max(m8, lg[:, 0:32]), da)
            d = copy(m4[:, 0:4], m8[:, 0:4], d, dc)
            d = op("dve", lambda e, rp=rp, m4=m4, lg=lg: e.match_replace(rp, m4, lg, 3.0e38), d, da, db)
            d = tt(rp[:, 0:32], rp[:, 0:32], lg[:, 0:32], ALU.not_equal, d)
            d_mask.append(d)
            nm, den = sm(), sm()
            d1 = ts(nm, m8[:, 0:1], -1.0, ALU.mult, None, None)
            d1 = act(lg[:, 0:32], lg[:, 0:32], ACT.Exp, d1, d, bias=nm)
            d = tt(lg[:, 0:32], lg[:, 0:32], rp[:, 0:32], ALU.mult, d1, d)
            d = op("dve", lambda e, den=den, lg=lg: e.tensor_reduce(den, lg[:, 0:32], AX_X, ALU.add), d)
            d = recip(den, den, d)
            d = ts(lg[:, 0:32], lg[:, 0:32], den, ALU.mult, None, None, d)
            d_gate.append(d)
            bk, free, users = banks.get()
            d = tr(bk[0:32, 0:128], lg[:, 0:32], d, free)
            d_gT = copy(gT[0:32, t * 128:(t + 1) * 128], bk[0:32, 0:128], d)
            users.append(d_gT)
        w.free(queue["pe"][-1][2])

        posm, gts = [take(32) for _ in range(2)], [g for g, _ in route]
        cnt = take(32)
        mxf = take(1)
        d_pos = []
        bk, free, users = banks.get()
        nx = NX
        at[1 + 1] = AR - nx * SLOT
        base = turn[0] % NS
        slots[:] = slots[base:] + slots[:base]
        turn[0] = 0
        for i in range(nx):
            sl = Slot(NS + i, arena[:, AR - (i + 1) * SLOT:AR - i * SLOT])
            sl.users = list(done)
            slots.insert(0, sl)
        for t in range(2):
            for u in range(t):
                mm(bk[:, 0:32], ones, route[u][1][:, 0:32], True, False, d_mask, free)
            m = mm(bk[:, 0:32], C("before"), route[t][1][:, 0:32], t == 0, True, d_mask, free)
            d = stt(posm[t], bk[:, 0:32], 1.0, route[t][1][:, 0:32], ALU.add, ALU.mult, m)
            d_pos.append(ts(posm[t], posm[t], -1.0, ALU.add, None, None, d))
            users.append(d)
            free = [free, d]
        mm(bk[:, 32:64], ones, route[0][1][:, 0:32], True, False, free)
        m = mm(bk[:, 32:64], ones, route[1][1][:, 0:32], False, True)
        bk_cnt = bk[:, 32:64]
        d = op("dve", lambda e: e.tensor_reduce(mxf, bk_cnt, AX_X, ALU.max), m)
        users.append(d)
        d_max = copy(most[:, 0:1], mxf, d)

        bfree = []
        for i in range(8):
            _, f, _ = banks.get()
            bfree.append(f)
        yb = [PS[:, i * 512:(i + 1) * 512] for i in range(4)]
        hb = Rot([PS[:, i * 512:(i + 1) * 512] for i in range(4, 8)])
        for f in hb.users:
            f.extend(bfree)
        b2s = take(1024)
        d_b2 = dma("act", b2s[0:32, :], I["b2"], done)
        for j in range(8):
            d_y = mm(yb[j // 2][:, (j % 2) * 256:(j % 2) * 256 + 256], b2s[0:32, j * 128:(j + 1) * 128], gT[0:32, :],
                     j % 2 == 0, False, bfree, d_b2, d_gT)
        sel = Rot([take(2, S) for _ in range(2)])
        selg = Rot([take(2, S) for _ in range(2)])
        xs_ = Rot([take(8, S) for _ in range(2)])
        pgt = Rot([take(256) for _ in range(3)])
        acts = Rot([take(8, S) for _ in range(2)])
        ysr = Rot([take(1024) for _ in range(2)])
        tg = Rot([take(2, S) for _ in range(3)])
        tu = Rot([take(2, S) for _ in range(3)])
        tsg = Rot([take(2, S) for _ in range(3)])
        b1a = PAR["b1"][0]

        def select(ex, p):
            P_, pf, pu_ = sel.get()
            Q_, qf, qu = selg.get()
            dp = []
            for t in range(2):
                io = C("iota")[:, p * S:(p + 1) * S]
                dp.append(ts(P_[:, t, :], io, posm[t][:, ex:ex + 1], ALU.is_equal, None, None, pf, d_pos, d_cst))
                dp.append(ts(Q_[:, t, :], io, posm[t][:, ex:ex + 1], ALU.is_equal, gts[t][:, ex:ex + 1], ALU.mult,
                             qf, d_gate))
            return P_, Q_, dp, pu_, qu

        def gather(P_, Q_, dp, pu_, qu):
            X, xf, xu = xs_.get()
            G, gf_, gu = pgt.get()
            dx, dg = [], []
            for c in range(2):
                bk, free, users = hb.get()
                for j in range(4):
                    for t in range(2):
                        f = (c * 4 + j) * 128
                        m = mm(bk[:, j * S:(j + 1) * S], hm[t][:, f:f + 128], P_[:, t, :], t == 0, t == 1, dp, free, d_hm)
                d1 = copy(X[:, c * 4:c * 4 + 4, :], bk[:, 0:4 * S].rearrange("p (a b) -> p a b", a=4), m, xf, eng="act")
                users.append(d1)
                dx.append(d1)
            bk, free, users = hb.get()
            for c in range(2):
                m = tr(bk[:, c * 128:(c + 1) * 128], Q_[:, c, :], dp, free)
            d2 = copy(G, bk[:, 0:256], m, gf_, eng="act")
            users.append(d2)
            dg.append(d2)
            pu_.append(m)
            qu.append(m)
            return X, dx, xu, G, dg, gu

        def up(ex, c, gat, A, dA, af):
            X, dx, xu = gat[:3]
            wg = W(I["w1"][ex, :, c * 512:(c + 1) * 512], 512)
            wu = W(I["w1"][ex, :, 1024 + c * 512:1024 + (c + 1) * 512], 512)
            for j in range(0, 4, 2):
                bk, free, users = hb.get()
                for q in range(2):
                    group(bk[:, q * S:(q + 1) * S], wg, (j + q) * 128, (j + q + 1) * 128, lambda k: X[:, k, :], 8, free, dx)
                    m = group(bk[:, (2 + q) * S:(3 + q) * S], wu, (j + q) * 128, (j + q + 1) * 128,
                              lambda k: X[:, k, :], 8)
                g1, f1, u1 = tg.get()
                uu, f2, u2 = tu.get()
                sg, f3, u3 = tsg.get()
                dg, du = [], []
                for q in range(2):
                    b = b1a + ex * 16 + c * 4 + j + q
                    dg.append(ts(g1[:, q, :], bk[:, q * S:(q + 1) * S], par[:, b:b + 1], ALU.add, 7.0, ALU.min, m, f1))
                for q in range(2):
                    b = b1a + ex * 16 + 8 + c * 4 + j + q
                    du.append(ts(uu[:, q, :], bk[:, (2 + q) * S:(3 + q) * S], par[:, b:b + 1], ALU.add, 7.0, ALU.min, m, f2))
                users.append(du)
                ds = act(sg, g1, ACT.Sigmoid, dg, f3, scale=1.702)
                du = ts(uu, uu, -7.0, ALU.max, 1.0, ALU.add, du)
                du = tt(uu, uu, g1, ALU.mult, du, dg)
                d = tt(A[:, c * 4 + j:c * 4 + j + 2, :], sg, uu, ALU.mult, ds, du, af)
                u1.append(du)
                u2.append(d)
                u3.append(d)
                dA.append(d)
            wg.free(m)
            wu.free(m)
            xu.append(m)

        def down(ex, A, dA, au):
            w = W(I["w2"][ex], 1024, per=2)
            bs = [hb.get() for _ in range(2)]
            for k in range(8):
                for c in range(2):
                    bk, free, users = bs[c]
                    m = mm(bk[0:S, :], A[:, k, :], w.ap(k, c * 512, (c + 1) * 512), k == 0, k == 7, free,
                           dA[k // 2], w.ready(k))
            w.free(m)
            au.append(m)
            Y, yf, yu = ysr.get()
            ds = []
            for c in range(2):
                bk, free, users = bs[c]
                d = copy(Y[0:S, c * 512:(c + 1) * 512], bk[0:S, :], m, yf, eng="act" if c else "dve")
                users.append(d)
                ds.append(d)
            return Y, ds, yu

        def scatter(Y, ds, yu, gat):
            G, dg, gu = gat[3:]
            for j in range(8):
                m = mm(yb[j // 2][:, (j % 2) * 256:(j % 2) * 256 + 256], Y[0:S, j * 128:(j + 1) * 128], G[0:S, :],
                       False, False, ds, dg)
            yu.append(m)
            gu.append(m)
            return m

        def all_experts(p):
            gat = gather(*select(0, p))
            prev = None
            for ex in range(NE):
                A, af, au = acts.get()
                dA = []
                picks = select(ex + 1, p) if ex + 1 < NE else None
                up(ex, 0, gat, A, dA, af)
                nxt = gather(*picks) if picks else None
                if p == 0:
                    next(side, None)
                    next(side, None)
                if prev:
                    y = down(*prev[0])
                up(ex, 1, gat, A, dA, af)
                if prev:
                    scatter(*y, prev[1])
                prev = ((ex, A, dA, au), gat)
                gat = nxt
            y = down(*prev[0])
            return scatter(*y, prev[1])

        tabm = take(12, 128)
        tabr = take(12)
        d = memset(tabr[32:64, :], 1.0, done, eng="pool")
        d0 = dma("act", tabr[0:32, :], I["rel_bias"], done)
        d_tabm = op("pool", lambda e: e.tensor_copy(tabm[0:33, :, :], tabr[0:33, :].unsqueeze(2).to_broadcast([33, 12, 128])), d, d0)
        d_skw = []
        tb = Rot([take(384) for _ in range(2)])
        hot = take(1152)
        d_hot = dma("act", hot[0:33, :], I["hot"], done)

        def bias_rows():
            for h in range(12):
                g = h // 4
                bk, free, users = hb.get()
                m = mm(bk[:, 0:384], tabm[0:33, h, :], hot[0:33, g * 384:(g + 1) * 384], True, True, d_tabm, free, d_hot)
                t, tfree, tuse = tb.get()
                c = copy(t, bk[:, 0:384], m, tfree, eng="act")
                users.append(c)
                s = dma("act", skew[h, :, :], t, c)
                tuse.append(s)
                d_skw.append(s)
                yield

        are, aim = Pm("s5_are"), Pm("s5_aim")
        rr, cfr, cfi = sm(16), sm(16), sm(16)
        d_tabs = []

        def phases():
            dt, th, kk, wc, wsn, lbr, lbi, dn, t1, t2, t3, t4, t5 = [take(16) for _ in range(13)]
            are, aim = Pm("s5_are"), Pm("s5_aim")
            d = act(dt, Pm("s5_ldt"), ACT.Exp, done)
            d = tt(th, aim, dt, ALU.mult, d)
            e1 = tt(t1, are, dt, ALU.mult, d)
            yield
            d_r = act(rr, t1, ACT.Exp, e1)
            two_pi = 6.283185307179586
            d = ts(kk, th, 1.0 / two_pi, ALU.mult, 12582912.0, ALU.add, d)
            d = ts(kk, kk, -12582912.0, ALU.add, None, None, d)
            yield
            for part in (6.28125, 0.0019350051879882812, 3.0199159819567e-07):
                d = stt(th, kk, -part, th, ALU.mult, ALU.add, d)
            d = ts(th, th, 3.1415925, ALU.min, -3.1415925, ALU.max, d)
            d_s = act(wsn, th, ACT.Sin, d)
            d = act(t2, th, ACT.Abs, d)
            yield
            d = ts(t2, t2, -1.0, ALU.mult, 1.5707963267948966, ALU.add, d)
            d_c = act(wc, t2, ACT.Sin, d)
            d = tt(lbr, rr, wc, ALU.mult, d_c, d_r)
            yield
            da = ts(lbr, lbr, -1.0, ALU.add, None, None, d)
            db = tt(lbi, rr, wsn, ALU.mult, d_s, d_r)
            d = tt(dn, are, are, ALU.mult)
            yield
            d1 = tt(t3, aim, aim, ALU.mult)
            d = tt(dn, dn, t3, ALU.add, d, d1)
            d = recip(dn, dn, d)
            yield
            d1 = tt(t4, lbr, are, ALU.mult, da)
            d2 = tt(t5, lbi, aim, ALU.mult, db)
            d3 = tt(t4, t4, t5, ALU.add, d1, d2)
            yield
            dr_ = tt(cfr, t4, dn, ALU.mult, d3, d)
            d1 = tt(t4, lbi, are, ALU.mult, dr_)
            d2 = tt(t5, lbr, aim, ALU.mult, d3)
            yield
            d3 = tt(t4, t4, t5, ALU.subtract, d1, d2)
            di_ = tt(cfi, t4, dn, ALU.mult, d3)
            pc = [wc] + [take(16) for _ in range(7)]
            psn = [wsn] + [take(16) for _ in range(7)]
            d = [d_c, d_s]
            for k in range(7):
                a = tt(pc[k + 1], pc[k], pc[k], ALU.mult, d)
                b = tt(t1, psn[k], psn[k], ALU.mult, d, e1, d_r)
                a = tt(pc[k + 1], pc[k + 1], t1, ALU.subtract, a, b)
                b = tt(psn[k + 1], pc[k], psn[k], ALU.mult, d)
                b = ts(psn[k + 1], psn[k + 1], 2.0, ALU.mult, None, None, b)
                e1 = a
                d = [a, b]
                yield
            d_pw = d
            Cw, Sw, tw = take(4, 256), take(4, 256), take(4, 256)
            d_keep = None
            for q in range(4):
                a = memset(Cw[:, :, 0:1], 1.0, d_keep)
                b = memset(Sw[:, :, 0:1], 0.0, d_keep)
                d = [a, b]
                yield
                for k in range(8):
                    n = 1 << k

                    def bc(x):
                        return x[:, q * 4:q * 4 + 4].unsqueeze(2).to_broadcast([128, 4, n])
                    o = slice(n, 2 * n)
                    p = slice(0, n)
                    x1 = tt(Cw[:, :, o], Cw[:, :, p], bc(pc[k]), ALU.mult, d, d_pw, eng="pool")
                    x2 = tt(tw[:, :, p], Sw[:, :, p], bc(psn[k]), ALU.mult, d, eng="pool")
                    x3 = tt(Cw[:, :, o], Cw[:, :, o], tw[:, :, p], ALU.subtract, x1, x2, eng="pool")
                    x1 = tt(Sw[:, :, o], Sw[:, :, p], bc(pc[k]), ALU.mult, d, eng="pool")
                    x2 = tt(tw[:, :, p], Cw[:, :, p], bc(psn[k]), ALU.mult, d, x3, eng="pool")
                    x4 = tt(Sw[:, :, o], Sw[:, :, o], tw[:, :, p], ALU.add, x1, x2, eng="pool")
                    d = [x3, x4]
                d_keep = [dma("pool", tabs[q, 0].rearrange("p (a b) -> p a b", a=4), Cw, d),
                          dma("pool", tabs[q, 1].rearrange("p (a b) -> p a b", a=4), Sw, d)]
                d_tabs.append(d_keep)
                yield


        side = steps([bias_rows(), phases()])

        all_experts(0)
        for _ in side:
            pass
        d_max.asked = True
        for p in range(1, 2):
            for e in queue:
                queue[e].append(("if", [d_max], p * S))
            all_experts(p)
        for p in range(1, 2):
            for e in queue:
                queue[e].append(("end", [], None))

        epoch[0] = 1
        fence = sm(4)
        f_dve = memset(fence[:, 0:1], 0.0, eng="dve")
        f_act = act(fence[:, 1:2], eps, ACT.Copy)
        f_pool = memset(fence[:, 2:3], 0.0, eng="pool")
        f_pe = mm(hb.aps[0][:, 0:1], ones, cst[:, 0:1], True, True, f_dve, f_act, f_pool)
        done = [f_dve, f_act, f_pool, f_pe, d_skw, d_tabs]
        slots[:] = fixed[:6]
        turn[0] = 0
        for sl in fixed:
            sl.users, sl.fills = [f_pe], 0
        d_xm = []
        for j in range(8):
            d_xm.append(stt(xv[:, j, :], yb[j // 2][:, (j % 2) * 256:(j % 2) * 256 + 256], mods[:, 40 + j, 0:1],
                            xv[:, j, :], ALU.mult, ALU.add, f_pe))
        at[2] = AR
        banks = Rot([PS[:, i * 512:(i + 1) * 512] for i in range(8)])
        banks.users = [[d_xm[-1], f_pe] for _ in range(8)]
        at[0] = 0
        sq = Rot([take(256) for _ in range(2)])
        rf = take(256)
        xn = take(8, 256)

        def norm_to(dst, wname, *after):
            r = rms(lambda k: xv[:, k, :], 8, 256, 1024, rf, sq, *after)
            for k in range(8):
                d = stt(dst[:, k, :], xv[:, k, :], Pm(wname, k), rf, ALU.mult, ALU.mult, r)
            return d

        d = norm_to(xv, "fin_w", d_xm, done)
        d_xn = norm_to(xn, "attn2_w", d)

        whole = banks
        start = [d_xn, f_pe, d_skw, d_tabs]

        def part(a, b):
            r = Rot([PS[:, i * 512:(i + 1) * 512] for i in range(a, b)])
            r.users = [list(whole.users[i]) for i in range(a, b)]
            return r

        fb, ab, s5b, s5o = part(0, 2), part(2, 5), part(5, 7), part(7, 8)
        w2i = I["w_in_2"]
        us = take(4, 256)
        sbq, sbk, sbv = take(4, 256), take(4, 256), take(2, 512)
        dlq, dlk, dlv = take(6, 256), take(6, 256), take(2, 768)
        pu = take(4, 256)
        Tr = Rot([take(3, 256) for _ in range(2)])
        ysT, ysb, ydl, ypl = take(4, 256), take(4, 256), take(2, 256), take(4, 256)
        Ct, St = take(4, 256), take(4, 256)
        bt, cc = take(2, 512), take(2, 512)
        scr = take(2048)
        Pb = Rot([take(768) for _ in range(2)])
        PT = Rot([take(768) for _ in range(2)])
        mgf = take(2048)
        mg = mgf.rearrange("p (k t) -> p k t", k=8)
        gs = Rot([take(256) for _ in range(3)])
        gst = [ring[:, (6 + i) * SLOT:(7 + i) * SLOT].rearrange("p (k t) -> p k t", k=8) for i in range(2)]

        def projT(c0, ntile, dst, ds):
            for j in range(0, ntile, 4):
                m = min(4, ntile - j)
                w = W(w2i[:, c0 + j * 128:c0 + (j + m) * 128], m * 128)
                for i in range(0, m, 2):
                    bk, free, users = fb.get()
                    for q in range(2):
                        d = group(bk[:, q * 256:(q + 1) * 256], w, (i + q) * 128, (i + q + 1) * 128,
                                  lambda k: xn[:, k, :], 8, free, d_xn)
                    if i + 2 >= m:
                        w.free(d)
                    c = copy(dst[:, j + i:j + i + 2, :], bk.rearrange("p (a b) -> p a b", a=2), d, eng="act")
                    users.append(c)
                    ds += [c, c]
                    yield

        def projV(c0, n, dst, ds):
            for j in range(0, n, 512):
                m = min(512, n - j)
                w = W(w2i[:, c0 + j:c0 + j + m], m)
                for t in range(2):
                    bk, free, users = fb.get()
                    for k in range(8):
                        d = mm(bk[:, 0:m], xn[:, k, t * 128:(t + 1) * 128], w.ap(k, 0, m), k == 0, k == 7,
                               free, d_xn, w.ready(k))
                    if t:
                        w.free(d)
                    c = copy(dst[:, t, j:j + m], bk[:, 0:m], d, eng="act")
                    users.append(c)
                    ds.append(c)
                    yield

        d_us, d_sq, d_sk, d_sv, d_lq, d_lk, d_lv, d_pu = [[] for _ in range(8)]
        d_pl, d_gst, d_mg = [], [[None] * 8, [None] * 8], [None] * 8

        def gates(bi, G, dG):
            for c in range(2):
                wg = W(I["w_gate"][bi, :, c * 512:(c + 1) * 512], 512)
                for j in range(4):
                    f = c * 4 + j
                    bk, free, users = fb.get()
                    m = group(bk[:, 0:256], wg, j * 128, (j + 1) * 128, lambda k: xn[:, k, :], 8, free)
                    if j == 3:
                        wg.free(m)
                    d = act(G[:, f, :], bk[:, 0:256], ACT.Sigmoid, m, start)
                    users.append(d)
                    dG[f] = d
                    yield

        def branch(bi, row, K, yt, dy):
            for c in range(2):
                wg = W(I["w_gate"][bi, :, c * 512:(c + 1) * 512], 512)
                wb = W(I["w_branch"][row:row + K * 128, c * 512:(c + 1) * 512], 512)
                for j in range(4):
                    f = c * 4 + j
                    bk, free, users = fb.get()
                    group(bk[:, 0:256], wg, j * 128, (j + 1) * 128, lambda k: xn[:, k, :], 8, free)
                    m = group(bk[:, 256:512], wb, j * 128, (j + 1) * 128, lambda k: yt[:, k, :], K, dy)
                    if j == 3:
                        wg.free(m)
                        wb.free(m)
                    s, sf, su = gs.get()
                    d = act(s, bk[:, 0:256], ACT.Sigmoid, m, sf)
                    if bi == 0:
                        d = tt(mg[:, f, :], bk[:, 256:512], s, ALU.mult, d, d_pl)
                        users.append(d)
                    else:
                        d = tt(s, bk[:, 256:512], s, ALU.mult, d)
                        users.append(d)
                        d = tt(mg[:, f, :], mg[:, f, :], s, ALU.add, d, d_mg[f])
                    su.append(d)
                    d_mg[f] = d
                    yield

        def kept_branch(G, dG, row, K, yt, dy):
            for c in range(2):
                wb = W(I["w_branch"][row:row + K * 128, c * 512:(c + 1) * 512], 512)
                for j in range(0, 4, 2):
                    f = c * 4 + j
                    bk, free, users = fb.get()
                    for q in range(2):
                        m = group(bk[:, q * 256:(q + 1) * 256], wb, (j + q) * 128, (j + q + 1) * 128,
                                  lambda k: yt[:, k, :], K, free, dy)
                    if j == 2:
                        wb.free(m)
                    g = G[:, f:f + 2, :]
                    d = tt(g, bk.rearrange("p (a b) -> p a b", a=2), g, ALU.mult, m, dG[f], dG[f + 1])
                    users.append(d)
                    d = tt(mg[:, f:f + 2, :], mg[:, f:f + 2, :], g, ALU.add, d, d_mg[f], d_mg[f + 1])
                    d_mg[f] = d_mg[f + 1] = d

        def pool_mixer():
            pa, pb = mgf[:, 0:1024].rearrange("p (a b) -> p a b", a=4), mgf[:, 1024:2048].rearrange("p (a b) -> p a b", a=4)
            src, d = pu, [d_pu, start]
            inv = C("inv").rearrange("p (a b) -> p a b", a=4)
            for i in range(4):
                n = 1 << i
                dst = pa if i % 2 == 0 else pb
                x1 = tt(dst[:, i:4, n:256], src[:, i:4, n:256], src[:, i:4, 0:256 - n], ALU.add, d, eng="pool")
                x2 = copy(dst[:, i:4, 0:n], src[:, i:4, 0:n], d, eng="pool")
                y = tt(ypl[:, i, :], dst[:, i, :], inv[:, i, :], ALU.mult, x1, x2, eng="pool")
                y = tt(ypl[:, i, :], ypl[:, i, :], pu[:, i, :], ALU.subtract, y, eng="pool")
                d = [x1, x2, y]
                src = dst
            return y

        def pool_product(y):
            w = W(I["pool_w"], 128)
            for i in range(4):
                bk, free, users = fb.get()
                m = mm(bk[:, 0:256], w.ap(i, 0, 128), ypl[:, i, :], True, True, free, y, w.ready(i))
                d = ts(ypl[:, i, :], bk[:, 0:256], Pm("pscale", i), ALU.mult, None, None, m)
                users.append(d)
                d_pl.append(d)
            w.free(m)

        def filler():
            yield from projT(512, 6, dlq, d_lq)
            yield from projT(1280, 6, dlk, d_lk)
            yield from projV(2048, 768, dlv, d_lv)
            yield from projT(0, 4, pu, d_pu)
            y = pool_mixer()
            yield from gates(2, gst[0], d_gst[0])
            pool_product(y)
            yield from branch(0, 0, 4, ypl, d_pl)
            yield from gates(1, gst[1], d_gst[1])

        d_sb, d_dl, d_s5y = [], [], []

        def stick(h):
            hc = slice(h * 128, h * 128 + 128)
            bk, free, users = ab.get()
            mm(bk[:, 0:256], sbk[:, h, 0:128], sbq[:, h, :], True, True, free, d_sq[h], d_sk[h])
            m = mm(bk[:, 256:384], sbk[:, h, 128:256], sbq[:, h, 128:256], True, True)
            ze, zf, zu = Pb.get()
            z, e_ = ze[:, 0:384], ze[:, 384:768]
            s, sf, su = PT.get()
            s = s[:, 0:384]
            dz = act(z, bk[:, 0:384], ACT.Copy, m, zf, start, scale=128 ** -0.5)
            users.append(dz)
            d = act(e_, z, ACT.Abs, dz)
            d = act(e_, e_, ACT.Exp, d, scale=-1.0)
            d = act(e_, e_, ACT.Ln, d, bias=1.0)
            d = stt(s, z, 0.0, e_, ALU.max, ALU.add, d, dz, sf, start)
            d = tt(s, s, C("m01"), ALU.mult, d)
            yield
            bk, free, users = ab.get()
            mm(bk[:, 0:256], C("tri"), s[:, 0:256], True, False, d, free)
            mm(bk[:, 128:256], ones, s[:, 256:384], False, True)
            m = mm(bk[:, 256:384], C("tri"), s[:, 256:384], True, True)
            d = tt(z, z, bk[:, 0:384], ALU.subtract, m)
            users.append(d)
            d = tt(z, z, C("mneg"), ALU.add, d)
            d = act(s, z, ACT.Exp, d)
            zu.append(d)
            yield
            bk, free, users = ab.get()
            assert len(d_sv) == 2
            mm(bk[:, 0:256], sbv[:, 0, hc], s[:, 0:256], True, False, d, free, d_sv)
            m = mm(bk[:, 128:256], sbv[:, 1, hc], s[:, 256:384], False, True)
            su.append(m)
            d = copy(ysb[:, h, :], bk[:, 0:256], m)
            users.append(d)
            d_sb.append(d)
            yield

        Tof = {}

        def bias_of(hs):
            T, tf, tu = Tr.get()
            d_T = []
            for g in range(3):
                base = skew[g * 4 + hs, :, :].rearrange("p n -> (p n)")[127:127 + 128 * 383]
                d_T.append(dma("pool", T[:, g, :], base.rearrange("(p n) -> p n", n=383)[:, 0:256], d_skw, tf, start))
            Tof[hs] = (T, d_T, tu)

        def dilated(hs, t):
            rows = slice((hs % 2) * 64, (hs % 2) * 64 + 64)
            T, d_T, tu = Tof[hs]
            assert len(d_lq) == 6 and len(d_lk) == 6
            nk = 128 * (t + 1)
            x, xf, xu = Pb.get()
            dd = []
            for g in range(3):
                h = g * 4 + hs
                bk, free, users = ab.get()
                m = mm(bk[:, 0:nk], dlq[rows, h // 2, t * 128:(t + 1) * 128], dlk[rows, h // 2, 0:nk], True, True,
                       free, d_lq[h // 2], d_lk[h // 2])
                d = stt(x[:, g * nk:(g + 1) * nk], bk[:, 0:nk], 0.125, T[:, g, 256 - nk:256], ALU.mult, ALU.add,
                        m, d_T, xf)
                users.append(d)
                dd.append(d)
            tu.append(d)
            mx, den = sm(), sm()
            xx = x[:, 0:3 * nk]
            d = op("dve", lambda e: e.tensor_reduce(mx, xx, AX_X, ALU.max), dd)
            d = ts(mx, mx, -1.0, ALU.mult, None, None, d)
            d = act(xx, xx, ACT.Exp, d, bias=mx, acc=den)
            d = recip(den, den, d)
            d = ts(xx, xx, den, ALU.mult, None, None, d)
            yield
            nb = 3 * (t + 1)
            pt, pf, pu_ = PT.get()
            for a in range(0, nb, 3):
                bk, free, users = ab.get()
                for b in range(3):
                    m = tr(bk[:, b * 128:(b + 1) * 128], x[:, (a + b) * 128:(a + b + 1) * 128], d, free)
                c = copy(pt[:, a * 128:(a + 3) * 128], bk[:, 0:384], m, pf, eng="act")
                users.append(c)
            xu.append(m)
            yield
            ob, ofree, ousers = ab.get()
            assert len(d_lv) == 4
            for b in range(nb):
                g, kb = b // (t + 1), b % (t + 1)
                h = g * 4 + hs
                m = mm(ob[rows, 0:128], dlv[:, kb, h * 64:(h + 1) * 64], pt[:, b * 128:(b + 1) * 128],
                       b == 0, b == nb - 1, c, d_lv, ofree)
            pu_.append(m)
            d = copy(ydl[rows, hs // 2, t * 128:(t + 1) * 128], ob[rows, 0:128], m)
            ousers.append(d)
            d_dl.append(d)
            yield

        def attention():
            def pairs(units):
                for a in range(0, len(units), 2):
                    one, two = units[a], units[a + 1]
                    for s in range(3):
                        next(one)
                        yield
                        next(two)
                        yield
            yield from pairs([stick(h) for h in range(4)])
            bias_of(0)
            for hs in range(4):
                if hs < 3:
                    bias_of(hs + 1)
                yield from pairs([dilated(hs, 0), dilated(hs, 1)])

        def recurrence():
            d_bt = [dma("pool", bt[:, v, :], I[n], start) for v, n in enumerate(("s5_bre", "s5_bim"))]
            ct = scr[:, 0:1024].rearrange("p (a b) -> p a b", a=2)
            ctmp = scr[:, 1024:1536]
            d_ct = [dma("pool", ct[:, v, :], I[n], start) for v, n in enumerate(("s5_cre", "s5_cim"))]
            d_tab = [dma("pool", x, tabs[0, v].rearrange("p (a b) -> p a b", a=4), d_tabs[0], start)
                     for v, x in enumerate((Ct, St))]

            def b32(x):
                return x.unsqueeze(2).to_broadcast([128, 16, 32])

            def v32(x):
                return x.rearrange("p (a b) -> p a b", b=32)

            d1 = tt(v32(cc[:, 0, :]), v32(ct[:, 0, :]), b32(cfr), ALU.mult, d_ct)
            d2 = tt(v32(ctmp), v32(ct[:, 1, :]), b32(cfi), ALU.mult)
            d_c0 = tt(cc[:, 0, :], cc[:, 0, :], ctmp, ALU.subtract, d1, d2)
            d1 = tt(v32(cc[:, 1, :]), v32(ct[:, 0, :]), b32(cfi), ALU.mult)
            d2 = tt(v32(ctmp), v32(ct[:, 1, :]), b32(cfr), ALU.mult, d_c0)
            d1 = tt(cc[:, 1, :], cc[:, 1, :], ctmp, ALU.add, d1, d2)
            d_cc = ts(cc[:, 1, :], cc[:, 1, :], -1.0, ALU.mult, None, None, d1)
            yield
            hr, xr, xi, tm = [scr[:, i * 512:(i + 1) * 512].rearrange("p (a b) -> p a b", a=2) for i in range(4)]
            d_prev = d_cc
            for q in range(4):
                ob, ofree, ousers = s5o.get()
                for hp in range(2):
                    b4 = []
                    for j in range(2):
                        i = hp * 2 + j
                        bk, free, users = s5b.get()
                        for v in range(2):
                            m = mm(bk[:, v * 256:(v + 1) * 256], bt[32 * i:32 * i + 32, v, q * 128:(q + 1) * 128],
                                   us[32 * i:32 * i + 32, q, :], True, True, free, d_bt, d_us)
                        Pr, Pi = bk[:, 0:256], bk[:, 256:512]
                        y1 = tt(xr[:, j, :], Pr, Ct[:, i, :], ALU.mult, m, d_tab, d_prev)
                        y2 = tt(tm[:, j, :], Pi, St[:, i, :], ALU.mult, m)
                        y1 = tt(xr[:, j, :], xr[:, j, :], tm[:, j, :], ALU.add, y1, y2)
                        y3 = tt(xi[:, j, :], Pi, Ct[:, i, :], ALU.mult)
                        y2 = tt(tm[:, j, :], Pr, St[:, i, :], ALU.mult, y1)
                        users.append(y2)
                        y3 = tt(xi[:, j, :], xi[:, j, :], tm[:, j, :], ALU.subtract, y3, y2)

                        def scan(x, *after, rbc=rr[:, q * 4 + i:q * 4 + i + 1].to_broadcast([128, 256])):
                            return op("dve", lambda e: e.tensor_tensor_scan(x, rbc, x, 0.0, ALU.mult, ALU.add), *after)
                        b4 += [scan(xr[:, j, :], y1), scan(xi[:, j, :], y3)]
                    cs, ss = Ct[:, hp * 2:hp * 2 + 2, :], St[:, hp * 2:hp * 2 + 2, :]
                    a1 = tt(hr, xr, cs, ALU.mult, b4, d_prev)
                    a2 = tt(tm, xi, ss, ALU.mult, b4)
                    a1 = tt(hr, hr, tm, ALU.subtract, a1, a2)
                    a3 = tt(xr, xr, ss, ALU.mult, a1)
                    a2 = tt(tm, xi, cs, ALU.mult, a1)
                    a3 = tt(xr, xr, tm, ALU.add, a3, a2)
                    if hp and q < 3:
                        d_tab = [dma("pool", x, tabs[q + 1, v].rearrange("p (a b) -> p a b", a=4), d_tabs[q + 1], a2)
                                 for v, x in enumerate((Ct, St))]
                    yield
                    for j in range(2):
                        i = hp * 2 + j
                        o = ob[32 * i:32 * i + 32, 0:256]
                        w = slice((q * 4 + i) * 32, (q * 4 + i) * 32 + 32)
                        mm(o, cc[:, 0, w], hr[:, j, :], True, False, a1, d_cc, ofree)
                        m = mm(o, cc[:, 1, w], xr[:, j, :], False, True, a3)
                    d_prev = [m, a3]
                d_s5y.append(stt(ysT[:, q, :], us[:, q, :], Pm("s5_d", q), ob[:, 0:256], ALU.mult, ALU.add, m))
                ousers.append(d_s5y[-1])

        for _ in projT(4352, 4, us, d_us):
            pass
        rec = recurrence()
        next(rec)
        for _ in projT(2816, 4, sbq, d_sq):
            pass
        for _ in projT(3328, 4, sbk, d_sk):
            pass
        next(rec)
        for _ in projV(3840, 512, sbv, d_sv):
            pass
        att = attention()
        for n, _ in enumerate(filler()):
            next(att, None)
            if n < 5:
                next(att, None)
            if n % 4 == 2:
                next(rec, None)
        for _ in rec:
            pass
        g1 = scr[:, 0:1024].rearrange("p (a b) -> p a b", a=4)
        d = act(g1, ysT, ACT.Square, d_s5y)
        d = ts(g1, g1, 0.044715, ALU.mult, 1.0, ALU.add, d)
        d = tt(g1, g1, ysT, ALU.mult, d)
        d = act(g1, g1, ACT.Sigmoid, d, scale=2.0 * 0.7978845608028654)
        d_gl = tt(g1, g1, ysT, ALU.mult, d)
        for _ in att:
            pass
        kept_branch(gst[0], d_gst[0], 768, 4, ysb, d_sb)
        sgl = Rot([scr[:, 1024:1280], scr[:, 1280:1536]])
        d_s5 = []
        for c in range(2):
            wg = W(I["s5_w_glu"][:, c * 256:(c + 1) * 256], 256)
            wu = W(I["s5_w_glu"][:, 512 + c * 256:512 + (c + 1) * 256], 256)
            for j in range(2):
                bk, free, users = ab.get()
                group(bk[:, 0:256], wg, j * 128, (j + 1) * 128, lambda k: g1[:, k, :], 4, free, d_gl)
                d = group(bk[:, 256:512], wu, j * 128, (j + 1) * 128, lambda k: g1[:, k, :], 4)
                s, sf, su = sgl.get()
                da = act(s, bk[:, 256:512], ACT.Sigmoid, d, sf)
                e = tt(ysT[:, c * 2 + j, :], bk[:, 0:256], s, ALU.mult, da)
                users.append(e)
                su.append(e)
                d_s5.append(e)
            wg.free(d)
            wu.free(d)
        kept_branch(gst[1], d_gst[1], 512, 2, ydl, d_dl)
        for _ in branch(3, 1280, 4, ysT, d_s5):
            pass
        banks = fb
        d_x2 = []
        for c in range(2):
            w = W(I["w_out_2"][:, c * 512:(c + 1) * 512], 512)
            for j in range(4):
                f = c * 4 + j
                bk, free, users = banks.get()
                m = group(bk[:, 0:256], w, j * 128, (j + 1) * 128, lambda k: mg[:, k, :], 8, free, d_mg)
                d = tt(xv[:, f, :], bk[:, 0:256], xv[:, f, :], ALU.add, m)
                users.append(d)
                d_x2.append(d)
            w.free(m)

        banks = whole
        done = barrier()
        banks.users = [list(done) for _ in range(8)]
        base = turn[0] % 6
        for sl in fixed[6:]:
            sl.users = list(done)
        slots[:] = fixed[6:] + slots[base:] + slots[:base]
        turn[0] = 0
        at[0] = 0
        sq = Rot([take(512) for _ in range(2)])
        rf = take(256)
        hn = take(8, 256)
        d_hn = norm_to(hn, "ffn2_w", d_x2, done)
        hh = take(22, 256)
        gs = Rot([take(256) for _ in range(3)])
        d_hh = []
        for c in range(6):
            n = 512 if c < 5 else 256
            wg = W(I["w_up"][:, c * 512:c * 512 + n], n)
            wu = W(I["w_up"][:, 2816 + c * 512:2816 + c * 512 + n], n)
            for j in range(n // 128):
                bk, free, users = banks.get()
                group(bk[:, 0:256], wg, j * 128, (j + 1) * 128, lambda k: hn[:, k, :], 8, free, d_hn)
                m = group(bk[:, 256:512], wu, j * 128, (j + 1) * 128, lambda k: hn[:, k, :], 8)
                s, sf, su = gs.get()
                d = act(s, bk[:, 0:256], ACT.Sigmoid, m, sf)
                d = tt(s, bk[:, 0:256], s, ALU.mult, d)
                d = tt(hh[:, c * 4 + j, :], bk[:, 256:512], s, ALU.mult, d)
                users.append(d)
                su.append(d)
                d_hh.append(d)
            wg.free(m)
            wu.free(m)
        acc = []
        for i in range(4):
            acc.append(banks.get())
        for c in range(11):
            w = W(I["w_down"][c * 256:(c + 1) * 256, :], 1024, per=2)
            for kk_ in range(2):
                k = c * 2 + kk_
                for j in range(8):
                    bk, free, users = acc[j // 2]
                    m = mm(bk[:, (j % 2) * 256:(j % 2) * 256 + 256], w.ap(kk_, j * 128, (j + 1) * 128), hh[:, k, :],
                           k == 0 and j % 2 == 0, k == 21, free, d_hh[k], w.ready(kk_))
            w.free(m)
        for i in range(4):
            bk, free, users = acc[i]
            d = tt(xv[:, 2 * i:2 * i + 2, :], bk.rearrange("p (a b) -> p a b", a=2), xv[:, 2 * i:2 * i + 2, :], ALU.add, m)
            users.append(d)
        d = norm_to(xv, "fin2_w", d)
        d_out = dma("sp", out.rearrange("(k p) t -> p k t", p=128), xv, d)
        last = [d_out, d_skw, d_tabs]
        queue["sp"].append((None, list(flat(last)), Done("sp")))

        for e in esem[0]:
            n = [0, 0]
            for fn, _, d in queue[e]:
                if callable(fn) and d.sem is None and d.asked:
                    n[d.epoch] += 1
                    d.sem, d.val = esem[d.epoch][e], n[d.epoch]

        block = ctx.enter_context(nc.Block())

        def play(name):
            def body(eng):
                seen, inner = {}, []
                for fn, waits, d in queue[name]:
                    if fn == "end":
                        body_, kept = inner.pop()
                        body_.__exit__(None, None, None)
                        seen = kept
                        continue
                    need = {}
                    for w in waits:
                        k = id(w.sem)
                        if seen.get(k, 0) < w.val and (k not in need or need[k].val < w.val):
                            need[k] = w
                    for k, w in need.items():
                        eng.wait_ge(w.sem, w.val)
                        seen[k] = w.val
                    if fn == "if":
                        n = eng.value_load(most[0:1, 0:1], min_val=0, max_val=256)
                        body_ = eng.If(n > d)
                        inner.append((body_, dict(seen)))
                        body_.__enter__()
                        continue
                    if fn is None:
                        continue
                    ins = fn(eng)
                    if d.sem is not None:
                        ins.then_inc(d.sem, 16 if d.dma else 1)
            return body

        block.sync(play("sp"))
        block.tensor(play("pe"))
        block.vector(play("dve"))
        block.scalar(play("act"))
        block.gpsimd(play("pool"))


_RAW = {"w_ada": (1024, 6144), "w_in": (1024, 1984), "w_uq": (256, 768), "w_ukv": (128, 1024), "w_out": (1024, 1024),
        "router_w": (1024, 32), "router_b": (1, 32), "w1": (32, 1024, 2048), "w2": (32, 1024, 1024), "b2": (32, 1024),
        "rel_bias_2": (32, 12), "w_in_2": (1024, 4864), "pool_w_2": (512, 128), "s5_w_glu_2": (512, 1024),
        "w_branch_2": (1792, 1024), "w_gate_2": (4, 1024, 1024), "w_out_2": (1024, 1024), "w_up_2": (1024, 5632),
        "w_down_2": (2816, 1024)}
_NAMES = {"rel_bias_2": "rel_bias", "pool_w_2": "pool_w", "s5_w_glu_2": "s5_w_glu", "w_branch_2": "w_branch",
          "w_gate_2": "w_gate", "w_up_2": "w_up", "w_down_2": "w_down"}


def constants():
    import numpy as np
    f = np.float32
    c = np.zeros((128, CST_N), f)

    def put(name, a):
        lo, hi = CST[name]
        c[:a.shape[0], lo:hi] = a
    i = np.arange(128)
    put("ident", np.eye(128, dtype=f))
    put("ones", np.ones((128, 128), f))
    rot = np.zeros((128, 128), f)
    for m in range(128):
        if (m // 16) % 2 == 0:
            rot[m + 16, m] = -1.0
        else:
            rot[m - 16, m] = 1.0
    put("rot", rot)
    put("tri", (i[:, None] >= i[None, :]).astype(f))
    put("before", (i[:, None] < i[None, :]).astype(f))
    put("iota", np.broadcast_to(np.arange(2 * S, dtype=f), (128, 2 * S)))
    t = np.arange(256)
    inv = f(10000.0) ** (-np.arange(16, dtype=f) / f(16))
    d = np.arange(128) % 64
    pos = np.where((d // 32 == 0)[:, None], (t // 64)[None, :], (t % 64)[None, :]).astype(f)
    ang = pos * inv[d % 16][:, None]
    put("cos", np.cos(ang).astype(f))
    put("sin", np.sin(ang).astype(f))
    q = np.concatenate([np.arange(256), np.arange(128, 256)])
    k = np.concatenate([np.zeros(256, int), np.full(128, 128)])[None, :] + i[:, None]
    valid = k < q[None, :]
    put("m01", valid.astype(f))
    put("mneg", np.where(valid, f(0), f(-BIG)))
    put("inv", np.broadcast_to(np.concatenate([1.0 / np.minimum(t + 1, w) for w in (2, 4, 8, 16)]).astype(f), (128, 1024)))
    dist = 255 - np.arange(384)
    df = np.maximum(dist, 1).astype(f)
    large = 16 + (np.log(df / f(16)) / f(np.log(2048 / 16)) * f(16)).astype(np.int32)
    bucket = np.where(dist < 16, dist, np.minimum(large, 31))
    hot = np.zeros((33, 3, 384), f)
    for g, (win, dil) in enumerate(((128, 1), (512, 4), (2048, 16))):
        ok = (dist >= 0) & (dist % dil == 0) & (dist <= win)
        for n in range(384):
            if ok[n]:
                hot[bucket[n], g, n] = 1.0
            else:
                hot[32, g, n] = -BIG
    put("eps", np.full((128, 1), EPS, f))
    return c, hot.reshape(33, 1152)


def kernel(**inputs):
    import numpy as _np
    import concourse.bacc as _bacc
    from concourse.bass_utils import run_bass_kernel_spmd as _run

    x = {k: _np.asarray(v) for k, v in inputs.items()}

    def col(a):
        return a.reshape(-1, 128).T

    p = _np.zeros((128, PAR_N), _np.float32)

    def put(name, a):
        lo, hi = PAR[name]
        p[:a.shape[0], lo:hi] = a

    put("c2", _np.stack([col(x["c"]), col(x["c_ctx"])], axis=2).reshape(128, 16))
    for name, src in (("b_ada", "b_ada"), ("attn_w", "attn_norm_w"), ("qn_w", "q_norm_w"), ("kvn_w", "kv_norm_w"),
                      ("sub_w", "subln_w"), ("ffn_w", "ffn_norm_w"), ("fin_w", "final_norm_w"),
                      ("attn2_w", "attn_norm_g_2"), ("ffn2_w", "ffn_norm_g_2"), ("fin2_w", "final_norm_g_2"),
                      ("b1", "b1"), ("pscale", "pool_scale_2"), ("s5_are", "s5_a_re_2"), ("s5_aim", "s5_a_im_2"),
                      ("s5_d", "s5_d_2")):
        put(name, col(x[src]))
    put("lam", _np.stack([x[n].reshape(64) for n in ("lambda_q1", "lambda_q2", "lambda_k1", "lambda_k2")], axis=1))
    put("s5_ldt", _np.repeat(x["s5_log_dt_2"].reshape(16, 2, 1), 64, axis=2).reshape(16, 128).T)
    cst, hot = constants()
    arrays = {"par": p, "cst": cst, "hot": hot,
              "xT": _np.ascontiguousarray(x["x"].reshape(256, 1024).T),
              "ctxT": _np.ascontiguousarray(x["ctx"].reshape(256, 1024).T)}
    for v in ("re", "im"):
        b = x[f"s5_b_{v}_2"].reshape(4, 4, 2, 64, 16)
        bt = _np.zeros((4, 2, 16, 4, 2, 64), _np.float32)
        c = x[f"s5_c_{v}_2"].reshape(16, 2, 16, 64)
        ct = _np.zeros((2, 64, 16, 2, 16), _np.float32)
        for g in range(2):
            bt[:, g, :, :, g, :] = b[:, :, g].transpose(1, 3, 0, 2)
            ct[g, :, :, g, :] = c[:, g].transpose(2, 0, 1)
        arrays["s5_b" + v] = bt.reshape(128, 512)
        arrays["s5_c" + v] = ct.reshape(128, 512)
    for name, shape in _RAW.items():
        arrays[_NAMES.get(name, name)] = _np.ascontiguousarray(x[name]).reshape(shape)

    nc = _bacc.Bacc("TRN2", target_bir_lowering=False, num_devices=1)
    aps = {n: nc.dram_tensor("in_" + n, a.shape, F32, kind="ExternalInput").ap() for n, a in arrays.items()}
    out = nc.dram_tensor("out_0", (1024, 256), F32, kind="ExternalOutput").ap()
    build(nc, aps, out)
    r = _run(nc, [{"in_" + n: a for n, a in arrays.items()}], core_ids=[0])
    return _np.ascontiguousarray(r.results[0]["out_0"].T).reshape(1, 256, 1024)
```
